# Optimizing a Trainium2 kernel written in Bass

```python
import math
import jax, jax.numpy as jnp
from jax import lax
import numpy as np

D_MODEL = 1024
BATCH = 1
SEQ = 256
DEPTH = 1

CHUNK = 64
Q_BLOCK = 128
EPS = 1e-6

FOX_HEADS = 4
FOX_DIM = 128
GDN_HEADS = 4
GDN_DK = 128
GDN_DV = 128
GDN_CONV = 4
SB_HEADS = 4
SB_DIM = 128
MEM_TOKENS = 256
MEM_HEADS = 4
MEM_DIM = 128
D_FF = 2816
FFN_CONV = 3
N_BRANCH = 3

FOX_W = FOX_HEADS * FOX_DIM
GDN_KW = GDN_HEADS * GDN_DK
GDN_VW = GDN_HEADS * GDN_DV
SB_W = SB_HEADS * SB_DIM
MEM_W = MEM_HEADS * MEM_DIM

IN_SPLITS = (
    FOX_W, FOX_W, FOX_W, FOX_HEADS,
    GDN_KW, GDN_KW, GDN_VW, GDN_HEADS, GDN_HEADS, GDN_VW,
    SB_W, SB_W, SB_W,
    N_BRANCH * D_MODEL,
)
N_IN = sum(IN_SPLITS)


def rmsnorm(x, g):
    xf = x.astype(jnp.float32)
    y = xf * lax.rsqrt(jnp.mean(xf * xf, axis=-1, keepdims=True) + EPS)
    return (y * g.astype(jnp.float32)).astype(x.dtype)

def l2norm(x):
    xf = x.astype(jnp.float32)
    return xf * lax.rsqrt(jnp.sum(xf * xf, axis=-1, keepdims=True) + EPS)

def heads(x, n):
    return x.reshape(x.shape[:-1] + (n, -1))

def causal_dwconv(x, w):
    width, ch = w.shape
    return lax.conv_general_dilated(
        x, w[:, None, :].astype(x.dtype), window_strides=(1,), padding=[(width - 1, 0)],
        dimension_numbers=("NWC", "WIO", "NWC"), feature_group_count=ch)

def split_projection(p):
    points = [int(s) for s in np.cumsum(IN_SPLITS)[:-1]]
    return jnp.split(p, points, axis=-1)

def fox_attention(q, k, v, logf):
    B, S, H, dh = q.shape
    c = jnp.cumsum(logf, axis=1).transpose(0, 2, 1)
    qh = q.transpose(0, 2, 1, 3)
    kh = k.transpose(0, 2, 1, 3)
    vh = v.transpose(0, 2, 1, 3)
    scale = dh ** -0.5
    outs = []
    for i in range(S // Q_BLOCK):
        lo, hi = i * Q_BLOCK, (i + 1) * Q_BLOCK
        s = (jnp.einsum("bhqd,bhkd->bhqk", qh[:, :, lo:hi], kh[:, :, :hi]).astype(jnp.float32) * scale
             + (c[:, :, lo:hi, None] - c[:, :, None, :hi]))
        mask = jnp.arange(hi)[None, :] <= jnp.arange(lo, hi)[:, None]
        p = jax.nn.softmax(jnp.where(mask, s, -jnp.inf), axis=-1).astype(vh.dtype)
        outs.append(jnp.einsum("bhqk,bhkd->bhqd", p, vh[:, :, :hi]))
    o = jnp.concatenate(outs, axis=2)
    return o.transpose(0, 2, 1, 3).reshape(B, S, H * dh)

def stick_breaking_attention(q, k, v):
    B, S, H, dh = q.shape
    qh = q.transpose(0, 2, 1, 3)
    kh = k.transpose(0, 2, 1, 3)
    vh = v.transpose(0, 2, 1, 3)
    scale = dh ** -0.5
    idx = jnp.arange(Q_BLOCK)
    tri_in = (idx[:, None] >= idx[None, :]).astype(jnp.float32)
    outs = []
    for i in range(S // Q_BLOCK):
        lo, hi = i * Q_BLOCK, (i + 1) * Q_BLOCK
        nk = i + 1
        z = jnp.einsum("bhqd,bhkd->bhqk", qh[:, :, lo:hi], kh[:, :, :hi]).astype(jnp.float32) * scale
        mask = jnp.arange(hi)[None, :] < jnp.arange(lo, hi)[:, None]
        log_keep = jnp.where(mask, -jax.nn.softplus(z), 0.0)
        lk = log_keep.reshape(B, H, Q_BLOCK, nk, Q_BLOCK)
        within = jnp.einsum("bhqnj,jk->bhqnk", lk, tri_in)
        tot = jnp.sum(lk, axis=-1)
        blk = jnp.arange(nk)
        tri_blk = (blk[:, None] > blk[None, :]).astype(jnp.float32)
        after = jnp.einsum("bhqm,mn->bhqn", tot, tri_blk)
        rc = (within + after[..., None]).reshape(B, H, Q_BLOCK, hi)
        a = jnp.exp(jnp.where(mask, z + rc, -jnp.inf)).astype(vh.dtype)
        outs.append(jnp.einsum("bhqk,bhkd->bhqd", a, vh[:, :, :hi]))
    o = jnp.concatenate(outs, axis=2)
    return o.transpose(0, 2, 1, 3).reshape(B, S, H * dh)

def gated_delta_rule(q, k, v, g, beta):
    B, T, H, dk = q.shape
    dv = v.shape[-1]
    N = T // CHUNK
    f32 = jnp.float32

    def chunks(a):
        a = a.astype(f32).reshape((B, N, CHUNK, H) + a.shape[3:])
        return jnp.moveaxis(a, (1, 3), (0, 2))

    qc = chunks(q) * dk ** -0.5
    kc = chunks(k)
    vc = chunks(v)
    bc = chunks(beta)
    gc = jnp.cumsum(chunks(g), axis=-1)
    idx = jnp.arange(CHUNK)
    causal = idx[:, None] >= idx[None, :]
    strict = idx[:, None] > idx[None, :]
    decay = jnp.exp(jnp.where(causal, gc[..., :, None] - gc[..., None, :], -jnp.inf))
    kk = jnp.einsum("nbhcd,nbhed->nbhce", kc, kc)
    a_mat = jnp.where(strict, bc[..., :, None] * kk * decay, 0.0) + jnp.eye(CHUNK, dtype=f32)
    rhs = jnp.concatenate([vc * bc[..., None], kc * (bc * jnp.exp(gc))[..., None]], axis=-1)
    sol = lax.linalg.triangular_solve(a_mat, rhs, left_side=True, lower=True)
    u, w = sol[..., :dv], sol[..., dv:]
    attn = jnp.where(causal, jnp.einsum("nbhcd,nbhed->nbhce", qc, kc) * decay, 0.0)
    g_last = gc[..., -1]
    k_tail = kc * jnp.exp(g_last[..., None] - gc)[..., None]

    def step(state, xs):
        q_n, u_n, w_n, g_n, attn_n, kt_n, gl_n = xs
        v_new = u_n - jnp.einsum("bhck,bhkv->bhcv", w_n, state)
        o = (jnp.einsum("bhck,bhkv->bhcv", q_n * jnp.exp(g_n)[..., None], state)
             + jnp.einsum("bhce,bhev->bhcv", attn_n, v_new))
        state = state * jnp.exp(gl_n)[..., None, None] + jnp.einsum("bhck,bhcv->bhkv", kt_n, v_new)
        return state, o

    s0 = jnp.zeros((B, H, dk, dv), f32)
    _, o = lax.scan(step, s0, (qc, u, w, gc, attn, k_tail, g_last))
    return jnp.moveaxis(o, (0, 2), (1, 3)).reshape(B, T, H, dv)

def memory_cross_attention(h, m, w_q, w_kv, q_g, k_g, w_o):
    B, S, _ = h.shape
    q = rmsnorm(heads(h @ w_q, MEM_HEADS), q_g)
    k, v = jnp.split(m @ w_kv, 2, axis=-1)
    k = rmsnorm(heads(k, MEM_HEADS), k_g)
    v = heads(v, MEM_HEADS)
    s = jnp.einsum("bqhd,bkhd->bhqk", q, k).astype(jnp.float32) * MEM_DIM ** -0.5
    p = jax.nn.softmax(s, axis=-1).astype(v.dtype)
    o = jnp.einsum("bhqk,bkhd->bqhd", p, v).reshape(B, S, MEM_W)
    return o @ w_o

def conv_ffn(h, w_up, conv_w, conv_b, w_down):
    u = causal_dwconv(h @ w_up, conv_w) + conv_b
    a, b = jnp.split(u, 2, axis=-1)
    return (jax.nn.silu(a) * b) @ w_down

def first_inputs(seed: int = 0) -> dict:
    key = jax.random.key(seed)
    ks = iter(jax.random.split(key, 40))
    L, D = DEPTH, D_MODEL
    f32 = jnp.float32

    def nrm(shape, scale):
        return jax.random.normal(next(ks), shape, f32) * scale

    def gain(shape):
        return 1.0 + 0.02 * jax.random.normal(next(ks), shape, f32)

    x = nrm((BATCH, SEQ, D), 1.0)
    mem = nrm((BATCH, MEM_TOKENS, D), 1.0)
    norm_mix = gain((L, D))
    w_in = nrm((L, D, N_IN), D ** -0.5)
    fox_fbias = jax.random.uniform(next(ks), (L, FOX_HEADS), f32, minval=1.0, maxval=5.0)
    fox_qnorm = gain((L, FOX_DIM))
    fox_knorm = gain((L, FOX_DIM))
    gdn_conv = nrm((L, GDN_CONV, 2 * GDN_KW + GDN_VW), GDN_CONV ** -0.5)
    gdn_a_log = jnp.log(jax.random.uniform(next(ks), (L, GDN_HEADS), f32, minval=1.0, maxval=16.0))
    dt = jnp.exp(jax.random.uniform(next(ks), (L, GDN_HEADS), f32,
                                    minval=math.log(1e-3), maxval=math.log(1e-1)))
    gdn_dt_bias = dt + jnp.log(-jnp.expm1(-dt))
    gdn_onorm = gain((L, GDN_DV))
    gate_bias = nrm((L, N_BRANCH * D), 0.01)
    w_oa = nrm((L, FOX_W, D), FOX_W ** -0.5)
    w_ob = nrm((L, GDN_VW, D), GDN_VW ** -0.5)
    w_oc = nrm((L, SB_W, D), SB_W ** -0.5)
    w_out = nrm((L, D, D), D ** -0.5)
    norm_xq = gain((L, D))
    norm_mem = gain((L, D))
    w_mq = nrm((L, D, MEM_W), D ** -0.5)
    w_mkv = nrm((L, D, 2 * MEM_W), D ** -0.5)
    mq_norm = gain((L, MEM_DIM))
    mk_norm = gain((L, MEM_DIM))
    w_mo = nrm((L, MEM_W, D), MEM_W ** -0.5)
    norm_ffn = gain((L, D))
    w_up = nrm((L, D, 2 * D_FF), D ** -0.5)
    ffn_conv = nrm((L, FFN_CONV, 2 * D_FF), FFN_CONV ** -0.5)
    ffn_conv_b = nrm((L, 2 * D_FF), 0.01)
    w_down = nrm((L, D_FF, D), D_FF ** -0.5)
    return {
        "x": x, "mem": mem, "norm_mix": norm_mix, "w_in": w_in,
        "fox_fbias": fox_fbias, "fox_qnorm": fox_qnorm, "fox_knorm": fox_knorm,
        "gdn_conv": gdn_conv, "gdn_a_log": gdn_a_log, "gdn_dt_bias": gdn_dt_bias,
        "gdn_onorm": gdn_onorm, "gate_bias": gate_bias,
        "w_oa": w_oa, "w_ob": w_ob, "w_oc": w_oc, "w_out": w_out,
        "norm_xq": norm_xq, "norm_mem": norm_mem, "w_mq": w_mq, "w_mkv": w_mkv,
        "mq_norm": mq_norm, "mk_norm": mk_norm, "w_mo": w_mo,
        "norm_ffn": norm_ffn, "w_up": w_up, "ffn_conv": ffn_conv,
        "ffn_conv_b": ffn_conv_b, "w_down": w_down,
    }

def first_block(x, mem, norm_mix, w_in, fox_fbias, fox_qnorm, fox_knorm, gdn_conv, gdn_a_log,
              gdn_dt_bias, gdn_onorm, gate_bias, w_oa, w_ob, w_oc, w_out, norm_xq, norm_mem,
              w_mq, w_mkv, mq_norm, mk_norm, w_mo, norm_ffn, w_up, ffn_conv, ffn_conv_b, w_down):
    B, S, D = x.shape
    f32 = jnp.float32
    for l in range(DEPTH):
        h = rmsnorm(x, norm_mix[l])
        (fq, fk, fv, ff, gq, gk, gv, gb, ga, gz, sq, sk, sv, gates) = split_projection(h @ w_in[l])

        fq = rmsnorm(heads(fq, FOX_HEADS), fox_qnorm[l])
        fk = rmsnorm(heads(fk, FOX_HEADS), fox_knorm[l])
        logf = jax.nn.log_sigmoid((ff + fox_fbias[l]).astype(f32))
        ya = fox_attention(fq, fk, heads(fv, FOX_HEADS), logf)

        qkv = jax.nn.silu(causal_dwconv(jnp.concatenate([gq, gk, gv], axis=-1), gdn_conv[l]))
        cq, ck, cv = jnp.split(qkv, [GDN_KW, 2 * GDN_KW], axis=-1)
        beta = jax.nn.sigmoid(gb.astype(f32))
        g_log = -jnp.exp(gdn_a_log[l].astype(f32)) * jax.nn.softplus((ga + gdn_dt_bias[l]).astype(f32))
        o = gated_delta_rule(l2norm(heads(cq, GDN_HEADS)), l2norm(heads(ck, GDN_HEADS)),
                             heads(cv, GDN_HEADS), g_log, beta)
        yb = (rmsnorm(o, gdn_onorm[l]) * jax.nn.silu(heads(gz, GDN_HEADS).astype(f32)))
        yb = yb.astype(x.dtype).reshape(B, S, GDN_VW)

        yc = stick_breaking_attention(heads(sq, SB_HEADS), heads(sk, SB_HEADS), heads(sv, SB_HEADS))

        g = jax.nn.sigmoid((gates + gate_bias[l]).astype(f32)).astype(x.dtype).reshape(B, S, N_BRANCH, D)
        mixed = (g[..., 0, :] * (ya @ w_oa[l]) + g[..., 1, :] * (yb @ w_ob[l])
                 + g[..., 2, :] * (yc @ w_oc[l]))
        x = x + mixed @ w_out[l]

        x = x + memory_cross_attention(rmsnorm(x, norm_xq[l]), rmsnorm(mem, norm_mem[l]),
                                       w_mq[l], w_mkv[l], mq_norm[l], mk_norm[l], w_mo[l])

        x = x + conv_ffn(rmsnorm(x, norm_ffn[l]), w_up[l], ffn_conv[l], ffn_conv_b[l], w_down[l])
    return x


RET_WIDTH = D_MODEL // 2
RET_HEADS = 4
RET_HEAD_DIM = RET_WIDTH // RET_HEADS
CONV_WIDTH = D_MODEL - RET_WIDTH
CONV_GROUPS = 8
CONV_K = 3
MIX_WIDTH = RET_WIDTH + CONV_WIDTH
IN_COLS = 4 * RET_WIDTH + 3 * CONV_WIDTH
CHUNK_2 = 128
ROPE_BASE = 10000.0
N_GROUPS = 8
EXPERTS_PER_GROUP = 8
N_EXPERTS = N_GROUPS * EXPERTS_PER_GROUP
TOP_K = 2
EXPERT_FF = D_MODEL // 2
MOE_BLOCK = 128


def rmsnorm_2(x, w):
    xf = x.astype(jnp.float32)
    y = xf * lax.rsqrt(jnp.mean(xf * xf, axis=-1, keepdims=True) + EPS)
    return (y * w.astype(jnp.float32)).astype(x.dtype)

def rotary(x, pos):
    half = x.shape[-1] // 2
    inv = ROPE_BASE ** (-jnp.arange(half, dtype=jnp.float32) / half)
    ang = pos.astype(jnp.float32)[:, None] * inv[None, :]
    cos = jnp.cos(ang)[None, :, None, :]
    sin = jnp.sin(ang)[None, :, None, :]
    xf = x.astype(jnp.float32)
    x1, x2 = xf[..., :half], xf[..., half:]
    return jnp.concatenate([x1 * cos - x2 * sin, x2 * cos + x1 * sin], axis=-1)

def retention_chunkwise(q, k, v):
    b, s, h, d = q.shape
    nc = s // CHUNK_2
    log_g = jnp.log1p(-(2.0 ** (-5.0 - jnp.arange(h, dtype=jnp.float32))))
    idx = jnp.arange(CHUNK_2, dtype=jnp.float32)
    rel = idx[:, None] - idx[None, :]
    causal = rel >= 0
    intra_decay = jnp.where(causal[None], jnp.exp(log_g[:, None, None] * jnp.where(causal, rel, 0.0)[None]), 0.0)
    k_decay = jnp.exp(log_g[:, None] * (CHUNK_2 - 1 - idx)[None, :])
    q_decay = jnp.exp(log_g[:, None] * (idx + 1)[None, :])
    chunk_decay = jnp.exp(log_g * CHUNK_2)

    qc = q.reshape(b, nc, CHUNK_2, h, d)
    kc = k.reshape(b, nc, CHUNK_2, h, d)
    vc = v.reshape(b, nc, CHUNK_2, h, d)

    scores = jnp.einsum('bnihd,bnjhd->bnhij', qc, kc) * intra_decay[None, None]
    o_intra = jnp.einsum('bnhij,bnjhd->bnihd', scores, vc)

    kv = jnp.einsum('bnjhd,hj,bnjhe->bnhde', kc, k_decay, vc)

    def step(state, kv_n):
        return chunk_decay[None, :, None, None] * state + kv_n, state

    _, prev = lax.scan(step, jnp.zeros((b, h, d, d), jnp.float32), jnp.moveaxis(kv, 1, 0))
    prev = jnp.moveaxis(prev, 0, 1)
    o_inter = jnp.einsum('bnihd,bnhde->bnihe', qc, prev) * q_decay.T[None, None, :, :, None]
    return (o_intra + o_inter).reshape(b, s, h, d)

def head_groupnorm(o, w):
    b, s, h, d = o.shape
    mu = jnp.mean(o, axis=-1, keepdims=True)
    var = jnp.mean(jnp.square(o - mu), axis=-1, keepdims=True)
    y = (o - mu) * lax.rsqrt(var + EPS)
    return y.reshape(b, s, h * d) * w.astype(jnp.float32)

def causal_depthwise_conv(u, w):
    return lax.conv_general_dilated(
        u, w[:, None, :], window_strides=(1,), padding=[(CONV_K - 1, 0)],
        dimension_numbers=('NWC', 'WIO', 'NWC'), feature_group_count=u.shape[-1])

def mixer(h, w_in, ret_gn_w, conv_w, w_o):
    b, s, _ = h.shape
    proj = h @ w_in
    R, C = RET_WIDTH, CONV_WIDTH
    q, k, v, g, gb, gc, u = jnp.split(proj, [R, 2 * R, 3 * R, 4 * R, 4 * R + C, 4 * R + 2 * C], axis=-1)
    pos = jnp.arange(s)
    q = rotary(q.reshape(b, s, RET_HEADS, RET_HEAD_DIM), pos) * (RET_HEAD_DIM ** -0.5)
    k = rotary(k.reshape(b, s, RET_HEADS, RET_HEAD_DIM), pos)
    v = v.reshape(b, s, RET_HEADS, RET_HEAD_DIM).astype(jnp.float32)
    ret = retention_chunkwise(q, k, v)
    ret = (jax.nn.silu(g.astype(jnp.float32)) * head_groupnorm(ret, ret_gn_w)).astype(h.dtype)
    conv = gb * causal_depthwise_conv(gc * u, conv_w)
    return jnp.concatenate([ret, conv], axis=-1) @ w_o

def expert_dispatch(t, expert, gate, w_gate, w_up, w_down):
    n, d = t.shape
    e_total = w_gate.shape[0]
    n_slots = n * TOP_K
    flat_e = expert.reshape(-1)
    flat_tok = jnp.repeat(jnp.arange(n, dtype=jnp.int32), TOP_K)
    flat_w = gate.reshape(-1)
    order = jnp.argsort(flat_e)
    se, stok, sw = flat_e[order], flat_tok[order], flat_w[order]
    counts = jnp.bincount(flat_e, length=e_total)
    starts = jnp.cumsum(counts) - counts
    padded = ((counts + MOE_BLOCK - 1) // MOE_BLOCK) * MOE_BLOCK
    pad_ends = jnp.cumsum(padded)
    pad_starts = pad_ends - padded
    dest = pad_starts[se] + (jnp.arange(n_slots) - starts[se])
    n_blocks = -(-n_slots // MOE_BLOCK) + e_total
    cap = n_blocks * MOE_BLOCK
    buf_tok = jnp.full((cap,), n, jnp.int32).at[dest].set(stok)
    buf_w = jnp.zeros((cap,), t.dtype).at[dest].set(sw.astype(t.dtype))
    block_e = jnp.minimum(jnp.searchsorted(pad_ends, jnp.arange(n_blocks) * MOE_BLOCK, side='right'), e_total - 1)
    t_pad = jnp.concatenate([t, jnp.zeros((1, d), t.dtype)], axis=0)

    def run_block(args):
        tok, e = args
        xb = t_pad[tok]
        hb = jax.nn.silu(xb @ w_gate[e]) * (xb @ w_up[e])
        return hb @ w_down[e]

    yb = lax.map(run_block, (buf_tok.reshape(n_blocks, MOE_BLOCK), block_e))
    y = jax.ops.segment_sum(yb.reshape(cap, d) * buf_w[:, None], buf_tok, num_segments=n + 1)
    return y[:n]

def hier_moe(h, rg_w, rg_b, re_w, re_b, w_gate, w_up, w_down):
    b, s, d = h.shape
    t = h.reshape(b * s, d)
    g_prob = jax.nn.softmax((t @ rg_w).astype(jnp.float32) + rg_b.astype(jnp.float32), axis=-1)
    p_group, g_sel = lax.top_k(g_prob, 1)
    p_group, g_sel = p_group[:, 0], g_sel[:, 0]
    e_logits_all = jnp.einsum('nd,gde->nge', t, re_w).astype(jnp.float32) + re_b.astype(jnp.float32)[None]
    e_logits = jnp.take_along_axis(e_logits_all, g_sel[:, None, None], axis=1)[:, 0]
    e_prob = jax.nn.softmax(e_logits, axis=-1)
    top_p, top_i = lax.top_k(e_prob, TOP_K)
    top_p = top_p / jnp.sum(top_p, axis=-1, keepdims=True)
    gate = p_group[:, None] * top_p
    expert = g_sel[:, None] * EXPERTS_PER_GROUP + top_i
    return expert_dispatch(t, expert, gate, w_gate, w_up, w_down).reshape(b, s, d)

def second_inputs(seed: int = 0) -> dict:
    key = jax.random.key(seed)
    ks = jax.random.split(key, 16)
    f32 = jnp.float32
    nrm = lambda k, shape, scale: jax.random.normal(k, shape, f32) * scale
    return {
        "x": nrm(ks[0], (BATCH, SEQ, D_MODEL), 1.0),
        "norm1_w": 1.0 + nrm(ks[1], (DEPTH, D_MODEL), 0.02),
        "w_in": nrm(ks[2], (DEPTH, D_MODEL, IN_COLS), D_MODEL ** -0.5),
        "ret_gn_w": 1.0 + nrm(ks[3], (DEPTH, RET_WIDTH), 0.02),
        "conv_w": nrm(ks[4], (DEPTH, CONV_K, CONV_WIDTH), CONV_K ** -0.5),
        "w_o": nrm(ks[5], (DEPTH, MIX_WIDTH, D_MODEL), MIX_WIDTH ** -0.5),
        "norm2_w": 1.0 + nrm(ks[6], (DEPTH, D_MODEL), 0.02),
        "router_g_w": nrm(ks[7], (DEPTH, D_MODEL, N_GROUPS), D_MODEL ** -0.5),
        "router_g_b": nrm(ks[8], (DEPTH, N_GROUPS), 0.01),
        "router_e_w": nrm(ks[9], (DEPTH, N_GROUPS, D_MODEL, EXPERTS_PER_GROUP), D_MODEL ** -0.5),
        "router_e_b": nrm(ks[10], (DEPTH, N_GROUPS, EXPERTS_PER_GROUP), 0.01),
        "w_gate": nrm(ks[11], (DEPTH, N_EXPERTS, D_MODEL, EXPERT_FF), D_MODEL ** -0.5),
        "w_up": nrm(ks[12], (DEPTH, N_EXPERTS, D_MODEL, EXPERT_FF), D_MODEL ** -0.5),
        "w_down": nrm(ks[13], (DEPTH, N_EXPERTS, EXPERT_FF, D_MODEL), EXPERT_FF ** -0.5),
        "final_norm_w": 1.0 + nrm(ks[14], (D_MODEL,), 0.02),
    }

def second_block(x, norm1_w, w_in, ret_gn_w, conv_w, w_o, norm2_w, router_g_w, router_g_b,
              router_e_w, router_e_b, w_gate, w_up, w_down, final_norm_w):
    for l in range(DEPTH):
        h = rmsnorm_2(x, norm1_w[l])
        x = x + mixer(h, w_in[l], ret_gn_w[l], conv_w[l], w_o[l])
        h = rmsnorm_2(x, norm2_w[l])
        x = x + hier_moe(h, router_g_w[l], router_g_b[l], router_e_w[l], router_e_b[l],
                         w_gate[l], w_up[l], w_down[l])
    return rmsnorm_2(x, final_norm_w)


def setup_inputs(seed=0):
    out = dict(first_inputs(seed))
    for name, value in second_inputs(seed + 1).items():
        if name != "x":
            out[name + "_2"] = value
    return out


def reference(
    x, mem, norm_mix, w_in, fox_fbias, fox_qnorm, fox_knorm, gdn_conv, gdn_a_log, gdn_dt_bias,
    gdn_onorm, gate_bias, w_oa, w_ob, w_oc, w_out, norm_xq, norm_mem, w_mq, w_mkv, mq_norm,
    mk_norm, w_mo, norm_ffn, w_up, ffn_conv, ffn_conv_b, w_down, norm1_w_2, w_in_2, ret_gn_w_2,
    conv_w_2, w_o_2, norm2_w_2, router_g_w_2, router_g_b_2, router_e_w_2, router_e_b_2,
    w_gate_2, w_up_2, w_down_2, final_norm_w_2,
):
    x = first_block(
        x, mem, norm_mix, w_in, fox_fbias, fox_qnorm, fox_knorm, gdn_conv, gdn_a_log,
        gdn_dt_bias, gdn_onorm, gate_bias, w_oa, w_ob, w_oc, w_out, norm_xq, norm_mem, w_mq,
        w_mkv, mq_norm, mk_norm, w_mo, norm_ffn, w_up, ffn_conv, ffn_conv_b, w_down,
    )
    return second_block(
        x, norm1_w_2, w_in_2, ret_gn_w_2, conv_w_2, w_o_2, norm2_w_2, router_g_w_2,
        router_g_b_2, router_e_w_2, router_e_b_2, w_gate_2, w_up_2, w_down_2, final_norm_w_2,
    )


_drawn_inputs = setup_inputs


def setup_inputs(seed=0):
    import zlib

    import numpy as np

    out = dict(_drawn_inputs(seed))
    spreads = {}
    factors = {'fox_qnorm': 5.192,
     'fox_knorm': 7.632,
     'gdn_onorm': 3.56,
     'gate_bias': 8.0,
     'norm_xq': 8.0,
     'norm_mem': 8.0,
     'mq_norm': 8.0,
     'mk_norm': 8.0,
     'ffn_conv_b': 4.565,
     'ret_gn_w_2': 5.577,
     'norm2_w_2': 3.207,
     'router_g_b_2': 8.0,
     'router_e_b_2': 8.0,
     'final_norm_w_2': 2.845}
    for name, (base, spread) in spreads.items():
        noise = np.random.default_rng([zlib.crc32(name.encode()), seed]).standard_normal(out[name].shape)
        drawn = base * np.exp(spread * noise) if base else spread * noise
        out[name] = __import__('jax').numpy.asarray(drawn.astype(out[name].dtype))
    for name, factor in factors.items():
        out[name] = (out[name] * factor).astype(out[name].dtype)
    return out
```

```python
from contextlib import ExitStack

import numpy as np

import concourse.bass as bass
from concourse import mybir

ALU = mybir.AluOpType
ACT = mybir.ActivationFunctionType
F32 = mybir.dt.float32
I32 = mybir.dt.int32
AX = mybir.AxisListType.X

P = 128
T = 256
TT = T // P
D = 1024
DC = D // P
H = 4
CHUNK = 64
LEVELS = (1, 2, 4, 8, 16, 32)
FC = 2816 // P
E = 64
CAP = 32
GROUP = 4
NG = E // GROUP
MAXPASS = T // CAP
EPS = 1e-6
SCALE = P ** -0.5
NEG = -1e30
SLOT = 4096
RING = 4



def columns(*parts):
    at, n = {}, 0
    for name, width in parts:
        at[name] = slice(n, n + width)
        n += width
    return at, n


C1, NC1 = columns(("ident", P), ("ones", 256), ("inv128", P), ("inv1024", P), ("tri", P), ("before", P),
                  ("fox_mask", 384), ("sb_neg", 384), ("sb_mask", 384), ("chunk_mask", P),
                  ("levels", P * len(LEVELS)), ("sel", H * 256), ("negsel", H * P), ("slots", CAP),
                  ("first", E), ("reset", T), ("steps", MAXPASS - 1), ("eps", 1))
C2, NC2 = columns(("rot", P), ("cosq", T), ("sinq", T), ("cosk", T), ("sink", T), ("decay", H * 384))
SM, NSM = columns(("norm_mix", DC), ("norm_xq", DC), ("norm_mem", DC), ("norm_ffn", DC), ("norm1", DC),
                  ("norm2", DC), ("final", DC), ("fox_q", 1), ("fox_k", 1), ("gdn_o", 1), ("mq", 1), ("mk", 1),
                  ("ret_gn", H), ("gate_b", 3 * DC), ("gdn_conv", 48), ("ffn_conv", 6 * FC), ("ffn_b", 2 * FC),
                  ("conv2", 12), ("rows", 3))
TILES = ["gq", "gk", "gv", "gz", "fq", "fk", "fv", "sq", "sk", "sv",
         "ga0", "oa", "ga1", "gc0", "oc", "gc1", "gb0", "ob", "gb1",
         "out0", "out1", "mk", "mv", "mq", "mo"]
for _j in range(FC // 2):
    TILES.append(f"U{_j}")
    if _j % 2:
        TILES.append(f"D{_j // 2}")
TILES += [f"D{FC // 4}", "q2", "k2", "v2", "g2", "gc2", "u2", "gb2", "o20", "o21"]
TILE = {name: n for n, name in enumerate(TILES)}


def program(nc, c1_in, c2_in, sm_in, rb_in, x_in, mem_in, dense_in, rows_w_in, router_w_in, experts_in, out):
    with ExitStack() as ctx:
        sems = {}

        def sem(name):
            if name not in sems:
                sems[name] = ctx.enter_context(nc.semaphore(name))
            return sems[name]

        WORDS = 53100
        arena = ctx.enter_context(nc.sbuf_tensor("arena", [P, WORDS], F32))
        psum = ctx.enter_context(nc.psum_tensor("psum", [P, 8, 512], F32))
        n_iter_i = ctx.enter_context(nc.sbuf_tensor("n_iter_i", [P, 1], I32))

        def carve(start, *parts):
            at, n = {}, start
            for name, *shape in parts:
                size = int(np.prod(shape))
                v = arena[:, n:n + size]
                if len(shape) == 2:
                    v = v.rearrange("p (a b) -> p a b", b=shape[1])
                elif len(shape) == 3:
                    v = v.rearrange("p (a b c) -> p a b c", b=shape[1], c=shape[2])
                at[name] = v
                n += size
            assert n <= WORDS, (n, WORDS)
            return at, n

        ring, PHASE = carve(0, ("slots", RING, SLOT))
        ring = ring["slots"]
        A, FREE = carve(PHASE, ("gdn_qk", H, 2, T), ("gdn_v", H, T), ("kd", 2 * H, 2, P), ("k_in", 2 * H, P),
                        ("k_tail", 2 * H, P))
        assert FREE <= 6 * SLOT, FREE
        B, _ = carve(6 * SLOT,
                     ("c1", NC1), ("sm", NSM), ("rb", 72), ("x", DC, T), ("h", DC, T), ("sq", DC, T))
        c1, sm, rb, x, h, sq = (B[k] for k in ("c1", "sm", "rb", "x", "h", "sq"))
        LATE = _
        AA, _ = carve(FREE, ("eg", H, T))
        assert _ <= 6 * SLOT
        A.update(AA)
        AB, _ = carve(LATE, ("t", 2 * H, P), ("u", 2 * H, P), ("fox_q", H, T), ("fox_k", H, T), ("fox_v", TT, 512), ("sb_q", H, T), ("sb_k", H, T),
                      ("sb_v", TT, 512), ("gz", H, T), ("v_in", 2 * H, P),
                      ("lm", 2 * H, P), ("xx", 2 * H, P), ("state", H, P), ("s", 2, 384), ("pt", 2, 384),
                      ("vnew", 512), ("rows", 6, T), ("rows_w", DC, 12), ("tok", TT, 24), ("st", 32), ("rs", 2, T))
        A.update(AB)
        A["gsb"] = A["xx"].rearrange("p a b -> p (a b)").rearrange("p (a b) -> p a b", b=512)
        A["tmp"] = A["lm"].rearrange("p a b -> p (a b)")[:, 0:512]
        A["tmp2"] = carve(LATE, ("tmp2", 4, 512))[0]["tmp2"]
        A["mixed"] = carve(PHASE, ("mixed", DC, T))[0]["mixed"]
        M, _ = carve(LATE, ("mem", DC, T), ("hm", DC, T), ("q", H, T), ("k", H, T), ("v", TT, 512), ("s", 2, 512),
                     ("pt", 2, 512), ("st", 32), ("rs", 2, T), ("y", 3, 2, T), ("sa", 3, T), ("act", 4, T), ("raw", 2, H, T))
        R, _ = carve(LATE, ("c2", NC2), ("qraw", H, T), ("kraw", H, T), ("q", H, T), ("k", H, T), ("v", TT, 512),
                     ("g", H, T), ("gb", H, T), ("gc", H, T), ("cat", DC, T), ("pt", 2, 384), ("rs", 2, T))
        X, _ = carve(LATE, ("router_w", DC, 72), ("lg", TT, 72), ("one_g", TT, 8), ("el", TT, E), ("r", TT, 64),
                     ("gate", TT, E), ("member", TT, E), ("rank", TT, E), ("htok", TT, D), ("s", TT, GROUP * CAP),
                     ("sg", TT, GROUP * P), ("xt", DC, P), ("sil", P), ("act", P), ("actT", P), ("yb", T),
                     ("scat", T), ("zero", 512), ("count", 80), ("rs", T))

        def C(name, rows=P, lo=0, n=None, base=0):
            s = C1[name]
            n = s.stop - s.start if n is None else n
            return c1[base:base + rows, s.start + lo:s.start + lo + n]

        def S_(name, i=0, base=0, rows=P):
            c = SM[name].start + i
            return sm[base:base + rows, c:c + 1]

        ident = C("ident")

        class Banks:

            def __init__(self, name, banks):
                self.banks, self.name, self.units = banks, name, {}

            def fill(self, pe, unit):
                n = len(self.units)
                self.units[unit] = n
                b, use = n % len(self.banks), n // len(self.banks)
                if use:
                    pe.wait_ge(sem(f"{self.name}_empty{b}"), use)
                return psum[:, self.banks[b], :]

            def filled(self, ins, unit):
                ins.then_inc(sem(f"{self.name}_full{self.units[unit] % len(self.banks)}"), 1)

            def full(self, unit):
                n = self.units[unit]
                return sem(f"{self.name}_full{n % len(self.banks)}"), n // len(self.banks) + 1

            def wait(self, eng, unit):
                n = self.units[unit]
                eng.wait_ge(*self.full(unit))
                return psum[:, self.banks[n % len(self.banks)], :]

            def release(self, eng, unit):
                eng.sem_inc(sem(f"{self.name}_empty{self.units[unit] % len(self.banks)}"), 1)

            def emptied(self, ins, unit):
                ins.then_inc(sem(f"{self.name}_empty{self.units[unit] % len(self.banks)}"), 1)

        proj = Banks("proj", (0, 1, 2, 3))
        aux = Banks("aux", (4, 5, 6, 7))

        def half(v, w=T):
            return v.rearrange("p (a b) -> p a b", b=w)

        def slot(name):
            return ring[:, TILE[name] % RING, :]

        expert_gu = [arena[:, b * 3 * SLOT:b * 3 * SLOT + 2 * SLOT].rearrange("p (c g f) -> p c g f", c=DC, g=2)
                     for b in range(2)]
        expert_dn = [arena[:, b * 3 * SLOT + 2 * SLOT:(b + 1) * 3 * SLOT].rearrange("p (c d) -> p c d", d=D)
                     for b in range(2)]

        tile_done = {}
        block = ctx.enter_context(nc.Block())

        @block.tensor
        def _(pe):
            mm = nc.tensor.matmul

            def arrive(name):
                pe.wait_ge(sem(f"tile_loaded{TILE[name] % RING}"), 16 * (TILE[name] // RING + 1))

            def unit(name, u, src, ready=None, kc=DC, last_of_tile=None):
                w = slot(name).rearrange("p (k n) -> p k n", k=kc)
                units = w.shape[2] // P // 2
                if u == 0:
                    arrive(name)
                ps = half(proj.fill(pe, f"{name}{u}"))
                for i in range(2):
                    n = 2 * u + i
                    for k in range(kc):
                        if ready and i == 0:
                            pe.wait_ge(sem(ready), k + 1)
                        last = mm(ps[:, i, :], w[:, k, n * P:(n + 1) * P], src[:, k, :],
                                  start=(k == 0), stop=(k == kc - 1))
                proj.filled(last, f"{name}{u}")
                if u == units - 1:
                    tile_done[name] = proj.full(f"{name}{u}")

            def unit_tok(name, t, src):
                w = slot(name).rearrange("p (k n) -> p k n", k=DC)
                if t == 0:
                    arrive(name)
                ps = proj.fill(pe, f"{name}{t}")
                for k in range(DC):
                    last = mm(ps, src[:, k, t * P:(t + 1) * P], w[:, k, :], start=(k == 0), stop=(k == DC - 1))
                proj.filled(last, f"{name}{t}")
                if t == TT - 1:
                    tile_done[name] = proj.full(f"{name}{t}")

            def mean_square(name):
                ps = aux.fill(pe, f"ms_{name}")
                for k in range(DC):
                    pe.wait_ge(sem(f"sq_{name}"), k // 2 + 1)
                    last = mm(ps[:, 0:T], C("inv1024"), sq[:, k, :], start=(k == 0), stop=(k == DC - 1))
                aux.filled(last, f"ms_{name}")

            def head_sums(name, ready, src, width, weights="inv128"):
                for hd in range(H):
                    ps = aux.fill(pe, f"{name}{hd}")
                    pe.wait_ge(sem(ready), hd + 1)
                    aux.filled(mm(ps[:, 0:width], C(weights, n=P), src(hd), start=True, stop=True), f"{name}{hd}")

            pe.wait_ge(sem("consts_loaded"), 32)
            mean_square("mix")
            unit("gq", 0, h, "h_mix"); unit("gq", 1, h)
            unit("gk", 0, h); unit("gk", 1, h)
            unit("gv", 0, h); unit("gv", 1, h)
            pe.wait_ge(sem("rows_w_loaded"), 16)
            ps = aux.fill(pe, "rows")
            for k in range(DC):
                for j in range(3):
                    last = mm(ps[32 * j:32 * j + H, 0:T], A["rows_w"][:, k, j * H:(j + 1) * H], h[:, k, :],
                              start=(k == 0), stop=(k == DC - 1), skip_group_check=True)
            aux.filled(last, "rows")
            unit("gz", 0, h); unit("gz", 1, h)
            unit("fq", 0, h); unit("fq", 1, h)
            head_sums("gss", "gdn_sq", lambda hd: sq[:, 2 * hd:2 * hd + 2, :].rearrange("p a b -> p (a b)"), 512, "ones")
            unit("fk", 0, h); unit("fk", 1, h)
            pe.wait_ge(sem("gdn_rows"), 1)
            for unit_name, rows_of in (("tok", ((0, 64), (1, 64))), ("tok_beta", ((2, 32),))):
                ps = aux.fill(pe, unit_name)
                for t in range(TT):
                    for j, (row, base) in enumerate(rows_of):
                        o = (len(rows_of) * t + j) * H
                        last = mm(ps[:, o:o + H], A["rows"][base:base + H, row, t * P:(t + 1) * P],
                                  ident[base:base + H, base:base + H], start=True, stop=True)
                aux.filled(last, unit_name)
            for q in range(2):
                ps = half(aux.fill(pe, f"decay{q}"))
                for i in range(2):
                    hd = 2 * q + i
                    last = mm(ps[:, i, :], C("sel", H, hd * 256, P, 64), A["rows"][64:64 + H, 0, :], start=True, stop=True)
                aux.filled(last, f"decay{q}")
            unit_tok("fv", 0, h); unit_tok("fv", 1, h)
            head_sums("fss_q", "fox_sq_q", lambda hd: sq[:, hd, :], T)
            head_sums("fss_k", "fox_sq_k", lambda hd: sq[:, H + hd, :], T)
            unit("sq", 0, h); unit("sq", 1, h)
            for t in range(TT):
                for nm, src, ready in (("k", lambda hd: A["gdn_qk"][:, hd, 1, t * P:(t + 1) * P], "gdn_k"),
                                       ("v", lambda hd: A["gdn_v"][:, hd, t * P:(t + 1) * P], "gdn_v")):
                    pe.wait_ge(sem(ready), H)
                    ps = aux.fill(pe, f"turn_{nm}{t}")
                    for hd in range(H):
                        last = nc.tensor.transpose(ps[:, hd * P:(hd + 1) * P], src(hd), ident)
                    aux.filled(last, f"turn_{nm}{t}")
            unit("sk", 0, h); unit("sk", 1, h)
            for t in range(TT):
                for q in range(2):
                    ps = half(aux.fill(pe, f"kk{t}{q}"))
                    for i in range(2):
                        hd = 2 * q + i
                        tk = A["gdn_qk"][:, hd, :, t * P:(t + 1) * P]
                        last = mm(ps[:, i, :], tk[:, 1, :], tk, start=True, stop=True)
                    aux.filled(last, f"kk{t}{q}")
            unit_tok("sv", 0, h); unit_tok("sv", 1, h)

            def fox_scores(hd):
                ps = aux.fill(pe, f"fs{hd}")
                if hd == 0:
                    pe.wait_ge(sem("fox_c"), 1)
                pe.wait_ge(sem("fox_qn"), hd + 1)
                pe.wait_ge(sem("fox_kn"), hd + 1)
                cs = A["rows"][0:H, 3, :]
                for t, (lo, n) in enumerate(((0, P), (P, T))):
                    o = ps[:, lo:lo + n]
                    mm(o, A["fox_q"][:, hd, t * P:(t + 1) * P], A["fox_k"][:, hd, 0:n], start=True, stop=False)
                    mm(o, C("negsel", H, hd * P, P), cs[:, 0:n], start=False, stop=False)
                    last = mm(o, cs[:, t * P:(t + 1) * P], C("sel", H, hd * 256, n), start=False, stop=True)
                aux.filled(last, f"fs{hd}")

            def fox_turn(hd):
                ps = aux.fill(pe, f"fpt{hd}")
                pe.wait_ge(sem("fox_p"), hd + 1)
                for j in range(3):
                    last = nc.tensor.transpose(ps[:, j * P:(j + 1) * P],
                                               A["s"][:, hd % 2, (0, 128, 256)[j]:(0, 128, 256)[j] + P], ident)
                aux.filled(last, f"fpt{hd}")

            def pv(name, hd, ready, pt, v):
                ps = aux.fill(pe, f"{name}{hd}")
                pe.wait_ge(sem(ready), hd + 1)
                mm(ps[:, 0:T], v[:, 0, hd * P:(hd + 1) * P], pt[:, hd % 2, 0:T], start=True, stop=False,
                   skip_group_check=True)
                aux.filled(mm(ps[:, P:T], v[:, 1, hd * P:(hd + 1) * P], pt[:, hd % 2, T:384], start=False, stop=True,
                              skip_group_check=True), f"{name}{hd}")

            def sb_scores(hd):
                ps = aux.fill(pe, f"sz{hd}")
                if hd == 0:
                    pe.wait_ge(sem("sb_q"), 2)
                    pe.wait_ge(sem("sb_k"), 2)
                    pe.wait_ge(sem("sb_v"), 2)
                q, k = A["sb_q"][:, hd, :], A["sb_k"][:, hd, :]
                mm(ps[:, 0:T], k[:, 0:P], q, start=True, stop=False, skip_group_check=True)
                aux.filled(mm(ps[:, T:384], k[:, P:T], q[:, P:T], start=False, stop=False, skip_group_check=True),
                           f"sz{hd}")

            def sb_sums(hd):
                n = aux.units[f"sz{hd}"]
                ps = psum[:, 4 + n % 4, :]
                lk = A["s"][:, hd % 2, :]
                pe.wait_ge(sem("sb_lk"), hd + 1)
                mm(ps[:, 0:T], C("tri"), lk[:, 0:T], start=False, stop=False, skip_group_check=True)
                mm(ps[:, P:T], C("ones", n=P), lk[:, T:384], start=False, stop=False, skip_group_check=True)
                mm(ps[:, T:384], C("tri"), lk[:, T:384], start=False, stop=True,
                   skip_group_check=True).then_inc(sem("sb_sum"), 1)

            def solve_x(lv, t):
                ps = aux.fill(pe, f"x{lv}{t}")
                pe.wait_ge(sem("gdn_lm"), lv + 1)
                if lv:
                    pe.wait_ge(sem("gdn_t"), 2 * (lv - 1) + t + 1)
                for hd in range(H):
                    un = t * H + hd
                    last = mm(ps[:, hd * P:(hd + 1) * P], A["lm"][:, un, :], ident if lv == 0 else A["t"][:, un, :],
                              start=True, stop=True)
                aux.filled(last, f"x{lv}{t}")

            def solve_tu(lv, t):
                pe.wait_ge(sem("gdn_xx"), 2 * lv + t + 1)
                if lv:
                    pe.wait_ge(sem("gdn_u"), 2 * (lv - 1) + t + 1)
                for nm in ("t", "u"):
                    if nm == "t" and lv == len(LEVELS) - 1:
                        continue
                    ps = aux.fill(pe, f"{nm}{lv}{t}")
                    for hd in range(H):
                        un = t * H + hd
                        u = ident if lv == 0 else A["u"][:, un, :]
                        xx = A["xx"][:, un, :]
                        last = mm(ps[:, hd * P:(hd + 1) * P], u if nm == "t" else xx, xx if nm == "t" else u,
                                  start=True, stop=True)
                    aux.filled(last, f"{nm}{lv}{t}")

            def solve_uw(t):
                pe.wait_ge(sem("gdn_u"), 2 * (len(LEVELS) - 1) + t + 1)
                ps = aux.fill(pe, f"sol_u{t}")
                for hd in range(H):
                    un = t * H + hd
                    last = mm(ps[:, hd * P:(hd + 1) * P], A["u"][:, un, :], A["v_in"][:, un, :], start=True, stop=True)
                aux.filled(last, f"sol_u{t}")
                ps = aux.fill(pe, f"sol_w{t}")
                for hd in range(H):
                    un = t * H + hd
                    last = mm(ps[:, hd * P:(hd + 1) * P], A["k_in"][:, un, :], A["u"][:, un, :], start=True, stop=True)
                aux.filled(last, f"sol_w{t}")

            def state_v(n):
                t, po = n // 2, CHUNK * (n % 2)
                ps = aux.fill(pe, f"wS{n}")
                pe.wait_ge(sem("gdn_state"), n)
                for hd in range(H):
                    last = mm(ps[po:po + CHUNK, hd * P:(hd + 1) * P], A["k_in"][:, t * H + hd, po:po + CHUNK],
                              A["state"][:, hd, :], start=True, stop=True)
                aux.filled(last, f"wS{n}")

            def state_o(n):
                t, po = n // 2, CHUNK * (n % 2)
                ps = aux.fill(pe, f"o{n}")
                pe.wait_ge(sem("gdn_vnew"), n + 1)
                for hd in range(H):
                    un = t * H + hd
                    vn = A["vnew"][po:po + CHUNK, hd * P:(hd + 1) * P]
                    if n:
                        mm(ps[:, hd * CHUNK:(hd + 1) * CHUNK], A["state"][:, hd, :],
                           A["gdn_qk"][:, hd, 0, n * CHUNK:(n + 1) * CHUNK], start=True, stop=False)
                    last = mm(ps[:, hd * CHUNK:(hd + 1) * CHUNK], vn,
                              A["kd"][po:po + CHUNK, un, 0, po:po + CHUNK], start=(n == 0), stop=True)
                aux.filled(last, f"o{n}")
                if n == T // CHUNK - 1:
                    return
                ps = aux.fill(pe, f"dS{n}")
                for hd in range(H):
                    un = t * H + hd
                    last = mm(ps[:, hd * P:(hd + 1) * P], A["k_tail"][po:po + CHUNK, un, :],
                              A["vnew"][po:po + CHUNK, hd * P:(hd + 1) * P], start=True, stop=True)
                aux.filled(last, f"dS{n}")

            fill_in = iter([lambda: fox_scores(0), lambda: fox_scores(1),
                            lambda: fox_turn(0), lambda: (fox_turn(1), pv("fpv", 0, "fox_pT", A["pt"], A["fox_v"])),
                            lambda: (pv("fpv", 1, "fox_pT", A["pt"], A["fox_v"]), fox_scores(2)),
                            lambda: fox_scores(3), lambda: fox_turn(2),
                            lambda: (fox_turn(3), pv("fpv", 2, "fox_pT", A["pt"], A["fox_v"])),
                            lambda: pv("fpv", 3, "fox_pT", A["pt"], A["fox_v"])])

            def between():
                f = next(fill_in, None)
                if f:
                    f()
            for lv in range(len(LEVELS)):
                solve_x(lv, 0)
                solve_x(lv, 1)
                between()
                solve_tu(lv, 0)
                solve_tu(lv, 1)
                between()
            solve_uw(0)
            solve_uw(1)

            def gate(b, hf, p):
                unit(f"g{b}{hf}", p, h)

            def o_unit(b, hf, p, src, ready):
                name = f"o{b}"
                u = 2 * hf + p
                if u == 0:
                    pe.wait_ge(sem(ready), H)
                unit(name, u, src, None, H)

            def branch(b, src, ready, steps):
                steps = iter(steps)

                def step():
                    f = next(steps, None)
                    if f:
                        f()
                for hf in range(2):
                    for p in range(2):
                        gate(b, hf, p)
                        step()
                        o_unit(b, hf, p, src, ready)
                        step()

            branch("a", A["fox_q"], "ya", [
                lambda: (state_o(0), sb_scores(0)), lambda: sb_scores(1), lambda: state_v(1), lambda: sb_sums(0),
                lambda: (sb_sums(1), state_o(1)), lambda: pv("spv", 0, "sb_a", A["pt"], A["sb_v"]),
                lambda: (pv("spv", 1, "sb_a", A["pt"], A["sb_v"]), state_v(2)), lambda: sb_scores(2)])
            sb_scores(3)
            state_o(2)
            sb_sums(2)
            sb_sums(3)
            pv("spv", 2, "sb_a", A["pt"], A["sb_v"])
            pv("spv", 3, "sb_a", A["pt"], A["sb_v"])
            branch("c", A["sb_q"], "yc", [
                lambda: state_v(3), lambda: None, lambda: state_o(3), lambda: None,
                lambda: head_sums("oss", "gdn_osq", lambda hd: sq[:, hd, :], T)])
            branch("b", A["gdn_v"], "yb", [])
            for nm in ("out0", "out1"):
                unit(nm, 0, A["mixed"], "mixed")
                unit(nm, 1, A["mixed"])

            mean_square("mem")
            unit("mk", 0, M["hm"], "h_mem"); unit("mk", 1, M["hm"])
            unit_tok("mv", 0, M["hm"]); unit_tok("mv", 1, M["hm"])
            head_sums("mss_k", "mem_sq_k", lambda hd: M["raw"][:, 1, hd, :], T)
            mean_square("xq")
            unit("mq", 0, h, "h_xq"); unit("mq", 1, h)
            head_sums("mss_q", "mem_sq_q", lambda hd: M["raw"][:, 1, hd, :], T)

            def mem_scores(hd):
                ps = half(aux.fill(pe, f"mS{hd}"))
                pe.wait_ge(sem("mem_qk"), H + hd + 1)
                for t in range(TT):
                    last = mm(ps[:, t, :], M["q"][:, hd, t * P:(t + 1) * P], M["k"][:, hd, :], start=True, stop=True)
                aux.filled(last, f"mS{hd}")

            def mem_turn(hd):
                ps = aux.fill(pe, f"mpt{hd}")
                pe.wait_ge(sem("mem_p"), hd + 1)
                for kb in range(2):
                    for t in range(TT):
                        last = nc.tensor.transpose(ps[:, kb * T + t * P:kb * T + (t + 1) * P],
                                                   M["s"][:, hd % 2, t * T + kb * P:t * T + (kb + 1) * P], ident)
                aux.filled(last, f"mpt{hd}")

            def mem_pv(hd):
                ps = aux.fill(pe, f"mpv{hd}")
                pe.wait_ge(sem("mem_pT"), hd + 1)
                for kb in range(2):
                    last = mm(ps[:, 0:T], M["v"][:, kb, hd * P:(hd + 1) * P], M["pt"][:, hd % 2, kb * T:(kb + 1) * T],
                              start=(kb == 0), stop=(kb == 1))
                aux.filled(last, f"mpv{hd}")
            mem_scores(0)
            mem_scores(1)
            for hd in range(H):
                mem_turn(hd)
                mem_pv(hd)
                if hd + 2 < H:
                    mem_scores(hd + 2)
            pe.wait_ge(sem("ym"), H)
            for u in range(4):
                unit("mo", u, M["q"], None, H)

            mean_square("ffn")

            def up(c):
                w = slot(f"U{c // 2}").rearrange("p (k g n) -> p k g n", k=DC, g=2)
                if c % 2 == 0:
                    arrive(f"U{c // 2}")
                ps = half(proj.fill(pe, f"up{c}"))
                for g in range(2):
                    for k in range(DC):
                        if c == 0 and g == 0:
                            pe.wait_ge(sem("h_ffn"), k + 1)
                        last = mm(ps[:, g, :], w[:, k, g, (c % 2) * P:(c % 2 + 1) * P], h[:, k, :],
                                  start=(k == 0), stop=(k == DC - 1))
                proj.filled(last, f"up{c}")
                if c % 2:
                    tile_done[f"U{c // 2}"] = proj.full(f"up{c}")

            down_ps = [half(aux.fill(pe, f"down{b}")) for b in range(4)]

            def down(c):
                w = slot(f"D{c // 4}").rearrange("p (k n) -> p k n", k=4)
                if c % 4 == 0:
                    arrive(f"D{c // 4}")
                pe.wait_ge(sem("ffn_act"), c + 1)
                for n in range(DC):
                    last = mm(down_ps[n // 2][:, n % 2, :], w[:, c % 4, n * P:(n + 1) * P], M["act"][:, c % 4, :],
                              start=(c == 0 and n % 2 == 0), stop=(c == FC - 1), skip_group_check=True)
                    if c == FC - 1 and n % 2:
                        aux.filled(last, f"down{n // 2}")
                if c < FC - 1:
                    last.then_inc(sem("ffn_act_used"), 1)
                if c == FC - 1:
                    tile_done[f"D{c // 4}"] = aux.full("down3")
                elif c % 4 == 3:
                    tile_done[f"D{c // 4}"] = (sem("ffn_act_used"), c + 1)
            for c in range(FC + 2):
                if c < FC:
                    up(c)
                if c >= 2:
                    down(c - 2)

            mean_square("n1")
            pe.wait_ge(sem("c2_loaded"), 16)
            rot = R["c2"][:, C2["rot"]]

            def rotate(nm):
                for q in range(2):
                    ps = half(aux.fill(pe, f"rot_{nm}{q}"))
                    pe.wait_ge(sem(f"raw_{nm}"), q + 1)
                    for i in range(2):
                        last = mm(ps[:, i, :], rot, R[f"{nm}raw"][:, 2 * q + i, :], start=True, stop=True)
                    aux.filled(last, f"rot_{nm}{q}")
            unit("q2", 0, h, "h_n1"); unit("q2", 1, h)
            unit("k2", 0, h); rotate("q"); unit("k2", 1, h)
            unit_tok("v2", 0, h); rotate("k"); unit_tok("v2", 1, h)
            unit("g2", 0, h); unit("g2", 1, h)

            def ret_scores(hd):
                ps = aux.fill(pe, f"rs{hd}")
                pe.wait_ge(sem("ret_q"), hd // 2 + 1)
                pe.wait_ge(sem("ret_k"), hd // 2 + 1)
                q, k = R["q"][:, hd, :], R["k"][:, hd, :]
                mm(ps[:, 0:T], k[:, 0:P], q, start=True, stop=True)
                aux.filled(mm(ps[:, T:384], k[:, P:T], q[:, P:T], start=True, stop=True), f"rs{hd}")
            ret_scores(0); ret_scores(1)
            unit("gc2", 0, h)
            pe.wait_ge(sem("ret_v"), 2)
            pv("ro", 0, "ret_p", R["pt"], R["v"]); pv("ro", 1, "ret_p", R["pt"], R["v"])
            unit("gc2", 1, h)
            ret_scores(2); ret_scores(3)
            unit("u2", 0, h)
            pv("ro", 2, "ret_p", R["pt"], R["v"]); pv("ro", 3, "ret_p", R["pt"], R["v"])
            unit("u2", 1, h)
            head_sums("rm", "ret_o", lambda hd: R["qraw"][:, hd, :], T)
            unit("gb2", 0, h)
            head_sums("rv", "ret_d2", lambda hd: sq[:, hd, :], T)
            unit("gb2", 1, h)
            pe.wait_ge(sem("cat_ret"), H)
            pe.wait_ge(sem("cat_conv"), 2)
            for nm in ("o20", "o21"):
                unit(nm, 0, R["cat"])
                unit(nm, 1, R["cat"])

            mean_square("n2")
            pe.wait_ge(sem("router_w_loaded"), 16)
            pe.wait_ge(sem("rb_loaded"), 16)
            ps = aux.fill(pe, "router")
            for t in range(TT):
                o = ps[:, t * 72:(t + 1) * 72]
                for k in range(DC):
                    pe.wait_ge(sem("h_n2"), k + 1)
                    mm(o, h[:, k, t * P:(t + 1) * P], X["router_w"][:, k, :], start=(k == 0), stop=False)
                last = mm(o, C("ones", 1, 0, P), rb[0:1, :], start=False, stop=True)
            aux.filled(last, "router")
            for t in range(TT):
                for hf in range(2):
                    ps = proj.fill(pe, f"htok{t}{hf}")
                    for i in range(4):
                        last = nc.tensor.transpose(ps[:, i * P:(i + 1) * P], h[:, 4 * hf + i, t * P:(t + 1) * P], ident)
                    proj.filled(last, f"htok{t}{hf}")
            pe.wait_ge(sem("member"), 1)
            ps = aux.fill(pe, "rank")
            mm(ps[:, 0:E], C("before"), X["member"][:, 0, :], start=True, stop=True)
            mm(ps[:, E:2 * E], C("ones", n=P), X["member"][:, 0, :], start=True, stop=False)
            mm(ps[:, E:2 * E], C("before"), X["member"][:, 1, :], start=False, stop=True)
            mm(ps[:, 2 * E:3 * E], C("ones", n=P), X["member"][:, 0, :], start=True, stop=False)
            aux.filled(mm(ps[:, 2 * E:3 * E], C("ones", n=P), X["member"][:, 1, :], start=False, stop=True), "rank")

            pe.wait_ge(sem("htok"), 4)
            pe.wait_ge(sem("zeroed"), 1)
            for b in range(4):
                mm(psum[:, b, :], ident, X["zero"], start=True, stop=False, skip_group_check=True)
            pe.wait_ge(sem("ranked"), 1)
            pe.wait_ge(sem("n_iter"), 1)
            n_iter = pe.value_load(n_iter_i[0:1, 0:1], min_val=NG, max_val=NG * MAXPASS)
            with pe.Fori(0, n_iter) as i:
                pe.wait_ge(sem("places"), i + 1)
                for c in range(DC):
                    for t in range(TT):
                        last = mm(psum[:, 4 + c // 4, (c % 4) * P:(c % 4 + 1) * P], X["htok"][:, t, c * P:(c + 1) * P],
                                  X["s"][:, t, :], start=(t == 0), stop=(t == TT - 1))
                    if c == 3:
                        last.then_inc(sem("xt_lo"), 1)
                last.then_inc(sem("xt_hi"), 1)
                for j in range(GROUP):
                    q = i * GROUP + (j + 1)
                    b = j % 2
                    if j == 0:
                        pe.wait_ge(sem("xt_lo_kept"), i + 1)
                        pe.wait_ge(sem("xt_hi_kept"), i + 1)
                    pe.wait_ge(sem(f"gu_loaded{b}"), i * 32 + 16 * (j // 2 + 1))
                    for k in range(DC):
                        for s in range(4):
                            last = mm(half(psum[32 * s:32 * s + 32, 6, 0:256], P), X["xt"][:, k, CAP * j:CAP * (j + 1)],
                                      expert_gu[b][:, k, :, s * P:(s + 1) * P], start=(k == 0), stop=(k == DC - 1))
                    last.then_inc(sem("gate_up"), 1)
                    for t in range(TT):
                        last = nc.tensor.transpose(psum[:, 7, 256 + t * P:256 + (t + 1) * P],
                                                   X["sg"][:, t, j * P:(j + 1) * P], ident)
                    last.then_inc(sem("scatter"), 1)
                    pe.wait_ge(sem("e_act"), q)
                    nc.tensor.transpose(psum[:, 6, 256:384], X["act"], ident).then_inc(sem("e_turned"), 1)
                    pe.wait_ge(sem("e_actT"), q)
                    pe.wait_ge(sem("scatter_kept"), q)
                    pe.wait_ge(sem(f"dn_loaded{b}"), i * 32 + 16 * (j // 2 + 1))
                    for c in range(4):
                        for s in range(4):
                            last = mm(psum[32 * s:32 * s + 32, 7, 0:256], X["actT"][:, CAP * c:CAP * (c + 1)],
                                      expert_dn[b][:, c, s * T:(s + 1) * T], start=(c == 0), stop=(c == 3))
                    last.then_inc(sem("down"), 1)
                    pe.wait_ge(sem("e_y"), q)
                    for d in range(2):
                        for s in range(4):
                            last = mm(psum[:, s, d * T:(d + 1) * T], X["yb"][32 * s:32 * s + 32, d * P:(d + 1) * P],
                                      X["scat"][32 * s:32 * s + 32, :], start=False, stop=False, skip_group_check=True)
            for b in range(4):
                last = mm(psum[:, b, :], ident, X["zero"], start=False, stop=True, skip_group_check=True)
            last.then_inc(sem("moe_done"), 1)
            ps = psum[:, 4, :]
            for k in range(DC):
                pe.wait_ge(sem("sq_final"), k // 2 + 1)
                last = mm(ps[:, 0:T], C("inv1024"), sq[:, k, :], start=(k == 0), stop=(k == DC - 1))
            last.then_inc(sem("ms_final"), 1)

        @block.scalar
        def _(act):
            chain = [0]
            ac = nc.scalar.activation

            def link(ins):
                chain[0] += 1
                ins.then_inc(sem("act_chain"), 1)
                act.wait_ge(sem("act_chain"), chain[0])

            def root(unit, out, n=T):
                ps = aux.wait(act, unit)[:, 0:n]
                ps = ps if n == T else half(ps)
                link(ac(out, ps, ACT.Sqrt, bias=C("eps")))
                aux.release(act, unit)
                act.sem_inc(sem("root_ready"), 1)

            def squares(name, src, ready, step=1):
                for q in range(DC // 2):
                    act.wait_ge(sem(ready), step * (q + 1))
                    ac(sq[:, 2 * q:2 * q + 2, :], src[:, 2 * q:2 * q + 2, :], ACT.Square).then_inc(sem(f"sq_{name}"), 1)

            act.wait_ge(sem("consts_loaded"), 32)
            act.wait_ge(sem("x_loaded"), 16)
            for q in range(DC // 2):
                ac(sq[:, 2 * q:2 * q + 2, :], x[:, 2 * q:2 * q + 2, :], ACT.Square).then_inc(sem("sq_mix"), 1)
            root("ms_mix", sq[:, 0, :])
            cv = lambda ch, tap: S_("gdn_conv", 4 * ch + tap)

            def conv_dst(ch):
                return A["gdn_qk"][:, ch % H, ch // H, :] if ch < 2 * H else A["gdn_v"][:, ch % H, :]
            for nm, first in (("gq", 0), ("gk", H), ("gv", 2 * H)):
                for u in range(2):
                    ps = half(proj.wait(act, f"{nm}{u}"))
                    for i in range(2):
                        ch = first + 2 * u + i
                        last = ac(conv_dst(ch), ps[:, i, :], ACT.Copy, scale=cv(ch, 3))
                    last.then_inc(sem("gdn_tap"), 1)
            ps = aux.wait(act, "rows")
            rw = A["rows"]
            ac(rw[0:H, 4, :], ps[0:H, 0:T], ACT.Abs, bias=S_("rows", 0, 0, H))
            ac(rw[64:64 + H, 4, :], ps[64:64 + H, 0:T], ACT.Abs, bias=S_("rows", 2, 64, H))
            link(ac(rw[32:32 + H, 2, :], ps[32:32 + H, 0:T], ACT.Sigmoid))
            ac(rw[0:H, 4, :], rw[0:H, 4, :], ACT.Exp, scale=-1.0)
            ac(A["st"][64:64 + H, 30:31], S_("rows", 1, 64, H), ACT.Exp)
            link(ac(rw[64:64 + H, 4, :], rw[64:64 + H, 4, :], ACT.Exp, scale=-1.0))
            ac(rw[0:H, 5, :], rw[0:H, 4, :], ACT.Ln, bias=1.0)
            ac(rw[64:64 + H, 5, :], rw[64:64 + H, 4, :], ACT.Ln, bias=1.0).then_inc(sem("rows_ln"), 1)
            for ch in range(3 * H):
                act.wait_ge(sem("gdn_conv"), ch + 1)
                ins = ac(conv_dst(ch), conv_dst(ch), ACT.Silu)
                ins.then_inc(sem("gdn_silu" if ch < 2 * H else "gdn_v"), 1)
            for hd in range(H):
                act.wait_ge(sem("gdn_silu"), H + hd + 1)
                if hd == 0:
                    act.wait_ge(sem("h_mix"), DC)
                ac(sq[:, 2 * hd:2 * hd + 2, :], A["gdn_qk"][:, hd, :, :], ACT.Square).then_inc(sem("gdn_sq"), 1)
            for u in range(2):
                ps = proj.wait(act, f"gz{u}")
                proj.emptied(ac(A["gz"][:, 2 * u:2 * u + 2, :], half(ps), ACT.Silu), f"gz{u}")

            for hd in range(H):
                root(f"gss{hd}", sq[:, 2 * hd:2 * hd + 2, :], 512)
            act.wait_ge(sem("gdn_tail"), 1)
            ac(rw[64:64 + H, 1, :], rw[64:64 + H, 1, :], ACT.Exp).then_inc(sem("gdn_rows"), 1)
            for u in range(2):
                ps = proj.wait(act, f"fq{u}")
                proj.emptied(ac(A["fox_q"][:, 2 * u:2 * u + 2, :], half(ps), ACT.Copy), f"fq{u}")
            act.wait_ge(sem("gdn_cols"), 1)
            ac(A["tok"][:, :, 12:16], A["tok"][:, :, 0:4], ACT.Exp).then_inc(sem("gdn_egc"), 1)
            for q in range(2):
                ps = aux.wait(act, f"decay{q}")
                ac(A["eg"][:, 2 * q:2 * q + 2, :], half(ps), ACT.Exp).then_inc(sem("gdn_eg"), 1)
            for un in range(2 * H):
                act.wait_ge(sem("gdn_expo"), un + 1)
                ac(A["t"][:, un, :], A["t"][:, un, :], ACT.Exp).then_inc(sem("gdn_dt"), 1)
            for u in range(2):
                ps = proj.wait(act, f"fk{u}")
                link(ac(A["fox_k"][:, 2 * u:2 * u + 2, :], half(ps), ACT.Copy))
                proj.release(act, f"fk{u}")
            act.wait_ge(sem("gdn_k"), H)
            for hd in range(H):
                ac(sq[:, hd, :], A["fox_q"][:, hd, :], ACT.Square).then_inc(sem("fox_sq_q"), 1)
            for hd in range(H):
                ac(sq[:, H + hd, :], A["fox_k"][:, hd, :], ACT.Square).then_inc(sem("fox_sq_k"), 1)
            for j, nm in enumerate("qk"):
                for hd in range(H):
                    root(f"fss_{nm}{hd}", sq[:, j * H + hd, :])
            for t in range(TT):
                ps = proj.wait(act, f"fv{t}")
                ins = ac(A["fox_v"][:, t, :], ps, ACT.Copy)
                proj.emptied(ins, f"fv{t}")
            for u in range(2):
                ps = proj.wait(act, f"sq{u}")
                link(ac(A["sb_q"][:, 2 * u:2 * u + 2, :], half(ps), ACT.Copy, scale=SCALE))
                proj.release(act, f"sq{u}")
                act.sem_inc(sem("sb_q"), 1)
            act.wait_ge(sem("gdn_beg"), 1)
            for t in range(TT):
                ps = aux.wait(act, f"turn_k{t}")
                for hd in range(H):
                    un = t * H + hd
                    ac(A["k_in"][:, un, :], ps[:, hd * P:(hd + 1) * P], ACT.Copy, scale=A["tok"][:, t, 16 + hd:17 + hd])
                    last = ac(A["k_tail"][:, un, :], ps[:, hd * P:(hd + 1) * P], ACT.Copy,
                              scale=A["tok"][:, t, 4 + hd:5 + hd])
                aux.emptied(last, f"turn_k{t}")
                ps = aux.wait(act, f"turn_v{t}")
                for hd in range(H):
                    un = t * H + hd
                    last = ac(A["v_in"][:, un, :], ps[:, hd * P:(hd + 1) * P], ACT.Copy,
                              scale=A["tok"][:, t, 8 + hd:9 + hd])
                aux.emptied(last, f"turn_v{t}")
            for u in range(2):
                ps = proj.wait(act, f"sk{u}")
                link(ac(A["sb_k"][:, 2 * u:2 * u + 2, :], half(ps), ACT.Copy))
                proj.release(act, f"sk{u}")
                act.sem_inc(sem("sb_k"), 1)
            for t in range(TT):
                ps = proj.wait(act, f"sv{t}")
                link(ac(A["sb_v"][:, t, :], ps, ACT.Copy))
                proj.release(act, f"sv{t}")
                act.sem_inc(sem("sb_v"), 1)

            def solve_evac(lv, t):
                ps = aux.wait(act, f"x{lv}{t}")
                for hd in range(H):
                    un = t * H + hd
                    last = ac(A["xx"][:, un, :], ps[:, hd * P:(hd + 1) * P], ACT.Copy,
                              scale=A["tok"][:, t, 8 + hd:9 + hd])
                link(last)
                aux.release(act, f"x{lv}{t}")
                act.sem_inc(sem("gdn_xx"), 1)

            def softmax_exp(buf, st, pre, hd, spans):
                act.wait_ge(sem(f"{pre}_max"), hd + 1)
                for t, (lo, n) in enumerate(spans):
                    last = ac(buf[:, hd % 2, lo:lo + n], buf[:, hd % 2, lo:lo + n], ACT.Exp,
                              bias=st[:, 8 * (hd % 2) + 2 + t:8 * (hd % 2) + 3 + t],
                              accum_out=st[:, 8 * (hd % 2) + 4 + t:8 * (hd % 2) + 5 + t])
                last.then_inc(sem(f"{pre}_exp"), 1)
            FSP = ((0, P), (P, T))

            def turned(name, hd, buf, n, done):
                ps = aux.wait(act, f"{name}{hd}")
                link(ac(buf[:, hd % 2, 0:n], ps[:, 0:n], ACT.Copy))
                aux.release(act, f"{name}{hd}")
                act.sem_inc(sem(done), 1)

            steps = iter([lambda: softmax_exp(A["s"], A["st"], "fox", 0, FSP),
                          lambda: softmax_exp(A["s"], A["st"], "fox", 1, FSP),
                          lambda: turned("fpt", 0, A["pt"], 384, "fox_pT"),
                          lambda: turned("fpt", 1, A["pt"], 384, "fox_pT"),
                          lambda: softmax_exp(A["s"], A["st"], "fox", 2, FSP),
                          lambda: softmax_exp(A["s"], A["st"], "fox", 3, FSP),
                          lambda: turned("fpt", 2, A["pt"], 384, "fox_pT"),
                          lambda: turned("fpt", 3, A["pt"], 384, "fox_pT")])

            def between():
                f = next(steps, None)
                if f:
                    f()
            for lv in range(len(LEVELS)):
                solve_evac(lv, 0)
                solve_evac(lv, 1)
                between()
                between()
            for t in range(TT):
                ps = aux.wait(act, f"sol_w{t}")
                last = ac(A["k_in"][:, t * H:(t + 1) * H, :], half(ps, P), ACT.Copy, scale=-1.0)
                link(last)
                aux.release(act, f"sol_w{t}")
                act.sem_inc(sem("gdn_w"), 1)

            def sb_log(hd):
                ps = aux.wait(act, f"sz{hd}")
                if hd >= 2:
                    act.wait_ge(sem("yc"), hd - 1)
                w = A["pt"][:, hd % 2, :]
                if hd == 0:
                    act.wait_ge(sem("ya"), H)
                link(ac(w, ps[:, 0:384], ACT.Abs))
                link(ac(w, w, ACT.Exp, scale=-1.0))
                ac(w, w, ACT.Ln, bias=1.0).then_inc(sem("sb_ln"), 1)

            def sb_exp(hd):
                act.wait_ge(sem("sb_s"), hd + 1)
                ac(A["pt"][:, hd % 2, :], A["s"][:, hd % 2, :], ACT.Exp).then_inc(sem("sb_a"), 1)
            ng = [0]

            def gates(b, hf, p):
                ps = half(proj.wait(act, f"g{b}{hf}{p}"))
                n = ng[0]
                if n >= 2:
                    act.wait_ge(sem("gate_used"), n - 1)
                for i in range(2):
                    br = "abc".index(b)
                    last = ac(A["gsb"][:, n % 2, i * T:(i + 1) * T], ps[:, i, :], ACT.Sigmoid,
                              bias=S_("gate_b", br * DC + hf * 4 + 2 * p + i))
                link(last)
                proj.release(act, f"g{b}{hf}{p}")
                act.sem_inc(sem("gate"), 1)
                ng[0] += 1

            def o_evac(n):
                ps = aux.wait(act, f"o{n}")
                link(ac(A["gdn_v"][:, :, n * CHUNK:(n + 1) * CHUNK], half(ps[:, 0:256], CHUNK), ACT.Copy))
                aux.release(act, f"o{n}")
            gates("a", 0, 0); o_evac(0); sb_log(0); gates("a", 0, 1); sb_log(1); gates("a", 1, 0)
            sb_exp(0); o_evac(1); sb_exp(1); gates("a", 1, 1)
            sb_log(2); sb_log(3); o_evac(2); sb_exp(2); sb_exp(3)
            gates("c", 0, 0); gates("c", 0, 1)
            o_evac(3)
            for hd in range(H):
                ac(sq[:, hd, :], A["gdn_v"][:, hd, :], ACT.Square).then_inc(sem("gdn_osq"), 1)
            gates("c", 1, 0)
            for hd in range(H):
                root(f"oss{hd}", sq[:, hd, :])
            gates("c", 1, 1)
            for hf in range(2):
                for p in range(2):
                    gates("b", hf, p)

            act.wait_ge(sem("mixed"), DC)
            act.wait_ge(sem("mem_loaded"), 16)
            for q in range(DC // 2):
                ac(sq[:, 2 * q:2 * q + 2, :], M["mem"][:, 2 * q:2 * q + 2, :], ACT.Square).then_inc(sem("sq_mem"), 1)
            root("ms_mem", sq[:, 0, :])
            for u in range(2):
                ps = proj.wait(act, f"mk{u}")
                ac(M["raw"][:, 1, 2 * u:2 * u + 2, :], half(ps), ACT.Square)
                link(ac(M["k"][:, 2 * u:2 * u + 2, :], half(ps), ACT.Copy))
                proj.release(act, f"mk{u}")
                act.sem_inc(sem("mem_sq_k"), 2)
            for t in range(TT):
                ps = proj.wait(act, f"mv{t}")
                proj.emptied(ac(M["v"][:, t, :], ps, ACT.Copy), f"mv{t}")
            for hd in range(H):
                root(f"mss_k{hd}", M["raw"][:, 1, hd, :])
            act.wait_ge(sem("h_mem"), DC)
            squares("xq", x, "x1")
            root("ms_xq", sq[:, 0, :])
            act.wait_ge(sem("mem_qk"), H)
            for u in range(2):
                ps = proj.wait(act, f"mq{u}")
                ac(M["raw"][:, 1, 2 * u:2 * u + 2, :], half(ps), ACT.Square)
                link(ac(M["q"][:, 2 * u:2 * u + 2, :], half(ps), ACT.Copy))
                proj.release(act, f"mq{u}")
                act.sem_inc(sem("mem_sq_q"), 2)
            for hd in range(H):
                root(f"mss_q{hd}", M["raw"][:, 1, hd, :])
            MSP = ((0, T), (T, T))
            softmax_exp(M["s"], M["st"], "mem", 0, MSP)
            for hd in range(H):
                if hd + 1 < H and hd < 1:
                    softmax_exp(M["s"], M["st"], "mem", hd + 1, MSP)
                turned("mpt", hd, M["pt"], 512, "mem_pT")
                if hd + 2 < H:
                    softmax_exp(M["s"], M["st"], "mem", hd + 2, MSP)

            act.wait_ge(sem("h_xq"), DC)
            squares("ffn", x, "x2")
            root("ms_ffn", sq[:, 0, :])

            def tap(c):
                ps = half(proj.wait(act, f"up{c}"))
                if c >= 3:
                    act.wait_ge(sem("ffn_act"), c - 2)
                for g in range(2):
                    ch = g * FC + c
                    last = ac(M["y"][:, c % 3, g, :], ps[:, g, :], ACT.Identity, bias=S_("ffn_b", ch),
                              scale=S_("ffn_conv", 3 * ch + 2))
                last.then_inc(sem("ffn_tap"), 1)

            def silu(c):
                act.wait_ge(sem("ffn_conv"), c + 1)
                ac(M["sa"][:, c % 3, :], M["y"][:, c % 3, 0, :], ACT.Silu).then_inc(sem("ffn_silu"), 1)
            for c in range(FC + 1):
                if c < FC:
                    tap(c)
                if c:
                    silu(c - 1)

            act.wait_ge(sem("h_ffn"), DC)
            squares("n1", x, "x3")
            root("ms_n1", sq[:, 0, :])
            act.wait_ge(sem("c2_loaded"), 16)
            for nm in ("q", "k"):
                for u in range(2):
                    ps = proj.wait(act, f"{nm}2{u}")
                    link(ac(R[f"{nm}raw"][:, 2 * u:2 * u + 2, :], half(ps), ACT.Copy))
                    proj.release(act, f"{nm}2{u}")
                    act.sem_inc(sem(f"raw_{nm}"), 1)
            for t in range(TT):
                ps = proj.wait(act, f"v2{t}")
                link(ac(R["v"][:, t, :], ps, ACT.Copy))
                proj.release(act, f"v2{t}")
                act.sem_inc(sem("ret_v"), 1)
            for u in range(2):
                ps = proj.wait(act, f"g2{u}")
                proj.emptied(ac(R["g"][:, 2 * u:2 * u + 2, :], half(ps), ACT.Silu), f"g2{u}")

            def ret_out(hd):
                ps = aux.wait(act, f"ro{hd}")
                if hd == 0:
                    act.wait_ge(sem("ret_q"), 2)
                link(ac(R["qraw"][:, hd, :], ps[:, 0:T], ACT.Copy))
                aux.release(act, f"ro{hd}")
                act.sem_inc(sem("ret_o"), 1)
            for u in range(2):
                ps = proj.wait(act, f"gc2{u}")
                link(ac(R["gc"][:, 2 * u:2 * u + 2, :], half(ps), ACT.Copy))
                proj.release(act, f"gc2{u}")
                act.sem_inc(sem("conv_gc"), 1)
                ret_out(2 * u) if u == 0 else None
                ret_out(1) if u == 0 else None
            ret_out(2)
            ret_out(3)
            for u in range(2):
                act.wait_ge(sem("conv_in"), u + 1)
                for i in range(2):
                    ch = 2 * u + i
                    last = ac(R["cat"][:, H + ch, :], R["gc"][:, ch, :], ACT.Copy, scale=S_("conv2", 3 * ch + 2))
                last.then_inc(sem("conv_tap"), 1)
            for hd in range(H):
                act.wait_ge(sem("ret_d"), hd + 1)
                if hd == 0:
                    act.wait_ge(sem("h_n1"), DC)
                ac(sq[:, hd, :], R["qraw"][:, hd, :], ACT.Square).then_inc(sem("ret_d2"), 1)
            for hd in range(H):
                root(f"rv{hd}", sq[:, hd, :])
            for u in range(2):
                ps = proj.wait(act, f"gb2{u}")
                link(ac(R["gb"][:, 2 * u:2 * u + 2, :], half(ps), ACT.Copy))
                proj.release(act, f"gb2{u}")
                act.sem_inc(sem("conv_gb"), 1)
            act.wait_ge(sem("cat_ret"), H)
            squares("n2", x, "x4")
            root("ms_n2", sq[:, 0, :])

            for t in range(TT):
                for hf in range(2):
                    ps = proj.wait(act, f"htok{t}{hf}")
                    ac(X["htok"][:, t, hf * 512:(hf + 1) * 512], ps, ACT.Copy).then_inc(sem("htok"), 1)
            act.wait_ge(sem("group_max"), 1)
            for t in range(TT):
                last = ac(X["r"][:, t, 8:16], X["lg"][:, t, 0:8], ACT.Exp, bias=X["r"][:, t, 1:2],
                          accum_out=X["r"][:, t, 2:3])
            last.then_inc(sem("group_exp"), 1)
            act.wait_ge(sem("expert_max"), 1)
            ac(X["r"][:, :, 6:7], X["r"][:, :, 5:6], ACT.Exp).then_inc(sem("expert_exp"), 1)

            act.wait_ge(sem("n_iter"), 1)
            n_iter = act.value_load(n_iter_i[0:1, 0:1], min_val=NG, max_val=NG * MAXPASS)
            with act.Fori(0, n_iter) as i:
                act.wait_ge(sem("xt_lo"), i + 1)
                ac(X["xt"][:, 0:4, :], half(psum[:, 4, :], P), ACT.Copy).then_inc(sem("xt_lo_kept"), 1)
                for j in range(GROUP):
                    q = i * GROUP + (j + 1)
                    act.wait_ge(sem("gate_up"), q)
                    ac(X["sil"], psum[:, 6, 0:P], ACT.Silu).then_inc(sem("e_silu"), 1)
                    act.wait_ge(sem("scatter"), q)
                    ac(X["scat"], psum[:, 7, 256:512], ACT.Copy).then_inc(sem("scatter_kept"), 1)
                    act.wait_ge(sem("e_turned"), q)
                    ac(X["actT"], psum[:, 6, 256:384], ACT.Copy).then_inc(sem("e_actT"), 1)
            squares("final", x, "x5")
            act.wait_ge(sem("ms_final"), 1)
            ac(sq[:, 0, :], psum[:, 4, 0:T], ACT.Sqrt, bias=C("eps")).then_inc(sem("root_ready"), 1)

        @block.vector
        def _(dve):
            V = nc.vector
            chain = [0]

            def link(ins):
                chain[0] += 1
                ins.then_inc(sem("dve_chain"), 1)
                dve.wait_ge(sem("dve_chain"), chain[0])

            roots = [0]

            def inverse_root(rs):
                roots[0] += 1
                dve.wait_ge(sem("root_ready"), roots[0])
                link(V.reciprocal(rs, rs))

            def normalise(name, src, dst, gain):
                rs = sq[:, 0, :]
                inverse_root(rs)
                for k in range(DC):
                    last = V.scalar_tensor_tensor(dst[:, k, :], src[:, k, :], S_(gain, k), rs, ALU.mult, ALU.mult)
                    last.then_inc(sem(f"h_{name}"), 1)

            dve.wait_ge(sem("consts_loaded"), 32)
            dve.wait_ge(sem("x_loaded"), 16)
            normalise("mix", x, h, "norm_mix")
            V.tensor_scalar(A["st"][:, 24:25], S_("fox_q"), SCALE, None, ALU.mult)

            def conv_dst(ch):
                return A["gdn_qk"][:, ch % H, ch // H, :] if ch < 2 * H else A["gdn_v"][:, ch % H, :]
            nu = 0
            for nm, first in (("gq", 0), ("gk", H), ("gv", 2 * H)):
                for u in range(2):
                    ps = half(proj.wait(dve, f"{nm}{u}"))
                    nu += 1
                    dve.wait_ge(sem("gdn_tap"), nu)
                    for s in (1, 2, 3):
                        for i in range(2):
                            ch = first + 2 * u + i
                            o = conv_dst(ch)[:, s:T]
                            ins = V.scalar_tensor_tensor(o, ps[:, i, 0:T - s], S_("gdn_conv", 4 * ch + 3 - s), o,
                                                         ALU.mult, ALU.add)
                            if s == 3:
                                ins.then_inc(sem("gdn_conv"), 1)
                        if s < 3:
                            link(ins)
                    dve.wait_ge(sem("gdn_conv"), 2 * nu)
                    proj.release(dve, f"{nm}{u}")
            ps = aux.wait(dve, "rows")
            dve.wait_ge(sem("rows_ln"), 1)
            rw = A["rows"]
            V.tensor_scalar(rw[0:H, 4, :], ps[0:H, 0:T], S_("rows", 0, 0, H), 0.0, ALU.add, ALU.min)
            link(V.tensor_scalar(rw[64:64 + H, 4, :], ps[64:64 + H, 0:T], S_("rows", 2, 64, H), 0.0, ALU.add, ALU.max))
            V.tensor_tensor(rw[0:H, 4, :], rw[0:H, 4, :], rw[0:H, 5, :], ALU.subtract)
            link(V.tensor_tensor(rw[64:64 + H, 4, :], rw[64:64 + H, 4, :], rw[64:64 + H, 5, :], ALU.add))
            aux.emptied(V.tensor_tensor_scan(rw[0:H, 3, :], C("ones", H), rw[0:H, 4, :], 0.0, ALU.mult, ALU.add), "rows")
            link(V.tensor_scalar(rw[64:64 + H, 4, :], rw[64:64 + H, 4, :], A["st"][64:64 + H, 30:31], -1.0, ALU.mult, ALU.mult))
            dve.sem_inc(sem("fox_c"), 1)
            link(V.tensor_tensor_scan(rw[64:64 + H, 0, :], C("reset", H, base=64), rw[64:64 + H, 4, :], 0.0, ALU.mult, ALU.add))
            g4 = half(rw[64:64 + H, 0, :], CHUNK)
            V.tensor_tensor(half(rw[64:64 + H, 1, :], CHUNK),
                            g4[:, :, CHUNK - 1:CHUNK].broadcast_to([H, T // CHUNK, CHUNK]), g4,
                            ALU.subtract).then_inc(sem("gdn_tail"), 1)

            for hd in range(H):
                rs = sq[:, 2 * hd:2 * hd + 2, :]
                inverse_root(rs)
                V.scalar_tensor_tensor(A["gdn_qk"][:, hd, 0, :], A["gdn_qk"][:, hd, 0, :], SCALE, rs[:, 0, :],
                                       ALU.mult, ALU.mult)
                V.tensor_tensor(A["gdn_qk"][:, hd, 1, :], A["gdn_qk"][:, hd, 1, :], rs[:, 1, :],
                                ALU.mult).then_inc(sem("gdn_k"), 1)
            ps = aux.wait(dve, "tok")
            aux.emptied(V.tensor_copy(A["tok"][:, :, 0:8], half(ps[:, 0:16], 8)), "tok")
            ps = aux.wait(dve, "tok_beta")
            link(V.tensor_copy(A["tok"][:, :, 8:12], half(ps[:, 0:8], 4)))
            aux.release(dve, "tok_beta")
            dve.sem_inc(sem("gdn_cols"), 1)
            dve.wait_ge(sem("gdn_egc"), 1)
            V.tensor_tensor(A["tok"][:, :, 16:20], A["tok"][:, :, 8:12], A["tok"][:, :, 12:16],
                            ALU.mult).then_inc(sem("gdn_beg"), 1)
            for q in range(2):
                ps = half(aux.wait(dve, f"decay{q}"))
                dve.wait_ge(sem("gdn_eg"), q + 1)
                for i in range(2):
                    hd = 2 * q + i
                    for t in range(TT):
                        un = q * H + 2 * i + t
                        last = V.scalar_tensor_tensor(A["t"][:, un, :], ps[:, i, t * P:(t + 1) * P],
                                                      A["tok"][:, t, hd:hd + 1], C("chunk_mask"), ALU.subtract, ALU.add)
                        last.then_inc(sem("gdn_expo"), 1)
                dve.wait_ge(sem("gdn_expo"), 4 * (q + 1))
                aux.release(dve, f"decay{q}")
            for nm, gain in (("q", A["st"][:, 24:25]), ("k", S_("fox_k"))):
                for hd in range(H):
                    rs = sq[:, (0 if nm == "q" else H) + hd, :]
                    inverse_root(rs)
                    o = A[f"fox_{nm}"][:, hd, :]
                    V.scalar_tensor_tensor(o, o, gain, rs, ALU.mult, ALU.mult).then_inc(sem(f"fox_{nm}n"), 1)
            for t in range(TT):
                for q in range(2):
                    ps = half(aux.wait(dve, f"kk{t}{q}"))
                    if t == 0 and q == 0:
                        dve.wait_ge(sem("gdn_dt"), 2 * H)
                    for i in range(2):
                        hd = 2 * q + i
                        dt = A["t"][:, 2 * hd + t, :].rearrange("p (a b) -> p a b", a=1).broadcast_to([P, 2, P])
                        last = V.tensor_tensor(A["kd"][:, t * H + hd, :, :], half(ps[:, i, :], P), dt, ALU.mult)
                    link(last)
                    aux.release(dve, f"kk{t}{q}")
            V.tensor_tensor(A["gdn_qk"][:, :, 0, :], A["gdn_qk"][:, :, 0, :], A["eg"], ALU.mult)

            def lm(lv):
                m = C("levels", lo=lv * P, n=P).rearrange("p (a b) -> p a b", a=1).broadcast_to([P, 2 * H, P])
                V.tensor_tensor(A["lm"], A["kd"][:, :, 1, :], m, ALU.mult).then_inc(sem("gdn_lm"), 1)

            def solve_sub(lv, t, nm):
                ps = half(aux.wait(dve, f"{nm}{lv}{t}"), P)
                o = A[nm][:, t * H:(t + 1) * H, :]
                src = ident.rearrange("p (a b) -> p a b", a=1).broadcast_to([P, H, P]) if lv == 0 else o
                link(V.tensor_tensor(o, src, ps, ALU.subtract))
                aux.release(dve, f"{nm}{lv}{t}")
                dve.sem_inc(sem(f"gdn_{nm}"), 1)

            def softmax_max(buf, st, pre, unit, hd, spans, mask):
                n = spans[-1][0] + spans[-1][1]
                s = buf[:, hd % 2, 0:n]
                st = st[:, 8 * (hd % 2):8 * (hd % 2) + 8]
                ps = aux.wait(dve, f"{unit}{hd}")
                if hd >= 2:
                    dve.wait_ge(sem(f"{pre}_pT"), hd - 1)
                link(V.tensor_copy(s, ps[:, 0:n]) if mask is None else V.tensor_tensor(s, ps[:, 0:n], mask, ALU.add))
                aux.release(dve, f"{unit}{hd}")
                for t, (lo, w) in enumerate(spans):
                    last = V.reduce_max(st[:, t:t + 1], s[:, lo:lo + w], AX)
                link(last)
                V.tensor_scalar(st[:, 2:4], st[:, 0:2], -1.0, None, ALU.mult).then_inc(sem(f"{pre}_max"), 1)

            def softmax_norm(buf, st, pre, hd, spans):
                st = st[:, 8 * (hd % 2):8 * (hd % 2) + 8]
                dve.wait_ge(sem(f"{pre}_exp"), hd + 1)
                link(V.reciprocal(st[:, 6:8], st[:, 4:6]))
                for t, (lo, w) in enumerate(spans):
                    o = buf[:, hd % 2, lo:lo + w]
                    last = V.tensor_scalar(o, o, st[:, 6 + t:7 + t], None, ALU.mult)
                last.then_inc(sem(f"{pre}_p"), 1)

            def head_out(unit, hd, dst, done):
                ps = aux.wait(dve, f"{unit}{hd}")
                link(V.tensor_copy(dst[:, hd, :], ps[:, 0:T]))
                aux.release(dve, f"{unit}{hd}")
                dve.sem_inc(sem(done), 1)
            FSP = ((0, P), (P, T))
            fmax = lambda hd: softmax_max(A["s"], A["st"], "fox", "fs", hd, FSP, C("fox_mask"))
            fnorm = lambda hd: softmax_norm(A["s"], A["st"], "fox", hd, FSP)
            fout = lambda hd: head_out("fpv", hd, A["fox_q"], "ya")
            steps = iter([lambda: fmax(0), lambda: (fmax(1), fnorm(0)), lambda: fnorm(1), lambda: fout(0),
                          lambda: (fout(1), fmax(2)), lambda: (fmax(3), fnorm(2)), lambda: fnorm(3), lambda: fout(2),
                          lambda: fout(3)])

            def between():
                f = next(steps, None)
                if f:
                    f()
            lm(0)
            for lv in range(len(LEVELS)):
                between()
                for t in range(TT):
                    for nm in ("t", "u"):
                        if nm == "u" or lv < len(LEVELS) - 1:
                            solve_sub(lv, t, nm)
                if lv + 1 < len(LEVELS):
                    lm(lv + 1)
                between()
            for t in range(TT):
                ps = aux.wait(dve, f"sol_u{t}")
                link(V.tensor_copy(A["v_in"][:, t * H:(t + 1) * H, :], half(ps, P)))
                aux.release(dve, f"sol_u{t}")
            V.tensor_copy(A["vnew"][0:CHUNK, :].rearrange("p (a b) -> p a b", b=P),
                          A["v_in"][0:CHUNK, 0:H, :]).then_inc(sem("gdn_vnew"), 1)
            dve.wait_ge(sem("gdn_w"), 2)

            def state(n):
                ps = aux.wait(dve, f"dS{n}")
                for hd in range(H):
                    o, d = A["state"][:, hd, :], ps[:, hd * P:(hd + 1) * P]
                    if n == 0:
                        last = V.tensor_copy(o, d)
                    else:
                        last = V.scalar_tensor_tensor(o, o, A["eg"][:, hd, (n + 1) * CHUNK - 1:(n + 1) * CHUNK], d,
                                                      ALU.mult, ALU.add)
                link(last)
                aux.release(dve, f"dS{n}")
                dve.sem_inc(sem("gdn_state"), 1)

            def vnew(n):
                t, po = n // 2, CHUNK * (n % 2)
                ps = aux.wait(dve, f"wS{n}")
                link(V.tensor_tensor(half(A["vnew"][po:po + CHUNK, :], P), A["v_in"][po:po + CHUNK, t * H:(t + 1) * H, :],
                                     half(ps[po:po + CHUNK, :], P), ALU.add))
                aux.release(dve, f"wS{n}")
                dve.sem_inc(sem("gdn_vnew"), 1)

            def sb_keep(hd):
                ps = psum[:, 4 + aux.units[f"sz{hd}"] % 4, 0:384]
                s = A["s"][:, hd % 2, :]
                dve.wait_ge(sem("sb_ln"), hd + 1)
                link(V.scalar_tensor_tensor(s, ps, 0.0, A["pt"][:, hd % 2, :], ALU.max, ALU.add))
                V.tensor_tensor(s, s, C("sb_neg"), ALU.mult).then_inc(sem("sb_lk"), 1)

            def sb_masked(hd):
                dve.wait_ge(sem("sb_sum"), hd + 1)
                ps = psum[:, 4 + aux.units[f"sz{hd}"] % 4, 0:384]
                link(V.tensor_tensor(A["s"][:, hd % 2, :], ps, C("sb_mask"), ALU.add))
                aux.release(dve, f"sz{hd}")
                dve.sem_inc(sem("sb_s"), 1)
            ng = [0]

            def mix(b, hf, p):
                n = ng[0]
                u = 2 * hf + p
                ps = proj.wait(dve, f"o{b}{u}")
                dve.wait_ge(sem("gate"), n + 1)
                g = A["gsb"][:, n % 2, :]
                o = A["mixed"][:, 2 * u:2 * u + 2, :].rearrange("p a b -> p (a b)")
                if b == "a":
                    link(V.tensor_tensor(A["tmp2"][:, u, :], ps, g, ALU.mult))
                elif b == "c":
                    link(V.tensor_tensor(A["tmp"], ps, g, ALU.mult))
                    link(V.tensor_tensor(A["tmp2"][:, u, :], A["tmp2"][:, u, :], A["tmp"], ALU.add))
                else:
                    link(V.tensor_tensor(A["tmp"], ps, g, ALU.mult))
                    V.tensor_tensor(o, A["tmp2"][:, u, :], A["tmp"], ALU.add).then_inc(sem("mixed"), 2)
                    dve.wait_ge(sem("mixed"), 2 * (u + 1))
                proj.release(dve, f"o{b}{u}")
                dve.sem_inc(sem("gate_used"), 1)
                ng[0] += 1
            sbout = lambda hd: head_out("spv", hd, A["sb_q"], "yc")
            mix("a", 0, 0); state(0); sb_keep(0); sb_keep(1); mix("a", 0, 1); vnew(1); sb_masked(0)
            mix("a", 1, 0); state(1); sb_masked(1); sbout(0); sbout(1); vnew(2); mix("a", 1, 1)
            sb_keep(2); sb_keep(3); state(2); sb_masked(2); sb_masked(3); sbout(2); sbout(3)
            mix("c", 0, 0); vnew(3); mix("c", 0, 1)
            mix("c", 1, 0)
            for hd in range(H):
                rs = sq[:, hd, :]
                inverse_root(rs)
                o = A["gdn_v"][:, hd, :]
                link(V.scalar_tensor_tensor(o, o, S_("gdn_o"), rs, ALU.mult, ALU.mult))
                link(V.tensor_tensor(o, o, A["gz"][:, hd, :], ALU.mult))
                dve.sem_inc(sem("yb"), 1)
            mix("c", 1, 1)
            for hf in range(2):
                for p in range(2):
                    mix("b", hf, p)

            def residual(names, done):
                n = 0
                for nm in names:
                    ps = proj.wait(dve, nm)
                    o = x[:, 2 * n:2 * n + 2, :]
                    link(V.tensor_tensor(o, o, half(ps), ALU.add))
                    proj.release(dve, nm)
                    dve.sem_inc(sem(done), 1)
                    n += 1
            residual(("out00", "out01", "out10", "out11"), "x1")
            normalise("mem", M["mem"], M["hm"], "norm_mem")
            V.tensor_scalar(M["st"][:, 24:25], S_("mq"), SCALE, None, ALU.mult)

            def mem_norm(nm, gain, base):
                for hd in range(H):
                    rs = M["raw"][:, 1, hd, :]
                    inverse_root(rs)
                    o = M[nm][:, hd, :]
                    V.scalar_tensor_tensor(o, o, gain, rs, ALU.mult, ALU.mult).then_inc(sem("mem_qk"), 1)
            mem_norm("k", S_("mk"), 0)
            normalise("xq", x, h, "norm_xq")
            mem_norm("q", M["st"][:, 24:25], H)
            MSP = ((0, T), (T, T))
            mmax = lambda hd: softmax_max(M["s"], M["st"], "mem", "mS", hd, MSP, None)
            mnorm = lambda hd: softmax_norm(M["s"], M["st"], "mem", hd, MSP)
            mout = lambda hd: head_out("mpv", hd, M["q"], "ym")
            mmax(0); mmax(1); mnorm(0); mnorm(1)
            for hd in range(H):
                mout(hd)
                if hd + 2 < H:
                    mmax(hd + 2)
                    mnorm(hd + 2)
            residual(("mo0", "mo1", "mo2", "mo3"), "x2")

            normalise("ffn", x, h, "norm_ffn")

            def taps(c):
                ps = half(proj.wait(dve, f"up{c}"))
                dve.wait_ge(sem("ffn_tap"), c + 1)
                for s in (1, 2):
                    for g in range(2):
                        ch = g * FC + c
                        o = M["y"][:, c % 3, g, s:T]
                        last = V.scalar_tensor_tensor(o, ps[:, g, 0:T - s], S_("ffn_conv", 3 * ch + 2 - s), o,
                                                      ALU.mult, ALU.add)
                    link(last)
                proj.release(dve, f"up{c}")
                dve.sem_inc(sem("ffn_conv"), 1)

            def product(c):
                dve.wait_ge(sem("ffn_silu"), c + 1)
                if c >= 4:
                    dve.wait_ge(sem("ffn_act_used"), c - 3)
                V.tensor_tensor(M["act"][:, c % 4, :], M["sa"][:, c % 3, :], M["y"][:, c % 3, 1, :],
                                ALU.mult).then_inc(sem("ffn_act"), 1)
            for c in range(FC + 1):
                if c < FC:
                    taps(c)
                if c:
                    product(c - 1)
            for b in range(4):
                ps = aux.wait(dve, f"down{b}")
                o = x[:, 2 * b:2 * b + 2, :]
                link(V.tensor_tensor(o, o, half(ps), ALU.add))
                aux.release(dve, f"down{b}")
                dve.sem_inc(sem("x3"), 1)

            normalise("n1", x, h, "norm1")
            dve.wait_ge(sem("c2_loaded"), 16)

            def rotary(nm):
                cos, sin = (R["c2"][:, C2[f"{f}{nm}"]].rearrange("p (a b) -> p a b", a=1).broadcast_to([P, 2, T])
                            for f in ("cos", "sin"))
                for q in range(2):
                    ps = half(aux.wait(dve, f"rot_{nm}{q}"))
                    raw, o = R[f"{nm}raw"][:, 2 * q:2 * q + 2, :], R[nm][:, 2 * q:2 * q + 2, :]
                    V.tensor_tensor(o, ps, sin, ALU.mult)
                    link(V.tensor_tensor(raw, raw, cos, ALU.mult))
                    link(V.tensor_tensor(o, o, raw, ALU.add))
                    aux.release(dve, f"rot_{nm}{q}")
                    dve.sem_inc(sem(f"ret_{nm}"), 1)
            rotary("q")
            rotary("k")

            def ret_decay(hd):
                ps = aux.wait(dve, f"rs{hd}")
                if hd >= 2:
                    dve.wait_ge(sem("ret_o"), hd - 1)
                d0 = C2["decay"].start + hd * 384
                link(V.tensor_tensor(R["pt"][:, hd % 2, :], ps[:, 0:384], R["c2"][:, d0:d0 + 384], ALU.mult))
                aux.release(dve, f"rs{hd}")
                dve.sem_inc(sem("ret_p"), 1)
            for hd in range(H):
                ret_decay(hd)
            for u in range(2):
                ps = half(proj.wait(dve, f"u2{u}"))
                dve.wait_ge(sem("conv_gc"), u + 1)
                o = R["gc"][:, 2 * u:2 * u + 2, :]
                link(V.tensor_tensor(o, o, ps, ALU.mult))
                proj.release(dve, f"u2{u}")
                dve.sem_inc(sem("conv_in"), 1)
            for hd in range(H):
                ps = aux.wait(dve, f"rm{hd}")
                o = R["qraw"][:, hd, :]
                link(V.tensor_tensor(o, o, ps[:, 0:T], ALU.subtract))
                aux.release(dve, f"rm{hd}")
                dve.sem_inc(sem("ret_d"), 1)
            for u in range(2):
                dve.wait_ge(sem("conv_tap"), u + 1)
                for s in (1, 2):
                    for i in range(2):
                        ch = 2 * u + i
                        o = R["cat"][:, H + ch, s:T]
                        last = V.scalar_tensor_tensor(o, R["gc"][:, ch, 0:T - s], S_("conv2", 3 * ch + 2 - s), o,
                                                      ALU.mult, ALU.add)
                    link(last)
            for hd in range(H):
                rs = sq[:, hd, :]
                inverse_root(rs)
                o = R["qraw"][:, hd, :]
                link(V.scalar_tensor_tensor(o, o, S_("ret_gn", hd), rs, ALU.mult, ALU.mult))
                link(V.tensor_tensor(R["cat"][:, hd, :], o, R["g"][:, hd, :], ALU.mult))
                dve.sem_inc(sem("cat_ret"), 1)
            for u in range(2):
                dve.wait_ge(sem("conv_gb"), u + 1)
                o = R["cat"][:, H + 2 * u:H + 2 * u + 2, :]
                V.tensor_tensor(o, o, R["gb"][:, 2 * u:2 * u + 2, :], ALU.mult).then_inc(sem("cat_conv"), 1)
            residual(("o200", "o201", "o210", "o211"), "x4")

            normalise("n2", x, h, "norm2")
            link(V.memset(X["zero"], 0.0))
            dve.sem_inc(sem("zeroed"), 1)
            ps = aux.wait(dve, "router")
            lg, r = X["lg"], X["r"]
            link(V.tensor_copy(lg, half(ps[:, 0:2 * 72], 72)))
            aux.release(dve, "router")
            link(V.tensor_reduce(r[:, :, 0:1], lg[:, :, 0:8], AX, ALU.max))
            link(V.tensor_scalar(r[:, :, 1:2], r[:, :, 0:1], -1.0, None, ALU.mult))
            dve.sem_inc(sem("group_max"), 1)

            def first_of_max(dst, src, top):
                for t in range(TT):
                    last = V.scalar_tensor_tensor(r[:, t, 16:24], src[:, t, :], r[:, t, top:top + 1], C("first", n=8),
                                                  ALU.is_ge, ALU.mult)
                link(last)
                link(V.tensor_reduce(r[:, :, 24:25], r[:, :, 16:24], AX, ALU.max))
                for t in range(TT):
                    last = V.tensor_scalar(dst[:, t, :], r[:, t, 16:24], r[:, t, 24:25], None, ALU.is_equal)
                link(last)
            first_of_max(X["one_g"], lg[:, :, 0:8], 0)
            for t in range(TT):
                oh = X["one_g"][:, t, :].rearrange("p (a b) -> p a b", b=1).broadcast_to([P, 8, 8])
                last = V.tensor_tensor(half(X["el"][:, t, :], 8), half(lg[:, t, 8:72], 8), oh, ALU.mult)
            link(last)
            for t in range(TT):
                last = V.tensor_reduce(r[:, t, 32:40], X["el"][:, t, :].rearrange("p (g e) -> p e g", e=8), AX, ALU.add)
            link(last)
            link(V.tensor_reduce(r[:, :, 3:4], r[:, :, 32:40], AX, ALU.max))
            first_of_max(r[:, :, 40:48], r[:, :, 32:40], 3)
            for t in range(TT):
                last = V.scalar_tensor_tensor(r[:, t, 32:40], r[:, t, 40:48], NEG, r[:, t, 32:40], ALU.mult, ALU.add)
            link(last)
            link(V.tensor_reduce(r[:, :, 4:5], r[:, :, 32:40], AX, ALU.max))
            first_of_max(r[:, :, 48:56], r[:, :, 32:40], 4)
            V.tensor_tensor(r[:, :, 5:6], r[:, :, 4:5], r[:, :, 3:4], ALU.subtract).then_inc(sem("expert_max"), 1)
            link(V.tensor_tensor(r[:, :, 56:64], r[:, :, 40:48], r[:, :, 48:56], ALU.add))
            for t in range(TT):
                oh = X["one_g"][:, t, :].rearrange("p (a b) -> p a b", b=1).broadcast_to([P, 8, 8])
                ee = r[:, t, 56:64].rearrange("p (a b) -> p a b", a=1).broadcast_to([P, 8, 8])
                last = V.tensor_tensor(half(X["member"][:, t, :], 8), oh, ee, ALU.mult)
            last.then_inc(sem("member"), 1)
            dve.wait_ge(sem("group_exp"), 1)
            dve.wait_ge(sem("expert_exp"), 1)
            link(V.tensor_scalar(r[:, :, 7:8], r[:, :, 6:7], 1.0, None, ALU.add))
            link(V.tensor_tensor(r[:, :, 7:8], r[:, :, 7:8], r[:, :, 2:3], ALU.mult))
            link(V.reciprocal(r[:, :, 7:8], r[:, :, 7:8]))
            link(V.tensor_tensor(r[:, :, 6:7], r[:, :, 6:7], r[:, :, 7:8], ALU.mult))
            for t in range(TT):
                last = V.tensor_scalar(r[:, t, 40:48], r[:, t, 40:48], r[:, t, 7:8], None, ALU.mult)
            link(last)
            for t in range(TT):
                last = V.scalar_tensor_tensor(r[:, t, 40:48], r[:, t, 48:56], r[:, t, 6:7], r[:, t, 40:48],
                                              ALU.mult, ALU.add)
            link(last)
            for t in range(TT):
                oh = X["one_g"][:, t, :].rearrange("p (a b) -> p a b", b=1).broadcast_to([P, 8, 8])
                ee = r[:, t, 40:48].rearrange("p (a b) -> p a b", a=1).broadcast_to([P, 8, 8])
                last = V.tensor_tensor(half(X["gate"][:, t, :], 8), oh, ee, ALU.mult)
            link(last)
            ps = aux.wait(dve, "rank")
            V.tensor_reduce(X["count"][:, 0:1], ps[:, 2 * E:3 * E], AX, ALU.max)
            link(V.scalar_tensor_tensor(X["rank"], half(ps[:, 0:2 * E], E), 2.0 * T, X["member"], ALU.add, ALU.mult))
            link(V.tensor_scalar(X["rank"], X["rank"], -2.0 * T, None, ALU.add))
            dve.sem_inc(sem("ranked"), 1)
            link(V.tensor_scalar(X["count"][:, 8:8 + MAXPASS - 1], C("steps"), X["count"][:, 0:1], float(NG),
                                 ALU.is_lt, ALU.mult))
            link(V.tensor_reduce(X["count"][:, 1:2], X["count"][:, 8:8 + MAXPASS - 1], AX, ALU.add))
            link(V.tensor_scalar(X["count"][:, 1:2], X["count"][:, 1:2], float(NG), None, ALU.add))
            V.tensor_copy(n_iter_i[:, :], X["count"][:, 1:2]).then_inc(sem("n_iter"), 1)

            def places(g0, done):
                for t in range(TT):
                    rk = X["rank"][:, t, bass.ds(g0, GROUP)]
                    last = V.tensor_tensor(half(X["s"][:, t, :], CAP),
                                           C("slots").rearrange("p (a b) -> p a b", a=1).broadcast_to([P, GROUP, CAP]),
                                           rk.rearrange("p (a b) -> p a b", b=1).broadcast_to([P, GROUP, CAP]),
                                           ALU.is_equal)
                last.then_inc(sem("placed"), 1)

            def gated(g0):
                for t in range(TT):
                    gt = X["gate"][:, t, bass.ds(g0, GROUP)]
                    s = X["s"][:, t, :].rearrange("p (a r c) -> p a r c", a=GROUP, r=1).broadcast_to([P, GROUP, 4, CAP])
                    last = V.tensor_tensor(X["sg"][:, t, :].rearrange("p (a r c) -> p a r c", a=GROUP, r=4), s,
                                           gt.rearrange("p (a r c) -> p a r c", r=1, c=1).broadcast_to([P, GROUP, 4, CAP]),
                                           ALU.mult)
                    rk = X["rank"][:, t, bass.ds(g0, GROUP)]
                    last = V.tensor_scalar(rk, rk, -float(CAP), None, ALU.add)
                last.then_inc(sem("places"), 1)
            dve.wait_ge(sem("n_iter"), 1)
            n_iter = dve.value_load(n_iter_i[0:1, 0:1], min_val=NG, max_val=NG * MAXPASS)
            places(0, 0)
            dve.wait_ge(sem("placed"), 1)
            gated(0)
            with dve.Fori(0, n_iter) as i:
                dve.wait_ge(sem("xt_hi"), i + 1)
                V.tensor_copy(X["xt"][:, 4:8, :], half(psum[:, 5, :], P)).then_inc(sem("xt_hi_kept"), 1)
                for j in range(GROUP):
                    q = i * GROUP + (j + 1)
                    dve.wait_ge(sem("e_silu"), q)
                    V.tensor_tensor(X["act"], X["sil"], psum[:, 6, P:2 * P], ALU.mult).then_inc(sem("e_act"), 1)
                    dve.wait_ge(sem("down"), q)
                    V.tensor_copy(X["yb"], psum[:, 7, 0:256]).then_inc(sem("e_y"), 1)
                g0 = ((i + 1) % NG) * GROUP
                dve.wait_ge(sem("places"), i + 1)
                places(g0, i)
                dve.wait_ge(sem("placed"), i + 2)
                gated(g0)
            dve.wait_ge(sem("moe_done"), 1)
            for b in range(4):
                o = x[:, 2 * b:2 * b + 2, :]
                V.tensor_tensor(o, o, half(psum[:, b, :]), ALU.add).then_inc(sem("x5"), 1)
            dve.wait_ge(sem("x5"), 4)
            inverse_root(sq[:, 0, :])
            for k in range(DC):
                V.scalar_tensor_tensor(h[:, k, :], x[:, k, :], S_("final", k), sq[:, 0, :], ALU.mult,
                                       ALU.mult).then_inc(sem("result"), 1)

        @block.sync
        def _(sp):
            sp.dma_start(x, x_in).then_inc(sem("x_loaded"), 16)
            sp.dma_start(c1, c1_in).then_inc(sem("consts_loaded"), 16)
            sp.dma_start(sm, sm_in).then_inc(sem("consts_loaded"), 16)
            sp.dma_start(A["rows_w"], rows_w_in).then_inc(sem("rows_w_loaded"), 16)
            sp.dma_start(rb[0:1, :], rb_in).then_inc(sem("rb_loaded"), 16)
            for n, name in enumerate(TILES):
                if n >= RING:
                    sp.wait_ge(*tile_done[TILES[n - RING]])
                if name == "mk":
                    sp.wait_ge(sem("mixed"), DC)
                    sp.dma_start(M["mem"], mem_in).then_inc(sem("mem_loaded"), 16)
                if name == "q2":
                    sp.wait_ge(sem("x3"), 4)
                    sp.dma_start(R["c2"], c2_in).then_inc(sem("c2_loaded"), 16)
                words = SLOT if name != f"D{FC // 4}" else SLOT // 2
                sp.dma_start(ring[:, n % RING, 0:words], dense_in[n, :, 0:words]).then_inc(sem(f"tile_loaded{n % RING}"), 16)

            def load(e, b):
                sp.dma_start(expert_gu[b].rearrange("p c g f -> p (c g f)"),
                             experts_in[e, :, 0:2 * SLOT]).then_inc(sem(f"gu_loaded{b}"), 16)

            def load_down(e, b):
                sp.dma_start(expert_dn[b].rearrange("p c d -> p (c d)"),
                             experts_in[e, :, 2 * SLOT:3 * SLOT]).then_inc(sem(f"dn_loaded{b}"), 16)
            for s in range(RING):
                sp.wait_ge(*tile_done[[name for name in TILES if TILE[name] % RING == s][-1]])
                if s == 1:
                    load(0, 0)
                if s == 2:
                    load_down(0, 0)
                if s == 3:
                    load(1, 1)
                    load_down(1, 1)
            sp.wait_ge(sem("x4"), 4)
            sp.dma_start(X["router_w"], router_w_in).then_inc(sem("router_w_loaded"), 16)
            for e in (2, 3):
                sp.wait_ge(sem("gate_up"), e - 1)
                load(e, e % 2)
                sp.wait_ge(sem("down"), e - 1)
                load_down(e, e % 2)
            sp.wait_ge(sem("n_iter"), 1)
            n_iter = sp.value_load(n_iter_i[0:1, 0:1], min_val=NG, max_val=NG * MAXPASS)
            with sp.Fori(1, n_iter) as i:
                for j in range(GROUP):
                    e = (i % NG) * GROUP + j
                    sp.wait_ge(sem("gate_up"), i * GROUP + (j - 1))
                    load_e = sp.snap(e)
                    sp.dma_start(expert_gu[j % 2].rearrange("p c g f -> p (c g f)"),
                                 experts_in[bass.ds(load_e, 1), :, 0:2 * SLOT].rearrange("a p w -> p (a w)")
                                 ).then_inc(sem(f"gu_loaded{j % 2}"), 16)
                    sp.wait_ge(sem("down"), i * GROUP + (j - 1))
                    sp.dma_start(expert_dn[j % 2].rearrange("p c d -> p (c d)"),
                                 experts_in[bass.ds(load_e, 1), :, 2 * SLOT:3 * SLOT].rearrange("a p w -> p (a w)")
                                 ).then_inc(sem(f"dn_loaded{j % 2}"), 16)
            for q in range(4):
                sp.wait_ge(sem("result"), 2 * (q + 1))
                sp.dma_start(out[:, 2 * q:2 * q + 2, :], h[:, 2 * q:2 * q + 2, :]).then_inc(sem("stored"), 16)
            sp.wait_ge(sem("stored"), 64)




def constants():
    i = np.arange(P)
    c1 = np.zeros((P, NC1), np.float32)

    def put(c, at, name, v):
        c[:, at[name]] = v
    put(c1, C1, "ident", np.eye(P))
    put(c1, C1, "ones", 1.0)
    put(c1, C1, "inv128", 1.0 / P)
    put(c1, C1, "inv1024", 1.0 / D)
    put(c1, C1, "tri", i[:, None] >= i[None, :])
    put(c1, C1, "before", i[:, None] < i[None, :])
    causal = np.where(i[None, :] <= i[:, None], 0.0, NEG)
    put(c1, C1, "fox_mask", np.concatenate([causal, np.zeros((P, P)), causal], 1))
    strict = i[:, None] < i[None, :]
    full = np.ones((P, P), bool)
    ok = np.concatenate([strict, full, strict], 1)
    put(c1, C1, "sb_neg", np.where(ok, -1.0, 0.0))
    put(c1, C1, "sb_mask", np.where(ok, 0.0, NEG))
    same = i[:, None] // CHUNK == i[None, :] // CHUNK
    put(c1, C1, "chunk_mask", np.where(same & (i[None, :] >= i[:, None]), 0.0, NEG))
    lv = []
    for s in LEVELS:
        lv.append((i[:, None] // (2 * s) == i[None, :] // (2 * s)) & (i[:, None] // s % 2 == 0) & (i[None, :] // s % 2 == 1))
    put(c1, C1, "levels", np.concatenate(lv, 1))
    for hd in range(H):
        c1[i % 32 == hd, C1["sel"].start + hd * 256:C1["sel"].start + (hd + 1) * 256] = 1.0
        c1[i % 32 == hd, C1["negsel"].start + hd * P:C1["negsel"].start + (hd + 1) * P] = -1.0
    put(c1, C1, "slots", np.arange(CAP)[None, :])
    put(c1, C1, "first", E - np.arange(E)[None, :])
    put(c1, C1, "reset", (np.arange(T) % CHUNK != 0)[None, :])
    put(c1, C1, "steps", CAP * np.arange(1, MAXPASS)[None, :])
    put(c1, C1, "eps", EPS)
    c2 = np.zeros((P, NC2), np.float32)
    hf = P // 2
    rot = np.zeros((P, P))
    rot[i[:hf] + hf, i[:hf]] = -1.0
    rot[i[:hf], i[:hf] + hf] = 1.0
    put(c2, C2, "rot", rot)
    inv = (np.float32(10000.0) ** (-np.arange(hf, dtype=np.float32) / np.float32(hf))).astype(np.float32)
    ang = (np.arange(T, dtype=np.float32)[None, :] * inv[:, None]).astype(np.float32)
    cos, sin = np.tile(np.cos(ang), (2, 1)), np.tile(np.sin(ang), (2, 1))
    put(c2, C2, "cosq", cos * SCALE)
    put(c2, C2, "sinq", sin * SCALE)
    put(c2, C2, "cosk", cos)
    put(c2, C2, "sink", sin)
    for hd in range(H):
        lg = np.log1p(-(2.0 ** (-5.0 - hd)))
        rel = (i[None, :] - i[:, None]).astype(np.float64)
        diag = np.where(rel >= 0, np.exp(lg * np.maximum(rel, 0)), 0.0)
        off = np.exp(lg * (rel + P))
        o = C2["decay"].start + hd * 384
        c2[:, o:o + 384] = np.concatenate([diag, off, diag], 1)
    return c1, c2


def kernel(**inputs):
    import concourse.bacc as bacc
    from concourse.bass_utils import run_bass_kernel_spmd

    a = {k: np.asarray(v) for k, v in inputs.items()}
    f32 = np.float32

    def chunks(v):
        return np.ascontiguousarray(v.reshape(-1, P).T)

    def tile(w):
        return w.reshape(-1, P, w.shape[1]).transpose(1, 0, 2)

    c1, c2 = constants()
    sm = np.zeros((P, NSM), f32)

    def put(name, v):
        sm[:, SM[name]] = v
    for name, key in (("norm_mix", "norm_mix"), ("norm_xq", "norm_xq"), ("norm_mem", "norm_mem"), ("norm_ffn", "norm_ffn"),
                      ("norm1", "norm1_w_2"), ("norm2", "norm2_w_2"), ("final", "final_norm_w_2"), ("fox_q", "fox_qnorm"),
                      ("fox_k", "fox_knorm"), ("gdn_o", "gdn_onorm"), ("mq", "mq_norm"), ("mk", "mk_norm"),
                      ("ret_gn", "ret_gn_w_2"), ("gate_b", "gate_bias"), ("ffn_b", "ffn_conv_b")):
        put(name, chunks(a[key].reshape(-1)))
    for name, key in (("gdn_conv", "gdn_conv"), ("ffn_conv", "ffn_conv"), ("conv2", "conv_w_2")):
        w = a[key][0]
        put(name, w.reshape(w.shape[0], -1, P).transpose(2, 1, 0).reshape(P, -1))
    r0 = SM["rows"].start
    sm[0:H, r0] = a["fox_fbias"][0]
    sm[64:64 + H, r0 + 1] = a["gdn_a_log"][0]
    sm[64:64 + H, r0 + 2] = a["gdn_dt_bias"][0]

    win = a["w_in"][0]
    col, n = {}, 0
    for name, width in (("fq", 512), ("fk", 512), ("fv", 512), ("ff", 4), ("gq", 512), ("gk", 512), ("gv", 512), ("gb", 4),
                        ("ga", 4), ("gz", 512), ("sq", 512), ("sk", 512), ("sv", 512), ("gate", 3072)):
        col[name] = win[:, n:n + width]
        n += width
    rows_w = np.ascontiguousarray(tile(np.concatenate([col["ff"], col["gb"], col["ga"]], 1)))
    win2, wo2 = a["w_in_2"][0], a["w_o_2"][0]
    dense = np.zeros((len(TILES), P, SLOT), f32)

    def lay(name, w):
        v = tile(w).reshape(P, -1)
        dense[TILE[name], :, 0:v.shape[1]] = v
    for name in ("gq", "gk", "gv", "gz", "fq", "fk", "fv", "sq", "sk", "sv"):
        lay(name, col[name])
    for bn, b in enumerate("abc"):
        for hf in range(2):
            lay(f"g{b}{hf}", col["gate"][:, bn * D + hf * 512:bn * D + (hf + 1) * 512])
        lay(f"o{b}", a[f"w_o{b}"][0])
    for hf in range(2):
        lay(f"out{hf}", a["w_out"][0][:, hf * 512:(hf + 1) * 512])
        lay(f"o2{hf}", wo2[:, hf * 512:(hf + 1) * 512])
    lay("mk", a["w_mkv"][0][:, 0:512])
    lay("mv", a["w_mkv"][0][:, 512:1024])
    lay("mq", a["w_mq"][0])
    lay("mo", a["w_mo"][0])
    up, dn = a["w_up"][0], a["w_down"][0]
    for j in range(FC // 2):
        lay(f"U{j}", np.concatenate([up[:, j * 256:(j + 1) * 256], up[:, FC * P + j * 256:FC * P + (j + 1) * 256]], 1))
    for j in range(FC // 4 + 1):
        lay(f"D{j}", dn[j * 512:(j + 1) * 512])
    for j, name in enumerate(("q2", "k2", "v2", "g2", "gb2", "gc2", "u2")):
        lay(name, win2[:, j * 512:(j + 1) * 512])
    router_w = np.ascontiguousarray(tile(np.concatenate(
        [a["router_g_w_2"][0], a["router_e_w_2"][0].transpose(1, 0, 2).reshape(D, E)], 1)))
    rb = np.ascontiguousarray(np.concatenate([a["router_g_b_2"][0], a["router_e_b_2"][0].reshape(-1)])[None, :])
    experts = np.empty((E, P, 3 * SLOT), f32)
    ev = experts.reshape(E, P, 3, SLOT)
    gub = np.stack([a["w_gate_2"][0], a["w_up_2"][0]], 2).reshape(E, DC, P, 1024).transpose(0, 2, 1, 3)
    ev[:, :, 0] = gub[:, :, 0:4].reshape(E, P, SLOT)
    ev[:, :, 1] = gub[:, :, 4:8].reshape(E, P, SLOT)
    ev[:, :, 2] = a["w_down_2"][0].reshape(E, 4, P, D).transpose(0, 2, 1, 3).reshape(E, P, SLOT)
    del gub

    def features(v):
        return np.ascontiguousarray(v[0].T.reshape(DC, P, T).transpose(1, 0, 2))

    nc = bacc.Bacc("TRN2", target_bir_lowering=False, num_devices=1)
    arrays, args = {}, []
    for name, v in (("c1", c1), ("c2", c2), ("small", sm), ("router_b", rb), ("x_t", features(a["x"])),
                    ("mem_t", features(a["mem"])), ("dense", dense), ("rows_w", rows_w), ("router_w", router_w),
                    ("experts", experts)):
        arrays[name] = v
        args.append(nc.dram_tensor(name, v.shape, mybir.dt.from_np(v.dtype), kind="ExternalInput").ap())
    args.append(nc.dram_tensor("out_t", (P, DC, T), F32, kind="ExternalOutput").ap())
    program(nc, *args)
    r = run_bass_kernel_spmd(nc, [arrays], core_ids=[0])
    got = r.results[0]["out_t"]
    return np.ascontiguousarray(got.transpose(1, 0, 2).reshape(D, T).T)[None]
```

```python
from contextlib import ExitStack

import numpy as np

import concourse.bass as bass
from concourse import mybir

ALU = mybir.AluOpType
ACT = mybir.ActivationFunctionType
F32 = mybir.dt.float32
I32 = mybir.dt.int32
F32R = mybir.dt.float32r
AX = mybir.AxisListType.X

P = 128
T = 256
TT = T // P
D = 1024
DC = D // P
H = 4
CHUNK = 64
LEVELS = (1, 2, 4, 8, 16, 32)
FC = 2816 // P
E = 64
CAP = 32
GROUP = 4
NG = E // GROUP
MAXPASS = T // CAP
EPS = 1e-6
SCALE = P ** -0.5
NEG = -1e30
SLOT = 4096
UNIT = 2048
RAW = 5
HIGH = 3



def columns(*parts):
    at, n = {}, 0
    for name, width in parts:
        at[name] = slice(n, n + width)
        n += width
    return at, n


C1, NC1 = columns(("ident", P), ("ones", 256), ("inv128", P), ("inv1024", P), ("eps", 1), ("tri", P), ("before", P),
                  ("fox_mask", 384), ("sb_neg", 384), ("sb_mask", 384), ("chunk_mask", P),
                  ("levels", P * len(LEVELS)), ("sel", H * 256), ("negsel", H * P), ("slots", CAP),
                  ("first", E), ("reset", T), ("steps", MAXPASS - 1))
C1_EARLY = C1["tri"].start
C2, NC2 = columns(("rot", P), ("cosq", T), ("sinq", T), ("cosk", T), ("sink", T), ("decay", H * 384))
SM, NSM = columns(("norm_mix", DC), ("norm_xq", DC), ("norm_mem", DC), ("norm_ffn", DC), ("norm1", DC),
                  ("norm2", DC), ("final", DC), ("fox_q", 1), ("fox_k", 1), ("gdn_o", 1), ("mq", 1), ("mk", 1),
                  ("ret_gn", H), ("gate_b", 3 * DC), ("gdn_conv", 48), ("ffn_conv", 6 * FC), ("ffn_b", 2 * FC),
                  ("conv2", 12), ("rows", 3))
UNITS = [f"{_w}{_u}" for _w in ("gq", "gk", "gv", "gz", "fq", "fk", "fv", "sq", "sk", "sv") for _u in range(2)]
for _b in "acb":
    UNITS += [f"g{_b}00", f"g{_b}01", f"o{_b}_0", f"g{_b}10", f"g{_b}11", f"o{_b}_1"]
UNITS += [f"{_w}{_u}" for _w in ("out0", "out1", "mk", "mv", "mq", "mo_") for _u in range(2)]
UNITS += ["U0", "U1"]
for _j in range(FC // 2):
    UNITS += [f"U{_c}" for _c in (2 * _j + 2, 2 * _j + 3) if _c < FC] + [f"D{_j}"]
UNITS += [f"{_w}{_u}" for _w in ("q2", "k2", "v2", "g2", "gc2", "u2", "gb2", "o20", "o21") for _u in range(2)]
ORDER = {name: n for n, name in enumerate(UNITS)}


def program(nc, c1_in, c2_in, sm_in, rb_in, x_in, mem_in, dense_in, rows_w_in, router_w_in, experts_in, out):
    with ExitStack() as ctx:
        sems = {}

        def sem(name):
            if name not in sems:
                sems[name] = ctx.enter_context(nc.semaphore(name))
            return sems[name]

        WORDS = 53100
        arena_at = -(-nc.sbuf_base // 32) * 32
        arena = ctx.enter_context(nc.sbuf_tensor("arena", [P, WORDS], F32))
        psum = ctx.enter_context(nc.psum_tensor("psum", [P, 8, 512], F32))
        n_iter_i = ctx.enter_context(nc.sbuf_tensor("n_iter_i", [P, 1], I32))

        def half(v, w=T):
            return v.rearrange("p (a b) -> p a b", b=w)

        def placed(name, at, shape, dtype=F32):
            assert at + int(np.prod(shape)) <= WORDS, (name, at, shape)
            t = nc.alloc_sbuf_tensor_at(name, [P, *shape], dtype, offset=arena_at + 4 * at)
            return t[(slice(None),) * (1 + len(shape))]

        def rounded(name, at, *shape):
            return placed(name, at, shape, F32R)

        def carve(stage, at, *parts):
            tensors = {}
            for name, *shape in parts:
                tensors[name] = placed(f"{stage}_{name}", at, shape)
                at += int(np.prod(shape))
            return tensors, at

        A, FREE = carve("a", 0, ("gdn_qk", H, 2, T), ("gdn_v", H, T), ("kd", 2 * H, 2, P), ("k_in", 2 * H, P),
                        ("k_tail", 2 * H, P), ("eg", H, T))
        RING = FREE
        raw = carve("w", RING, ("raw", RAW, UNIT))[0]["raw"]
        w_low = rounded("w_low", RING, RAW, UNIT)
        w_high = rounded("w_high", RING + RAW * UNIT, HIGH, UNIT)
        RINGS_END = RING + (RAW + HIGH) * UNIT
        assert RINGS_END == 6 * SLOT, RINGS_END
        B, LATE = carve("all", RINGS_END, ("c1", NC1), ("sm", NSM), ("rb", 72), ("x", DC, T), ("h", DC, T), ("h_lo", DC, T),
                        ("sq", DC, T))
        c1, sm, rb, x, h, sq = (B[k] for k in ("c1", "sm", "rb", "x", "h", "sq"))
        H_AT = LATE - 3 * DC * T
        h_high, h_low = rounded("h_high", H_AT, DC, T), rounded("h_low", H_AT + DC * T, DC, T)
        AB, _ = carve("a", LATE, ("t", 2 * H, P), ("u", 2 * H, P), ("fox_q", H, T), ("fox_k", H, T), ("fox_v", TT, 512),
                      ("sb_q", H, T), ("sb_k", H, T), ("sb_v", TT, 512), ("gz", H, T), ("v_in", 2 * H, P),
                      ("state", H, P), ("s", 2, 384), ("pt", 2, 384), ("vnew", 512), ("rows", 6, T), ("rows_w", DC, 12),
                      ("tok", TT, 24), ("st", 32), ("tmp", 512))
        A.update(AB)
        A["h"] = carve("a", LATE, ("h", DC, T))[0]["h"]
        A["lm"], A["xx"] = (half(sq[:, 4 * i:4 * i + 4, :].rearrange("p a b -> p (a b)"), P) for i in range(2))
        A["gsb"] = half(sq[:, 4:8, :].rearrange("p a b -> p (a b)"), 512)
        A["tmp2"] = carve("a", LATE, ("tmp2", 4, 512))[0]["tmp2"]
        W4 = H * T
        ya = rounded("ya_high", LATE + 2 * W4, H, T), rounded("ya_low", LATE + 3 * W4, H, T)
        yc = rounded("yc_high", LATE + 5 * W4, H, T), rounded("yc_low", LATE + 6 * W4, H, T)
        yb = rounded("yb_high", LATE + 9 * W4, H, T), rounded("yb_low", LATE + 8 * W4, H, T)
        A["mixed"] = carve("a", 0, ("mixed", DC, T))[0]["mixed"]
        mixed = rounded("mixed_high", 3 * W4, DC, T), rounded("mixed_low", 5 * W4, DC, T)
        M, _ = carve("m", LATE, ("mem", DC, T), ("hm_hi", DC, T), ("hm_lo", DC, T), ("q", H, T), ("k", H, T), ("v", TT, 512),
                     ("s", 2, 512), ("pt", 2, 512), ("st", 32), ("sq", H, T))
        assert _ <= LATE + 14400
        hm = rounded("hm_high", LATE + 2 * W4, DC, T), rounded("hm_low", LATE + 4 * W4, DC, T)
        ym = rounded("ym_high", LATE + 6 * W4, H, T), rounded("ym_low", LATE + 7 * W4, H, T)
        F, _ = carve("f", LATE + DC * T, ("y", 3, 2, T), ("sa", 3, T), ("act", 2, T), ("act_hi", 4, T), ("act_lo", 4, T))
        assert _ <= LATE + 14400
        act_high, act_low = rounded("act_high", _ - 2 * W4, 4, T), rounded("act_low", _ - W4, 4, T)
        R, _ = carve("r", LATE, ("cat", DC, T), ("q", H, T), ("k", H, T), ("kraw", H, T), ("v", TT, 512), ("qraw", H, T),
                     ("g", H, T), ("gb", H, T), ("gc", H, T), ("pt", 2, 384))
        assert _ <= LATE + 14400
        R["c2"] = carve("r", 0, ("c2", NC2))[0]["c2"]
        cat = rounded("cat_high", LATE + 2 * W4, DC, T), rounded("cat_low", LATE + 4 * W4, DC, T)
        X, _ = carve("x", LATE, ("lg", TT, 72), ("one_g", TT, 8), ("el", TT, E), ("r", TT, 64),
                     ("gate", TT, E), ("member", TT, E), ("rank", TT, E), ("htok", TT, D), ("s", TT, GROUP * CAP),
                     ("sg", TT, GROUP * P), ("xt", DC, P), ("sil", P), ("act", P), ("actT", P), ("yb", T),
                     ("scat", T), ("zero", 512), ("count", 80), ("rs", T))
        X["router_w"] = carve("x", LATE + 14400, ("router_w", DC, 72))[0]["router_w"]

        def C(name, rows=P, lo=0, n=None, base=0):
            s = C1[name]
            n = s.stop - s.start if n is None else n
            return c1[base:base + rows, s.start + lo:s.start + lo + n]

        def S_(name, i=0, base=0, rows=P):
            c = SM[name].start + i
            return sm[base:base + rows, c:c + 1]

        ident = C("ident")

        class Banks:

            def __init__(self, name, banks):
                self.banks, self.name, self.units = banks, name, {}

            def fill(self, pe, unit):
                n = len(self.units)
                self.units[unit] = n
                b, use = n % len(self.banks), n // len(self.banks)
                if use:
                    pe.wait_ge(sem(f"{self.name}_empty{b}"), use)
                return psum[:, self.banks[b], :]

            def filled(self, ins, unit):
                ins.then_inc(sem(f"{self.name}_full{self.units[unit] % len(self.banks)}"), 1)

            def full(self, unit):
                n = self.units[unit]
                return sem(f"{self.name}_full{n % len(self.banks)}"), n // len(self.banks) + 1

            def wait(self, eng, unit):
                n = self.units[unit]
                eng.wait_ge(*self.full(unit))
                return psum[:, self.banks[n % len(self.banks)], :]

            def release(self, eng, unit):
                eng.sem_inc(sem(f"{self.name}_empty{self.units[unit] % len(self.banks)}"), 1)

            def emptied(self, ins, unit):
                ins.then_inc(sem(f"{self.name}_empty{self.units[unit] % len(self.banks)}"), 1)

        proj = Banks("proj", (0, 1, 2, 3))
        aux = Banks("aux", (4, 5, 6, 7))

        E_W, _ = carve("e", 0, *((f"{nm}{b}", *shape) for b in range(2)
                                 for nm, shape in (("gu", (DC, 2, 512)), ("dn", (4, D)))))
        expert_gu, expert_dn = ([E_W[f"{nm}{b}"] for b in range(2)] for nm in ("gu", "dn"))

        LAST = len(UNITS) - 1

        def place(name):
            return (ORDER[name] - LAST - 1) % RAW

        def loaded(name):
            n = place(name)
            return sem(f"unit_loaded{n}"), 16 * (1 + len([u for u in UNITS[:ORDER[name]] if place(u) == n]))

        def high(name):
            return w_high[:, ORDER[name] % HIGH, :]

        def low(name):
            return w_low[:, place(name), :]
        NORMS = ("mix", "mem", "xq", "ffn", "n1", "n2", "final")

        def quarter(name, q):
            return 4 * NORMS.index(name) + q + 1

        def chunks(name, k=DC - 1):
            return DC * NORMS.index(name) + k + 1
        done = {}
        block = ctx.enter_context(nc.Block())

        @block.tensor
        def _(pe):
            mm = nc.tensor.matmul

            def parts(name, kc):
                pe.wait_ge(sem("w_low"), ORDER[name] + 1)
                return [v.rearrange("p (k n) -> p k n", k=kc) for v in (high(name), low(name))]

            def product(ps, w, src, start, stop, **kw):
                mm(ps, w[0], src[0], start=start, stop=False, **kw)
                mm(ps, w[0], src[1], start=False, stop=False, **kw)
                return mm(ps, w[1], src[0], start=False, stop=stop, **kw)

            def chunk_of(pair, *at):
                return [v[(slice(None), *at)] for v in pair]
            HI = (h_high, h_low)

            def split_input(name):
                return "input_low", lambda q: quarter(name, q)

            def unit(name, src=HI, ready=None):
                w = parts(name, DC)
                ps = half(proj.fill(pe, name))
                for i in range(2):
                    for k in range(DC):
                        if ready and i == 0 and k % 2 == 0:
                            pe.wait_ge(sem(ready[0]), ready[1](k // 2))
                        last = product(ps[:, i, :], chunk_of(w, k, slice(i * P, (i + 1) * P)), chunk_of(src, k, slice(None)),
                                       k == 0, k == DC - 1)
                proj.filled(last, name)
                done[name] = proj.full(name)

            def unit_tok(name, src=HI):
                w = parts(name, DC)
                ps = half(proj.fill(pe, name))
                for t in range(TT):
                    for k in range(DC):
                        last = product(ps[:, t, :], chunk_of(src, k, slice(t * P, (t + 1) * P)), chunk_of(w, k, slice(None)),
                                       k == 0, k == DC - 1)
                proj.filled(last, name)
                done[name] = proj.full(name)

            def unit_o(tile, u, src):
                name = f"{tile}_{u // 2}"
                w = parts(name, H)
                ps = half(proj.fill(pe, f"{tile}{u}"))
                for i in range(2):
                    n = 2 * (u % 2) + i
                    for k in range(H):
                        last = product(ps[:, i, :], chunk_of(w, k, slice(n * P, (n + 1) * P)), chunk_of(src, k, slice(None)),
                                       k == 0, k == H - 1)
                proj.filled(last, f"{tile}{u}")
                done[name] = proj.full(f"{tile}{u}")

            def mean_square(name):
                ps = aux.fill(pe, f"ms_{name}")
                for k in range(DC):
                    pe.wait_ge(sem("squares"), quarter(name, k // 2))
                    last = mm(ps[:, 0:T], C("inv1024"), sq[:, k, :], start=(k == 0), stop=(k == DC - 1))
                aux.filled(last, f"ms_{name}")

            def head_sums(name, ready, src, width, weights="inv128"):
                for hd in range(H):
                    ps = aux.fill(pe, f"{name}{hd}")
                    pe.wait_ge(sem(ready), hd + 1)
                    aux.filled(mm(ps[:, 0:width], C(weights, n=P), src(hd), start=True, stop=True), f"{name}{hd}")

            pe.wait_ge(sem("consts_loaded"), 32)
            mean_square("mix")
            unit("gq0", HI, split_input("mix")); unit("gq1")
            unit("gk0"); unit("gk1")
            unit("gv0"); unit("gv1")
            pe.wait_ge(sem("rows_w_loaded"), 16)
            ps = aux.fill(pe, "rows")
            for k in range(DC):
                for j in range(3):
                    last = mm(ps[32 * j:32 * j + H, 0:T], A["rows_w"][:, k, j * H:(j + 1) * H], A["h"][:, k, :],
                              start=(k == 0), stop=(k == DC - 1), skip_group_check=True)
            aux.filled(last, "rows")
            unit("gz0"); unit("gz1")
            unit("fq0"); unit("fq1")
            head_sums("gss", "gdn_sq", lambda hd: sq[:, 2 * hd:2 * hd + 2, :].rearrange("p a b -> p (a b)"), 512, "ones")
            unit("fk0"); unit("fk1")
            pe.wait_ge(sem("late_consts_loaded"), 16)
            pe.wait_ge(sem("gdn_rows"), 1)
            for unit_name, rows_of in (("tok", ((0, 64), (1, 64))), ("tok_beta", ((2, 32),))):
                ps = aux.fill(pe, unit_name)
                for t in range(TT):
                    for j, (row, base) in enumerate(rows_of):
                        o = (len(rows_of) * t + j) * H
                        last = mm(ps[:, o:o + H], A["rows"][base:base + H, row, t * P:(t + 1) * P],
                                  ident[base:base + H, base:base + H], start=True, stop=True)
                aux.filled(last, unit_name)
            for q in range(2):
                ps = half(aux.fill(pe, f"decay{q}"))
                for i in range(2):
                    hd = 2 * q + i
                    last = mm(ps[:, i, :], C("sel", H, hd * 256, P, 64), A["rows"][64:64 + H, 0, :], start=True, stop=True)
                aux.filled(last, f"decay{q}")
            unit_tok("fv0"); unit_tok("fv1")
            head_sums("fss_q", "fox_sq_q", lambda hd: sq[:, hd, :], T)
            head_sums("fss_k", "fox_sq_k", lambda hd: sq[:, H + hd, :], T)
            unit("sq0"); unit("sq1")
            for t in range(TT):
                for nm, src, ready in (("k", lambda hd: A["gdn_qk"][:, hd, 1, t * P:(t + 1) * P], "gdn_k"),
                                       ("v", lambda hd: A["gdn_v"][:, hd, t * P:(t + 1) * P], "gdn_v")):
                    pe.wait_ge(sem(ready), H)
                    ps = aux.fill(pe, f"turn_{nm}{t}")
                    for hd in range(H):
                        last = nc.tensor.transpose(ps[:, hd * P:(hd + 1) * P], src(hd), ident)
                    aux.filled(last, f"turn_{nm}{t}")
            unit("sk0"); unit("sk1")
            for t in range(TT):
                for q in range(2):
                    ps = half(aux.fill(pe, f"kk{t}{q}"))
                    for i in range(2):
                        hd = 2 * q + i
                        tk = A["gdn_qk"][:, hd, :, t * P:(t + 1) * P]
                        last = mm(ps[:, i, :], tk[:, 1, :], tk, start=True, stop=True)
                    aux.filled(last, f"kk{t}{q}")
            unit_tok("sv0"); unit_tok("sv1")

            def fox_scores(hd):
                ps = aux.fill(pe, f"fs{hd}")
                if hd == 0:
                    pe.wait_ge(sem("fox_c"), 1)
                pe.wait_ge(sem("fox_qn"), hd + 1)
                pe.wait_ge(sem("fox_kn"), hd + 1)
                cs = A["rows"][0:H, 3, :]
                for t, (lo, n) in enumerate(((0, P), (P, T))):
                    o = ps[:, lo:lo + n]
                    mm(o, A["fox_q"][:, hd, t * P:(t + 1) * P], A["fox_k"][:, hd, 0:n], start=True, stop=False)
                    mm(o, C("negsel", H, hd * P, P), cs[:, 0:n], start=False, stop=False)
                    last = mm(o, cs[:, t * P:(t + 1) * P], C("sel", H, hd * 256, n), start=False, stop=True)
                aux.filled(last, f"fs{hd}")

            def fox_turn(hd):
                ps = aux.fill(pe, f"fpt{hd}")
                pe.wait_ge(sem("fox_p"), hd + 1)
                for j in range(3):
                    last = nc.tensor.transpose(ps[:, j * P:(j + 1) * P],
                                               A["s"][:, hd % 2, (0, 128, 256)[j]:(0, 128, 256)[j] + P], ident)
                aux.filled(last, f"fpt{hd}")

            def pv(name, hd, ready, pt, v):
                ps = aux.fill(pe, f"{name}{hd}")
                pe.wait_ge(sem(ready), hd + 1)
                mm(ps[:, 0:T], v[:, 0, hd * P:(hd + 1) * P], pt[:, hd % 2, 0:T], start=True, stop=False,
                   skip_group_check=True)
                aux.filled(mm(ps[:, P:T], v[:, 1, hd * P:(hd + 1) * P], pt[:, hd % 2, T:384], start=False, stop=True,
                              skip_group_check=True), f"{name}{hd}")

            def sb_scores(hd):
                ps = aux.fill(pe, f"sz{hd}")
                if hd == 0:
                    pe.wait_ge(sem("sb_q"), 2)
                    pe.wait_ge(sem("sb_k"), 2)
                    pe.wait_ge(sem("sb_v"), 2)
                q, k = A["sb_q"][:, hd, :], A["sb_k"][:, hd, :]
                mm(ps[:, 0:T], k[:, 0:P], q, start=True, stop=False, skip_group_check=True)
                aux.filled(mm(ps[:, T:384], k[:, P:T], q[:, P:T], start=False, stop=False, skip_group_check=True),
                           f"sz{hd}")

            def sb_sums(hd):
                n = aux.units[f"sz{hd}"]
                ps = psum[:, 4 + n % 4, :]
                lk = A["s"][:, hd % 2, :]
                pe.wait_ge(sem("sb_lk"), hd + 1)
                mm(ps[:, 0:T], C("tri"), lk[:, 0:T], start=False, stop=False, skip_group_check=True)
                mm(ps[:, P:T], C("ones", n=P), lk[:, T:384], start=False, stop=False, skip_group_check=True)
                mm(ps[:, T:384], C("tri"), lk[:, T:384], start=False, stop=True,
                   skip_group_check=True).then_inc(sem("sb_sum"), 1)

            def solve_x(lv, t):
                ps = aux.fill(pe, f"x{lv}{t}")
                pe.wait_ge(sem("gdn_lm"), lv + 1)
                if lv:
                    pe.wait_ge(sem("gdn_t"), 2 * (lv - 1) + t + 1)
                for hd in range(H):
                    un = t * H + hd
                    last = mm(ps[:, hd * P:(hd + 1) * P], A["lm"][:, un, :], ident if lv == 0 else A["t"][:, un, :],
                              start=True, stop=True)
                aux.filled(last, f"x{lv}{t}")

            def solve_tu(lv, t):
                pe.wait_ge(sem("gdn_xx"), 2 * lv + t + 1)
                if lv:
                    pe.wait_ge(sem("gdn_u"), 2 * (lv - 1) + t + 1)
                for nm in ("t", "u"):
                    if nm == "t" and lv == len(LEVELS) - 1:
                        continue
                    ps = aux.fill(pe, f"{nm}{lv}{t}")
                    for hd in range(H):
                        un = t * H + hd
                        u = ident if lv == 0 else A["u"][:, un, :]
                        xx = A["xx"][:, un, :]
                        last = mm(ps[:, hd * P:(hd + 1) * P], u if nm == "t" else xx, xx if nm == "t" else u,
                                  start=True, stop=True)
                    aux.filled(last, f"{nm}{lv}{t}")

            def solve_uw(t):
                pe.wait_ge(sem("gdn_u"), 2 * (len(LEVELS) - 1) + t + 1)
                ps = aux.fill(pe, f"sol_u{t}")
                for hd in range(H):
                    un = t * H + hd
                    last = mm(ps[:, hd * P:(hd + 1) * P], A["u"][:, un, :], A["v_in"][:, un, :], start=True, stop=True)
                aux.filled(last, f"sol_u{t}")
                ps = aux.fill(pe, f"sol_w{t}")
                for hd in range(H):
                    un = t * H + hd
                    last = mm(ps[:, hd * P:(hd + 1) * P], A["k_in"][:, un, :], A["u"][:, un, :], start=True, stop=True)
                aux.filled(last, f"sol_w{t}")

            def state_v(n):
                t, po = n // 2, CHUNK * (n % 2)
                ps = aux.fill(pe, f"wS{n}")
                pe.wait_ge(sem("gdn_state"), n)
                for hd in range(H):
                    last = mm(ps[po:po + CHUNK, hd * P:(hd + 1) * P], A["k_in"][:, t * H + hd, po:po + CHUNK],
                              A["state"][:, hd, :], start=True, stop=True)
                aux.filled(last, f"wS{n}")

            def state_o(n):
                t, po = n // 2, CHUNK * (n % 2)
                ps = aux.fill(pe, f"o{n}")
                pe.wait_ge(sem("gdn_vnew"), n + 1)
                for hd in range(H):
                    un = t * H + hd
                    vn = A["vnew"][po:po + CHUNK, hd * P:(hd + 1) * P]
                    if n:
                        mm(ps[:, hd * CHUNK:(hd + 1) * CHUNK], A["state"][:, hd, :],
                           A["gdn_qk"][:, hd, 0, n * CHUNK:(n + 1) * CHUNK], start=True, stop=False)
                    last = mm(ps[:, hd * CHUNK:(hd + 1) * CHUNK], vn,
                              A["kd"][po:po + CHUNK, un, 0, po:po + CHUNK], start=(n == 0), stop=True)
                aux.filled(last, f"o{n}")
                if n == T // CHUNK - 1:
                    return
                ps = aux.fill(pe, f"dS{n}")
                for hd in range(H):
                    un = t * H + hd
                    last = mm(ps[:, hd * P:(hd + 1) * P], A["k_tail"][po:po + CHUNK, un, :],
                              A["vnew"][po:po + CHUNK, hd * P:(hd + 1) * P], start=True, stop=True)
                aux.filled(last, f"dS{n}")

            fill_in = iter([lambda: fox_scores(0), lambda: fox_scores(1),
                            lambda: fox_turn(0), lambda: (fox_turn(1), pv("fpv", 0, "fox_pT", A["pt"], A["fox_v"])),
                            lambda: (pv("fpv", 1, "fox_pT", A["pt"], A["fox_v"]), fox_scores(2)),
                            lambda: fox_scores(3), lambda: fox_turn(2),
                            lambda: (fox_turn(3), pv("fpv", 2, "fox_pT", A["pt"], A["fox_v"])),
                            lambda: pv("fpv", 3, "fox_pT", A["pt"], A["fox_v"])])

            def between():
                f = next(fill_in, None)
                if f:
                    f()
            for lv in range(len(LEVELS)):
                solve_x(lv, 0)
                solve_x(lv, 1)
                between()
                solve_tu(lv, 0)
                solve_tu(lv, 1)
                between()
            solve_uw(0)
            solve_uw(1)

            def gate(b, hf, p):
                unit(f"g{b}{hf}{p}")

            def o_unit(b, hf, p, src, ready):
                u = 2 * hf + p
                if u == 0:
                    pe.wait_ge(sem(ready), H)
                unit_o(f"o{b}", u, src)

            def branch(b, src, ready, steps):
                steps = iter(steps)

                def step():
                    f = next(steps, None)
                    if f:
                        f()
                for hf in range(2):
                    for p in range(2):
                        gate(b, hf, p)
                        step()
                    for p in range(2):
                        o_unit(b, hf, p, src, ready)
                        step()

            branch("a", ya, "ya", [
                lambda: (state_o(0), sb_scores(0)), lambda: sb_scores(1), lambda: state_v(1), lambda: sb_sums(0),
                lambda: (sb_sums(1), state_o(1)), lambda: pv("spv", 0, "sb_a", A["pt"], A["sb_v"]),
                lambda: (pv("spv", 1, "sb_a", A["pt"], A["sb_v"]), state_v(2)), lambda: sb_scores(2)])
            sb_scores(3)
            state_o(2)
            sb_sums(2)
            sb_sums(3)
            pv("spv", 2, "sb_a", A["pt"], A["sb_v"])
            pv("spv", 3, "sb_a", A["pt"], A["sb_v"])
            branch("c", yc, "yc", [
                lambda: state_v(3), lambda: None, lambda: state_o(3), lambda: None,
                lambda: head_sums("oss", "gdn_osq", lambda hd: sq[:, hd, :], T)])
            branch("b", yb, "yb", [])
            unit("out00", mixed, ("mixed", lambda q: q + 1)); unit("out01", mixed)

            mean_square("mem")
            unit("out10", mixed); unit("out11", mixed)
            unit("mk0", hm, split_input("mem")); unit("mk1", hm)
            mean_square("xq")
            unit_tok("mv0", hm); unit_tok("mv1", hm)
            head_sums("mss_k", "mem_sq_k", lambda hd: M["sq"][:, hd, :], T)
            unit("mq0", HI, split_input("xq")); unit("mq1")
            head_sums("mss_q", "mem_sq_q", lambda hd: M["sq"][:, hd, :], T)

            def mem_scores(hd):
                ps = half(aux.fill(pe, f"mS{hd}"))
                pe.wait_ge(sem("mem_qk"), H + hd + 1)
                for t in range(TT):
                    last = mm(ps[:, t, :], M["q"][:, hd, t * P:(t + 1) * P], M["k"][:, hd, :], start=True, stop=True)
                aux.filled(last, f"mS{hd}")

            def mem_turn(hd):
                ps = aux.fill(pe, f"mpt{hd}")
                pe.wait_ge(sem("mem_p"), hd + 1)
                for kb in range(2):
                    for t in range(TT):
                        last = nc.tensor.transpose(ps[:, kb * T + t * P:kb * T + (t + 1) * P],
                                                   M["s"][:, hd % 2, t * T + kb * P:t * T + (kb + 1) * P], ident)
                aux.filled(last, f"mpt{hd}")

            def mem_pv(hd):
                ps = aux.fill(pe, f"mpv{hd}")
                pe.wait_ge(sem("mem_pT"), hd + 1)
                for kb in range(2):
                    last = mm(ps[:, 0:T], M["v"][:, kb, hd * P:(hd + 1) * P], M["pt"][:, hd % 2, kb * T:(kb + 1) * T],
                              start=(kb == 0), stop=(kb == 1))
                aux.filled(last, f"mpv{hd}")
            mem_scores(0)
            mem_scores(1)
            for hd in range(H):
                mem_turn(hd)
                mem_pv(hd)
                if hd + 2 < H:
                    mem_scores(hd + 2)
            pe.wait_ge(sem("ym"), H)
            for u in range(4):
                unit_o("mo", u, ym)

            mean_square("ffn")

            def up(c):
                name = f"U{c}"
                w = parts(name, DC)
                ps = half(proj.fill(pe, f"up{c}"))
                for g in range(2):
                    for k in range(DC):
                        if c == 0 and g == 0 and k % 2 == 0:
                            pe.wait_ge(sem("input_low"), quarter("ffn", k // 2))
                        last = product(ps[:, g, :], chunk_of(w, k, slice(g * P, (g + 1) * P)), chunk_of(HI, k, slice(None)),
                                       k == 0, k == DC - 1)
                proj.filled(last, f"up{c}")
                done[name] = proj.full(f"up{c}")

            down_ps = [half(aux.fill(pe, f"down{b}")) for b in range(4)]

            def down(c):
                w = parts(f"D{c // 2}", 2)
                pe.wait_ge(sem("ffn_act"), c + 1)
                for n in range(DC):
                    last = product(down_ps[n // 2][:, n % 2, :], chunk_of(w, c % 2, slice(n * P, (n + 1) * P)),
                                   chunk_of((act_high, act_low), c % 4, slice(None)),
                                   c == 0 and n % 2 == 0, c == FC - 1, skip_group_check=True)
                    if c == FC - 1 and n % 2:
                        aux.filled(last, f"down{n // 2}")
                if c < FC - 1:
                    last.then_inc(sem("ffn_act_used"), 1)
                done[f"D{c // 2}"] = (sem("ffn_act_used"), c + 1) if c < FC - 1 else aux.full("down3")
            up(0)
            up(1)
            for c in range(0, FC, 2):
                if c + 2 < FC:
                    up(c + 2)
                    up(c + 3)
                down(c)
                down(c + 1)

            mean_square("n1")
            pe.wait_ge(sem("c2_loaded"), 16)
            rot = R["c2"][:, C2["rot"]]

            def rotate(nm):
                for q in range(2):
                    ps = half(aux.fill(pe, f"rot_{nm}{q}"))
                    pe.wait_ge(sem(f"raw_{nm}"), q + 1)
                    for i in range(2):
                        last = mm(ps[:, i, :], rot, R[f"{nm}raw"][:, 2 * q + i, :], start=True, stop=True)
                    aux.filled(last, f"rot_{nm}{q}")
            unit("q20", HI, split_input("n1")); unit("q21")
            unit("k20"); rotate("q"); unit("k21")
            unit_tok("v20"); rotate("k"); unit_tok("v21")
            unit("g20"); unit("g21")

            def ret_scores(hd):
                ps = aux.fill(pe, f"rs{hd}")
                pe.wait_ge(sem("ret_q"), hd // 2 + 1)
                pe.wait_ge(sem("ret_k"), hd // 2 + 1)
                q, k = R["q"][:, hd, :], R["k"][:, hd, :]
                mm(ps[:, 0:T], k[:, 0:P], q, start=True, stop=True)
                aux.filled(mm(ps[:, T:384], k[:, P:T], q[:, P:T], start=True, stop=True), f"rs{hd}")
            ret_scores(0); ret_scores(1)
            unit("gc20")
            pe.wait_ge(sem("ret_v"), 2)
            pv("ro", 0, "ret_p", R["pt"], R["v"]); pv("ro", 1, "ret_p", R["pt"], R["v"])
            unit("gc21")
            ret_scores(2); ret_scores(3)
            unit("u20")
            pv("ro", 2, "ret_p", R["pt"], R["v"]); pv("ro", 3, "ret_p", R["pt"], R["v"])
            unit("u21")
            head_sums("rm", "ret_o", lambda hd: R["qraw"][:, hd, :], T)
            unit("gb20")
            head_sums("rv", "ret_d2", lambda hd: sq[:, hd, :], T)
            unit("gb21")
            pe.wait_ge(sem("cat"), 2 * H)
            for nm in ("o200", "o201", "o210", "o211"):
                unit(nm, cat)

            mean_square("n2")
            pe.wait_ge(sem("router_w_loaded"), 16)
            pe.wait_ge(sem("rb_loaded"), 16)
            ps = aux.fill(pe, "router")
            for t in range(TT):
                o = ps[:, t * 72:(t + 1) * 72]
                for k in range(DC):
                    pe.wait_ge(sem("normed"), chunks("n2", k))
                    mm(o, h[:, k, t * P:(t + 1) * P], X["router_w"][:, k, :], start=(k == 0), stop=False)
                last = mm(o, C("ones", 1, 0, P), rb[0:1, :], start=False, stop=True)
            aux.filled(last, "router")
            for t in range(TT):
                for hf in range(2):
                    ps = proj.fill(pe, f"htok{t}{hf}")
                    for i in range(4):
                        last = nc.tensor.transpose(ps[:, i * P:(i + 1) * P], h[:, 4 * hf + i, t * P:(t + 1) * P], ident)
                    proj.filled(last, f"htok{t}{hf}")
            pe.wait_ge(sem("member"), 1)
            ps = aux.fill(pe, "rank")
            mm(ps[:, 0:E], C("before"), X["member"][:, 0, :], start=True, stop=True)
            mm(ps[:, E:2 * E], C("ones", n=P), X["member"][:, 0, :], start=True, stop=False)
            mm(ps[:, E:2 * E], C("before"), X["member"][:, 1, :], start=False, stop=True)
            mm(ps[:, 2 * E:3 * E], C("ones", n=P), X["member"][:, 0, :], start=True, stop=False)
            aux.filled(mm(ps[:, 2 * E:3 * E], C("ones", n=P), X["member"][:, 1, :], start=False, stop=True), "rank")

            pe.wait_ge(sem("htok"), 4)
            pe.wait_ge(sem("zeroed"), 1)
            for b in range(4):
                mm(psum[:, b, :], ident, X["zero"], start=True, stop=False, skip_group_check=True)
            pe.wait_ge(sem("ranked"), 1)
            pe.wait_ge(sem("n_iter"), 1)
            n_iter = pe.value_load(n_iter_i[0:1, 0:1], min_val=NG, max_val=NG * MAXPASS)
            with pe.Fori(0, n_iter) as i:
                pe.wait_ge(sem("places"), i + 1)
                for c in range(DC):
                    for t in range(TT):
                        last = mm(psum[:, 4 + c // 4, (c % 4) * P:(c % 4 + 1) * P], X["htok"][:, t, c * P:(c + 1) * P],
                                  X["s"][:, t, :], start=(t == 0), stop=(t == TT - 1))
                    if c == 3:
                        last.then_inc(sem("xt_lo"), 1)
                last.then_inc(sem("xt_hi"), 1)
                for j in range(GROUP):
                    q = i * GROUP + (j + 1)
                    b = j % 2
                    if j == 0:
                        pe.wait_ge(sem("xt_lo_kept"), i + 1)
                        pe.wait_ge(sem("xt_hi_kept"), i + 1)
                    pe.wait_ge(sem(f"gu_loaded{b}"), i * 32 + 16 * (j // 2 + 1))
                    for k in range(DC):
                        for s in range(4):
                            last = mm(half(psum[32 * s:32 * s + 32, 6, 0:256], P), X["xt"][:, k, CAP * j:CAP * (j + 1)],
                                      expert_gu[b][:, k, :, s * P:(s + 1) * P], start=(k == 0), stop=(k == DC - 1))
                    last.then_inc(sem("gate_up"), 1)
                    for t in range(TT):
                        last = nc.tensor.transpose(psum[:, 7, 256 + t * P:256 + (t + 1) * P],
                                                   X["sg"][:, t, j * P:(j + 1) * P], ident)
                    last.then_inc(sem("scatter"), 1)
                    pe.wait_ge(sem("e_act"), q)
                    nc.tensor.transpose(psum[:, 6, 256:384], X["act"], ident).then_inc(sem("e_turned"), 1)
                    pe.wait_ge(sem("e_actT"), q)
                    pe.wait_ge(sem("scatter_kept"), q)
                    pe.wait_ge(sem(f"dn_loaded{b}"), i * 32 + 16 * (j // 2 + 1))
                    for c in range(4):
                        for s in range(4):
                            last = mm(psum[32 * s:32 * s + 32, 7, 0:256], X["actT"][:, CAP * c:CAP * (c + 1)],
                                      expert_dn[b][:, c, s * T:(s + 1) * T], start=(c == 0), stop=(c == 3))
                    last.then_inc(sem("down"), 1)
                    pe.wait_ge(sem("e_y"), q)
                    for d in range(2):
                        for s in range(4):
                            last = mm(psum[:, s, d * T:(d + 1) * T], X["yb"][32 * s:32 * s + 32, d * P:(d + 1) * P],
                                      X["scat"][32 * s:32 * s + 32, :], start=False, stop=False, skip_group_check=True)
            for b in range(4):
                last = mm(psum[:, b, :], ident, X["zero"], start=False, stop=True, skip_group_check=True)
            last.then_inc(sem("moe_done"), 1)
            ps = psum[:, 4, :]
            for k in range(DC):
                pe.wait_ge(sem("squares"), quarter("final", k // 2))
                last = mm(ps[:, 0:T], C("inv1024"), sq[:, k, :], start=(k == 0), stop=(k == DC - 1))
            last.then_inc(sem("ms_final"), 1)

        @block.scalar
        def _(act):
            chain = [0]
            ac = nc.scalar.activation

            def link(ins):
                chain[0] += 1
                ins.then_inc(sem("act_chain"), 1)
                act.wait_ge(sem("act_chain"), chain[0])

            def root(unit, out, n=T):
                ps = aux.wait(act, unit)[:, 0:n]
                ps = ps if n == T else half(ps)
                link(ac(out, ps, ACT.Sqrt, bias=C("eps")))
                aux.release(act, unit)
                act.sem_inc(sem("root_ready"), 1)

            def squares(name, src, ready, counts=(1, 2, 3, 4)):
                for q in range(DC // 2):
                    act.wait_ge(sem(ready), counts[q])
                    ac(sq[:, 2 * q:2 * q + 2, :], src[:, 2 * q:2 * q + 2, :], ACT.Square).then_inc(sem("squares"), 1)

            def high_parts(name, src, dst):
                for q in range(DC // 2):
                    act.wait_ge(sem("normed"), chunks(name, 2 * q + 1))
                    ac(dst[:, 2 * q:2 * q + 2, :], src[:, 2 * q:2 * q + 2, :], ACT.Copy).then_inc(sem("input_high"), 1)
            w_next = [0]

            def ahead(name, n=HIGH):
                while w_next[0] <= min(ORDER[name] + n, LAST):
                    w = UNITS[w_next[0]]
                    act.wait_ge(*loaded(w))
                    if w_next[0] >= HIGH:
                        act.wait_ge(*done[UNITS[w_next[0] - HIGH]])
                    ac(high(w), raw[:, place(w), :], ACT.Copy).then_inc(sem("w_high"), 1)
                    w_next[0] += 1

            act.wait_ge(sem("consts_loaded"), 32)
            squares("mix", x, "x_loaded", (16,) * 4)
            ahead(UNITS[0], 0)
            root("ms_mix", sq[:, 0, :])
            ahead(UNITS[0], 1)
            high_parts("mix", A["h"], h_high)
            ahead(UNITS[0], 2)
            cv = lambda ch, tap: S_("gdn_conv", 4 * ch + tap)

            def conv_dst(ch):
                return A["gdn_qk"][:, ch % H, ch // H, :] if ch < 2 * H else A["gdn_v"][:, ch % H, :]
            for nm, first in (("gq", 0), ("gk", H), ("gv", 2 * H)):
                for u in range(2):
                    ps = half(proj.wait(act, f"{nm}{u}"))
                    for i in range(2):
                        ch = first + 2 * u + i
                        last = ac(conv_dst(ch), ps[:, i, :], ACT.Copy, scale=cv(ch, 3))
                    last.then_inc(sem("gdn_tap"), 1)
                    ahead(f"{nm}{u}")
            ps = aux.wait(act, "rows")
            rw = A["rows"]
            ac(rw[0:H, 4, :], ps[0:H, 0:T], ACT.Abs, bias=S_("rows", 0, 0, H))
            ac(rw[64:64 + H, 4, :], ps[64:64 + H, 0:T], ACT.Abs, bias=S_("rows", 2, 64, H))
            link(ac(rw[32:32 + H, 2, :], ps[32:32 + H, 0:T], ACT.Sigmoid))
            ac(rw[0:H, 4, :], rw[0:H, 4, :], ACT.Exp, scale=-1.0)
            ac(A["st"][64:64 + H, 30:31], S_("rows", 1, 64, H), ACT.Exp)
            link(ac(rw[64:64 + H, 4, :], rw[64:64 + H, 4, :], ACT.Exp, scale=-1.0))
            ac(rw[0:H, 5, :], rw[0:H, 4, :], ACT.Ln, bias=1.0)
            ac(rw[64:64 + H, 5, :], rw[64:64 + H, 4, :], ACT.Ln, bias=1.0).then_inc(sem("rows_ln"), 1)
            for ch in range(3 * H):
                act.wait_ge(sem("gdn_conv"), ch + 1)
                ins = ac(conv_dst(ch), conv_dst(ch), ACT.Silu)
                ins.then_inc(sem("gdn_silu" if ch < 2 * H else "gdn_v"), 1)
            for hd in range(H):
                act.wait_ge(sem("gdn_silu"), H + hd + 1)
                if hd == 0:
                    act.wait_ge(sem("normed"), chunks("mix"))
                ac(sq[:, 2 * hd:2 * hd + 2, :], A["gdn_qk"][:, hd, :, :], ACT.Square).then_inc(sem("gdn_sq"), 1)
            for u in range(2):
                ps = proj.wait(act, f"gz{u}")
                proj.emptied(ac(A["gz"][:, 2 * u:2 * u + 2, :], half(ps), ACT.Silu), f"gz{u}")
                ahead(f"gz{u}")

            for hd in range(H):
                root(f"gss{hd}", sq[:, 2 * hd:2 * hd + 2, :], 512)
            act.wait_ge(sem("gdn_tail"), 1)
            ac(rw[64:64 + H, 1, :], rw[64:64 + H, 1, :], ACT.Exp).then_inc(sem("gdn_rows"), 1)
            for u in range(2):
                ps = proj.wait(act, f"fq{u}")
                proj.emptied(ac(A["fox_q"][:, 2 * u:2 * u + 2, :], half(ps), ACT.Copy), f"fq{u}")
                ahead(f"fq{u}")
            act.wait_ge(sem("gdn_cols"), 1)
            ac(A["tok"][:, :, 12:16], A["tok"][:, :, 0:4], ACT.Exp).then_inc(sem("gdn_egc"), 1)
            for q in range(2):
                ps = aux.wait(act, f"decay{q}")
                ac(A["eg"][:, 2 * q:2 * q + 2, :], half(ps), ACT.Exp).then_inc(sem("gdn_eg"), 1)
            for un in range(2 * H):
                act.wait_ge(sem("gdn_expo"), un + 1)
                ac(A["t"][:, un, :], A["t"][:, un, :], ACT.Exp).then_inc(sem("gdn_dt"), 1)
            for u in range(2):
                ps = proj.wait(act, f"fk{u}")
                link(ac(A["fox_k"][:, 2 * u:2 * u + 2, :], half(ps), ACT.Copy))
                proj.release(act, f"fk{u}")
                ahead(f"fk{u}")
            act.wait_ge(sem("gdn_k"), H)
            for hd in range(H):
                ac(sq[:, hd, :], A["fox_q"][:, hd, :], ACT.Square).then_inc(sem("fox_sq_q"), 1)
            for hd in range(H):
                ac(sq[:, H + hd, :], A["fox_k"][:, hd, :], ACT.Square).then_inc(sem("fox_sq_k"), 1)
            for j, nm in enumerate("qk"):
                for hd in range(H):
                    root(f"fss_{nm}{hd}", sq[:, j * H + hd, :])
            for u in range(2):
                ps = half(proj.wait(act, f"fv{u}"))
                proj.emptied(ac(A["fox_v"][:, :, u * 256:(u + 1) * 256], ps, ACT.Copy), f"fv{u}")
                ahead(f"fv{u}")
            for u in range(2):
                ps = proj.wait(act, f"sq{u}")
                link(ac(A["sb_q"][:, 2 * u:2 * u + 2, :], half(ps), ACT.Copy, scale=SCALE))
                proj.release(act, f"sq{u}")
                ahead(f"sq{u}")
                act.sem_inc(sem("sb_q"), 1)
            act.wait_ge(sem("gdn_beg"), 1)
            for t in range(TT):
                ps = aux.wait(act, f"turn_k{t}")
                for hd in range(H):
                    un = t * H + hd
                    ac(A["k_in"][:, un, :], ps[:, hd * P:(hd + 1) * P], ACT.Copy, scale=A["tok"][:, t, 16 + hd:17 + hd])
                    last = ac(A["k_tail"][:, un, :], ps[:, hd * P:(hd + 1) * P], ACT.Copy,
                              scale=A["tok"][:, t, 4 + hd:5 + hd])
                aux.emptied(last, f"turn_k{t}")
                ps = aux.wait(act, f"turn_v{t}")
                for hd in range(H):
                    un = t * H + hd
                    last = ac(A["v_in"][:, un, :], ps[:, hd * P:(hd + 1) * P], ACT.Copy,
                              scale=A["tok"][:, t, 8 + hd:9 + hd])
                aux.emptied(last, f"turn_v{t}")
            for u in range(2):
                ps = proj.wait(act, f"sk{u}")
                link(ac(A["sb_k"][:, 2 * u:2 * u + 2, :], half(ps), ACT.Copy))
                proj.release(act, f"sk{u}")
                ahead(f"sk{u}")
                act.sem_inc(sem("sb_k"), 1)
            for u in range(2):
                ps = half(proj.wait(act, f"sv{u}"))
                link(ac(A["sb_v"][:, :, u * 256:(u + 1) * 256], ps, ACT.Copy))
                proj.release(act, f"sv{u}")
                ahead(f"sv{u}")
                act.sem_inc(sem("sb_v"), 1)

            def solve_evac(lv, t):
                ps = aux.wait(act, f"x{lv}{t}")
                for hd in range(H):
                    un = t * H + hd
                    last = ac(A["xx"][:, un, :], ps[:, hd * P:(hd + 1) * P], ACT.Copy,
                              scale=A["tok"][:, t, 8 + hd:9 + hd])
                link(last)
                aux.release(act, f"x{lv}{t}")
                act.sem_inc(sem("gdn_xx"), 1)

            def softmax_exp(buf, st, pre, hd, spans):
                act.wait_ge(sem(f"{pre}_max"), hd + 1)
                for t, (lo, n) in enumerate(spans):
                    last = ac(buf[:, hd % 2, lo:lo + n], buf[:, hd % 2, lo:lo + n], ACT.Exp,
                              bias=st[:, 8 * (hd % 2) + 2 + t:8 * (hd % 2) + 3 + t],
                              accum_out=st[:, 8 * (hd % 2) + 4 + t:8 * (hd % 2) + 5 + t])
                last.then_inc(sem(f"{pre}_exp"), 1)
            FSP = ((0, P), (P, T))

            def turned(name, hd, buf, n, done):
                ps = aux.wait(act, f"{name}{hd}")
                link(ac(buf[:, hd % 2, 0:n], ps[:, 0:n], ACT.Copy))
                aux.release(act, f"{name}{hd}")
                act.sem_inc(sem(done), 1)

            steps = iter([lambda: softmax_exp(A["s"], A["st"], "fox", 0, FSP),
                          lambda: softmax_exp(A["s"], A["st"], "fox", 1, FSP),
                          lambda: turned("fpt", 0, A["pt"], 384, "fox_pT"),
                          lambda: turned("fpt", 1, A["pt"], 384, "fox_pT"),
                          lambda: softmax_exp(A["s"], A["st"], "fox", 2, FSP),
                          lambda: softmax_exp(A["s"], A["st"], "fox", 3, FSP),
                          lambda: turned("fpt", 2, A["pt"], 384, "fox_pT"),
                          lambda: turned("fpt", 3, A["pt"], 384, "fox_pT")])

            def between():
                f = next(steps, None)
                if f:
                    f()
            for lv in range(len(LEVELS)):
                solve_evac(lv, 0)
                solve_evac(lv, 1)
                between()
                between()
            for t in range(TT):
                ps = aux.wait(act, f"sol_w{t}")
                last = ac(A["k_in"][:, t * H:(t + 1) * H, :], half(ps, P), ACT.Copy, scale=-1.0)
                link(last)
                aux.release(act, f"sol_w{t}")
                act.sem_inc(sem("gdn_w"), 1)

            def sb_log(hd):
                ps = aux.wait(act, f"sz{hd}")
                if hd >= 2:
                    act.wait_ge(sem("yc"), hd - 1)
                w = A["pt"][:, hd % 2, :]
                if hd == 0:
                    act.wait_ge(sem("ya"), H)
                link(ac(w, ps[:, 0:384], ACT.Abs))
                link(ac(w, w, ACT.Exp, scale=-1.0))
                ac(w, w, ACT.Ln, bias=1.0).then_inc(sem("sb_ln"), 1)

            def sb_exp(hd):
                act.wait_ge(sem("sb_s"), hd + 1)
                ac(A["pt"][:, hd % 2, :], A["s"][:, hd % 2, :], ACT.Exp).then_inc(sem("sb_a"), 1)
            ng = [0]

            def gates(b, hf, p):
                if hf and not p:
                    ahead(f"o{b}_0")
                ps = half(proj.wait(act, f"g{b}{hf}{p}"))
                n = ng[0]
                if n >= 2:
                    act.wait_ge(sem("gate_used"), n - 1)
                for i in range(2):
                    br = "abc".index(b)
                    last = ac(A["gsb"][:, n % 2, i * T:(i + 1) * T], ps[:, i, :], ACT.Sigmoid,
                              bias=S_("gate_b", br * DC + hf * 4 + 2 * p + i))
                link(last)
                proj.release(act, f"g{b}{hf}{p}")
                act.sem_inc(sem("gate"), 1)
                ng[0] += 1
                ahead(f"g{b}{hf}{p}")

            def o_evac(n):
                ps = aux.wait(act, f"o{n}")
                link(ac(A["gdn_v"][:, :, n * CHUNK:(n + 1) * CHUNK], half(ps[:, 0:256], CHUNK), ACT.Copy))
                aux.release(act, f"o{n}")
            gates("a", 0, 0); o_evac(0); sb_log(0); gates("a", 0, 1); sb_log(1); sb_exp(0)
            gates("a", 1, 0); o_evac(1); sb_exp(1); gates("a", 1, 1)
            sb_log(2); sb_log(3); o_evac(2); sb_exp(2); sb_exp(3)
            gates("c", 0, 0); gates("c", 0, 1)
            o_evac(3)
            for hd in range(H):
                ac(sq[:, hd, :], A["gdn_v"][:, hd, :], ACT.Square).then_inc(sem("gdn_osq"), 1)
            gates("c", 1, 0)
            for hd in range(H):
                root(f"oss{hd}", sq[:, hd, :])
            gates("c", 1, 1)
            for hf in range(2):
                for p in range(2):
                    gates("b", hf, p)

            ahead("ob_1")
            act.wait_ge(sem("mixed"), 4)
            squares("mem", M["mem"], "mem_loaded", (16,) * 4)
            ahead("out00")
            root("ms_mem", sq[:, 0, :])
            ahead("out01")
            high_parts("mem", M["mem"], hm[0])
            ahead("out10")
            act.wait_ge(sem("normed"), chunks("mem"))
            squares("xq", x, "x1")
            ahead("out11")
            for u in range(2):
                ps = proj.wait(act, f"mk{u}")
                ac(M["sq"][:, 2 * u:2 * u + 2, :], half(ps), ACT.Square)
                link(ac(M["k"][:, 2 * u:2 * u + 2, :], half(ps), ACT.Copy))
                proj.release(act, f"mk{u}")
                act.sem_inc(sem("mem_sq_k"), 2)
                ahead(f"mk{u}")
            root("ms_xq", sq[:, 0, :])
            high_parts("xq", M["mem"], h_high)
            for u in range(2):
                ps = half(proj.wait(act, f"mv{u}"))
                proj.emptied(ac(M["v"][:, :, u * 256:(u + 1) * 256], ps, ACT.Copy), f"mv{u}")
                ahead(f"mv{u}")
            for hd in range(H):
                root(f"mss_k{hd}", M["sq"][:, hd, :])
            act.wait_ge(sem("mem_qk"), H)
            for u in range(2):
                ps = proj.wait(act, f"mq{u}")
                ac(M["sq"][:, 2 * u:2 * u + 2, :], half(ps), ACT.Square)
                link(ac(M["q"][:, 2 * u:2 * u + 2, :], half(ps), ACT.Copy))
                proj.release(act, f"mq{u}")
                act.sem_inc(sem("mem_sq_q"), 2)
                ahead(f"mq{u}")
            for hd in range(H):
                root(f"mss_q{hd}", M["sq"][:, hd, :])
            MSP = ((0, T), (T, T))
            softmax_exp(M["s"], M["st"], "mem", 0, MSP)
            for hd in range(H):
                if hd + 1 < H and hd < 1:
                    softmax_exp(M["s"], M["st"], "mem", hd + 1, MSP)
                turned("mpt", hd, M["pt"], 512, "mem_pT")
                if hd + 2 < H:
                    softmax_exp(M["s"], M["st"], "mem", hd + 2, MSP)

            act.wait_ge(sem("normed"), chunks("xq"))
            ahead("mo_0")
            squares("ffn", x, "x2")
            ahead("mo_1")
            root("ms_ffn", sq[:, 0, :])
            high_parts("ffn", M["mem"], h_high)

            def tap(c):
                if c >= 4 and c % 2 == 0:
                    ahead(f"D{c // 2 - 2}")
                ps = half(proj.wait(act, f"up{c}"))
                if c >= 3:
                    act.wait_ge(sem("ffn_act"), c - 2)
                for g in range(2):
                    ch = g * FC + c
                    last = ac(F["y"][:, c % 3, g, :], ps[:, g, :], ACT.Identity, bias=S_("ffn_b", ch),
                              scale=S_("ffn_conv", 3 * ch + 2))
                last.then_inc(sem("ffn_tap"), 1)
                ahead(f"U{c}")

            def silu(c):
                act.wait_ge(sem("ffn_conv"), c + 1)
                ac(F["sa"][:, c % 3, :], F["y"][:, c % 3, 0, :], ACT.Silu).then_inc(sem("ffn_silu"), 1)
            for c in range(FC + 1):
                if c < FC:
                    tap(c)
                if c:
                    silu(c - 1)

            for j in (FC // 2 - 2, FC // 2 - 1):
                ahead(f"D{j}")
            act.wait_ge(sem("normed"), chunks("ffn"))
            squares("n1", x, "x3")
            root("ms_n1", sq[:, 0, :])
            high_parts("n1", R["cat"], h_high)
            for nm in ("q", "k"):
                for u in range(2):
                    ps = proj.wait(act, f"{nm}2{u}")
                    link(ac(R[f"{nm}raw"][:, 2 * u:2 * u + 2, :], half(ps), ACT.Copy))
                    proj.release(act, f"{nm}2{u}")
                    ahead(f"{nm}2{u}")
                    act.sem_inc(sem(f"raw_{nm}"), 1)
            for u in range(2):
                ps = half(proj.wait(act, f"v2{u}"))
                link(ac(R["v"][:, :, u * 256:(u + 1) * 256], ps, ACT.Copy))
                proj.release(act, f"v2{u}")
                act.sem_inc(sem("ret_v"), 1)
                ahead(f"v2{u}")
            for u in range(2):
                ps = proj.wait(act, f"g2{u}")
                proj.emptied(ac(R["g"][:, 2 * u:2 * u + 2, :], half(ps), ACT.Silu), f"g2{u}")
                ahead(f"g2{u}")

            def ret_out(hd):
                ps = aux.wait(act, f"ro{hd}")
                if hd == 0:
                    act.wait_ge(sem("ret_q"), 2)
                link(ac(R["qraw"][:, hd, :], ps[:, 0:T], ACT.Copy))
                aux.release(act, f"ro{hd}")
                act.sem_inc(sem("ret_o"), 1)
            for u in range(2):
                ps = proj.wait(act, f"gc2{u}")
                link(ac(R["gc"][:, 2 * u:2 * u + 2, :], half(ps), ACT.Copy))
                proj.release(act, f"gc2{u}")
                act.sem_inc(sem("conv_gc"), 1)
                ahead(f"gc2{u}")
                if u == 0:
                    ret_out(0)
                    ret_out(1)
            ahead("u20")
            ret_out(2)
            ret_out(3)
            ahead("u21")
            for u in range(2):
                act.wait_ge(sem("conv_in"), u + 1)
                for i in range(2):
                    ch = 2 * u + i
                    last = ac(R["cat"][:, H + ch, :], R["gc"][:, ch, :], ACT.Copy, scale=S_("conv2", 3 * ch + 2))
                last.then_inc(sem("conv_tap"), 1)
            for hd in range(H):
                act.wait_ge(sem("ret_d"), hd + 1)
                if hd == 0:
                    act.wait_ge(sem("normed"), chunks("n1"))
                ac(sq[:, hd, :], R["qraw"][:, hd, :], ACT.Square).then_inc(sem("ret_d2"), 1)
            for hd in range(H):
                root(f"rv{hd}", sq[:, hd, :])
            for u in range(2):
                ps = proj.wait(act, f"gb2{u}")
                link(ac(R["gb"][:, 2 * u:2 * u + 2, :], half(ps), ACT.Copy))
                proj.release(act, f"gb2{u}")
                act.sem_inc(sem("conv_gb"), 1)
                ahead(f"gb2{u}")
            ahead("o200")
            act.wait_ge(sem("cat"), 2 * H)
            squares("n2", x, "x4")
            root("ms_n2", sq[:, 0, :])

            for t in range(TT):
                for hf in range(2):
                    ps = proj.wait(act, f"htok{t}{hf}")
                    ac(X["htok"][:, t, hf * 512:(hf + 1) * 512], ps, ACT.Copy).then_inc(sem("htok"), 1)
            act.wait_ge(sem("group_max"), 1)
            for t in range(TT):
                last = ac(X["r"][:, t, 8:16], X["lg"][:, t, 0:8], ACT.Exp, bias=X["r"][:, t, 1:2],
                          accum_out=X["r"][:, t, 2:3])
            last.then_inc(sem("group_exp"), 1)
            act.wait_ge(sem("expert_max"), 1)
            ac(X["r"][:, :, 6:7], X["r"][:, :, 5:6], ACT.Exp).then_inc(sem("expert_exp"), 1)

            act.wait_ge(sem("n_iter"), 1)
            n_iter = act.value_load(n_iter_i[0:1, 0:1], min_val=NG, max_val=NG * MAXPASS)
            with act.Fori(0, n_iter) as i:
                act.wait_ge(sem("xt_lo"), i + 1)
                ac(X["xt"][:, 0:4, :], half(psum[:, 4, :], P), ACT.Copy).then_inc(sem("xt_lo_kept"), 1)
                for j in range(GROUP):
                    q = i * GROUP + (j + 1)
                    act.wait_ge(sem("gate_up"), q)
                    ac(X["sil"], psum[:, 6, 0:P], ACT.Silu).then_inc(sem("e_silu"), 1)
                    act.wait_ge(sem("scatter"), q)
                    ac(X["scat"], psum[:, 7, 256:512], ACT.Copy).then_inc(sem("scatter_kept"), 1)
                    act.wait_ge(sem("e_turned"), q)
                    ac(X["actT"], psum[:, 6, 256:384], ACT.Copy).then_inc(sem("e_actT"), 1)
            squares("final", x, "x5")
            act.wait_ge(sem("ms_final"), 1)
            ac(sq[:, 0, :], psum[:, 4, 0:T], ACT.Sqrt, bias=C("eps")).then_inc(sem("root_ready"), 1)

        @block.vector
        def _(dve):
            V = nc.vector
            chain = [0]

            def link(ins):
                chain[0] += 1
                ins.then_inc(sem("dve_chain"), 1)
                dve.wait_ge(sem("dve_chain"), chain[0])

            roots = [0]

            def inverse_root(rs):
                roots[0] += 1
                dve.wait_ge(sem("root_ready"), roots[0])
                link(V.reciprocal(rs, rs))

            def normalise(name, src, dst, gain, parts=None):
                rs = sq[:, 0, :]
                inverse_root(rs)

                def low_part(q):
                    c = slice(2 * q, 2 * q + 2)
                    dve.wait_ge(sem("input_high"), quarter(name, q))
                    V.tensor_tensor(parts[1][:, c, :], dst[:, c, :], parts[0][:, c, :].bitcast(F32),
                                    ALU.subtract).then_inc(sem("input_low"), 1)
                for k in range(DC):
                    last = V.scalar_tensor_tensor(dst[:, k, :], src[:, k, :], S_(gain, k), rs, ALU.mult, ALU.mult)
                    last.then_inc(sem("normed"), 1)
                    if parts and k >= 3 and k % 2:
                        low_part(k // 2 - 1)
                if parts:
                    low_part(DC // 2 - 1)

            def split(high_part, low_part, src):
                link(V.tensor_copy(high_part, src))
                return V.tensor_tensor(low_part, src, high_part.bitcast(F32), ALU.subtract)
            H_PARTS = (h_high, h_low)

            dve.wait_ge(sem("consts_loaded"), 32)
            dve.wait_ge(sem("x_loaded"), 16)
            normalise("mix", x, A["h"], "norm_mix", H_PARTS)
            V.tensor_scalar(A["st"][:, 24:25], S_("fox_q"), SCALE, None, ALU.mult)

            def conv_dst(ch):
                return A["gdn_qk"][:, ch % H, ch // H, :] if ch < 2 * H else A["gdn_v"][:, ch % H, :]
            nu = 0
            for nm, first in (("gq", 0), ("gk", H), ("gv", 2 * H)):
                for u in range(2):
                    ps = half(proj.wait(dve, f"{nm}{u}"))
                    nu += 1
                    dve.wait_ge(sem("gdn_tap"), nu)
                    for s in (1, 2, 3):
                        for i in range(2):
                            ch = first + 2 * u + i
                            o = conv_dst(ch)[:, s:T]
                            ins = V.scalar_tensor_tensor(o, ps[:, i, 0:T - s], S_("gdn_conv", 4 * ch + 3 - s), o,
                                                         ALU.mult, ALU.add)
                            if s == 3:
                                ins.then_inc(sem("gdn_conv"), 1)
                        if s < 3:
                            link(ins)
                    dve.wait_ge(sem("gdn_conv"), 2 * nu)
                    proj.release(dve, f"{nm}{u}")
            dve.wait_ge(sem("late_consts_loaded"), 16)
            ps = aux.wait(dve, "rows")
            dve.wait_ge(sem("rows_ln"), 1)
            rw = A["rows"]
            V.tensor_scalar(rw[0:H, 4, :], ps[0:H, 0:T], S_("rows", 0, 0, H), 0.0, ALU.add, ALU.min)
            link(V.tensor_scalar(rw[64:64 + H, 4, :], ps[64:64 + H, 0:T], S_("rows", 2, 64, H), 0.0, ALU.add, ALU.max))
            V.tensor_tensor(rw[0:H, 4, :], rw[0:H, 4, :], rw[0:H, 5, :], ALU.subtract)
            link(V.tensor_tensor(rw[64:64 + H, 4, :], rw[64:64 + H, 4, :], rw[64:64 + H, 5, :], ALU.add))
            aux.emptied(V.tensor_tensor_scan(rw[0:H, 3, :], C("ones", H), rw[0:H, 4, :], 0.0, ALU.mult, ALU.add), "rows")
            link(V.tensor_scalar(rw[64:64 + H, 4, :], rw[64:64 + H, 4, :], A["st"][64:64 + H, 30:31], -1.0, ALU.mult, ALU.mult))
            dve.sem_inc(sem("fox_c"), 1)
            link(V.tensor_tensor_scan(rw[64:64 + H, 0, :], C("reset", H, base=64), rw[64:64 + H, 4, :], 0.0, ALU.mult, ALU.add))
            g4 = half(rw[64:64 + H, 0, :], CHUNK)
            V.tensor_tensor(half(rw[64:64 + H, 1, :], CHUNK),
                            g4[:, :, CHUNK - 1:CHUNK].broadcast_to([H, T // CHUNK, CHUNK]), g4,
                            ALU.subtract).then_inc(sem("gdn_tail"), 1)

            for hd in range(H):
                rs = sq[:, 2 * hd:2 * hd + 2, :]
                inverse_root(rs)
                V.scalar_tensor_tensor(A["gdn_qk"][:, hd, 0, :], A["gdn_qk"][:, hd, 0, :], SCALE, rs[:, 0, :],
                                       ALU.mult, ALU.mult)
                V.tensor_tensor(A["gdn_qk"][:, hd, 1, :], A["gdn_qk"][:, hd, 1, :], rs[:, 1, :],
                                ALU.mult).then_inc(sem("gdn_k"), 1)
            ps = aux.wait(dve, "tok")
            aux.emptied(V.tensor_copy(A["tok"][:, :, 0:8], half(ps[:, 0:16], 8)), "tok")
            ps = aux.wait(dve, "tok_beta")
            link(V.tensor_copy(A["tok"][:, :, 8:12], half(ps[:, 0:8], 4)))
            aux.release(dve, "tok_beta")
            dve.sem_inc(sem("gdn_cols"), 1)
            dve.wait_ge(sem("gdn_egc"), 1)
            V.tensor_tensor(A["tok"][:, :, 16:20], A["tok"][:, :, 8:12], A["tok"][:, :, 12:16],
                            ALU.mult).then_inc(sem("gdn_beg"), 1)
            for q in range(2):
                ps = half(aux.wait(dve, f"decay{q}"))
                dve.wait_ge(sem("gdn_eg"), q + 1)
                for i in range(2):
                    hd = 2 * q + i
                    for t in range(TT):
                        un = q * H + 2 * i + t
                        last = V.scalar_tensor_tensor(A["t"][:, un, :], ps[:, i, t * P:(t + 1) * P],
                                                      A["tok"][:, t, hd:hd + 1], C("chunk_mask"), ALU.subtract, ALU.add)
                        last.then_inc(sem("gdn_expo"), 1)
                dve.wait_ge(sem("gdn_expo"), 4 * (q + 1))
                aux.release(dve, f"decay{q}")
            for nm, gain in (("q", A["st"][:, 24:25]), ("k", S_("fox_k"))):
                for hd in range(H):
                    rs = sq[:, (0 if nm == "q" else H) + hd, :]
                    inverse_root(rs)
                    o = A[f"fox_{nm}"][:, hd, :]
                    V.scalar_tensor_tensor(o, o, gain, rs, ALU.mult, ALU.mult).then_inc(sem(f"fox_{nm}n"), 1)
            for t in range(TT):
                for q in range(2):
                    ps = half(aux.wait(dve, f"kk{t}{q}"))
                    if t == 0 and q == 0:
                        dve.wait_ge(sem("gdn_dt"), 2 * H)
                    for i in range(2):
                        hd = 2 * q + i
                        dt = A["t"][:, 2 * hd + t, :].rearrange("p (a b) -> p a b", a=1).broadcast_to([P, 2, P])
                        last = V.tensor_tensor(A["kd"][:, t * H + hd, :, :], half(ps[:, i, :], P), dt, ALU.mult)
                    link(last)
                    aux.release(dve, f"kk{t}{q}")
            V.tensor_tensor(A["gdn_qk"][:, :, 0, :], A["gdn_qk"][:, :, 0, :], A["eg"], ALU.mult)

            def lm(lv):
                m = C("levels", lo=lv * P, n=P).rearrange("p (a b) -> p a b", a=1).broadcast_to([P, 2 * H, P])
                V.tensor_tensor(A["lm"], A["kd"][:, :, 1, :], m, ALU.mult).then_inc(sem("gdn_lm"), 1)

            def solve_sub(lv, t, nm):
                ps = half(aux.wait(dve, f"{nm}{lv}{t}"), P)
                o = A[nm][:, t * H:(t + 1) * H, :]
                src = ident.rearrange("p (a b) -> p a b", a=1).broadcast_to([P, H, P]) if lv == 0 else o
                link(V.tensor_tensor(o, src, ps, ALU.subtract))
                aux.release(dve, f"{nm}{lv}{t}")
                dve.sem_inc(sem(f"gdn_{nm}"), 1)

            def softmax_max(buf, st, pre, unit, hd, spans, mask):
                n = spans[-1][0] + spans[-1][1]
                s = buf[:, hd % 2, 0:n]
                st = st[:, 8 * (hd % 2):8 * (hd % 2) + 8]
                ps = aux.wait(dve, f"{unit}{hd}")
                if hd >= 2:
                    dve.wait_ge(sem(f"{pre}_pT"), hd - 1)
                link(V.tensor_copy(s, ps[:, 0:n]) if mask is None else V.tensor_tensor(s, ps[:, 0:n], mask, ALU.add))
                aux.release(dve, f"{unit}{hd}")
                for t, (lo, w) in enumerate(spans):
                    last = V.reduce_max(st[:, t:t + 1], s[:, lo:lo + w], AX)
                link(last)
                V.tensor_scalar(st[:, 2:4], st[:, 0:2], -1.0, None, ALU.mult).then_inc(sem(f"{pre}_max"), 1)

            def softmax_norm(buf, st, pre, hd, spans):
                st = st[:, 8 * (hd % 2):8 * (hd % 2) + 8]
                dve.wait_ge(sem(f"{pre}_exp"), hd + 1)
                link(V.reciprocal(st[:, 6:8], st[:, 4:6]))
                for t, (lo, w) in enumerate(spans):
                    o = buf[:, hd % 2, lo:lo + w]
                    last = V.tensor_scalar(o, o, st[:, 6 + t:7 + t], None, ALU.mult)
                last.then_inc(sem(f"{pre}_p"), 1)

            def head_out(unit, hd, dst, done):
                ps = aux.wait(dve, f"{unit}{hd}")
                link(split(dst[0][:, hd, :], dst[1][:, hd, :], ps[:, 0:T]))
                aux.release(dve, f"{unit}{hd}")
                dve.sem_inc(sem(done), 1)
            FSP = ((0, P), (P, T))
            fmax = lambda hd: softmax_max(A["s"], A["st"], "fox", "fs", hd, FSP, C("fox_mask"))
            fnorm = lambda hd: softmax_norm(A["s"], A["st"], "fox", hd, FSP)
            fout = lambda hd: head_out("fpv", hd, ya, "ya")
            steps = iter([lambda: fmax(0), lambda: (fmax(1), fnorm(0)), lambda: fnorm(1), lambda: fout(0),
                          lambda: (fout(1), fmax(2)), lambda: (fmax(3), fnorm(2)), lambda: fnorm(3), lambda: fout(2),
                          lambda: fout(3)])

            def between():
                f = next(steps, None)
                if f:
                    f()
            lm(0)
            for lv in range(len(LEVELS)):
                between()
                for t in range(TT):
                    for nm in ("t", "u"):
                        if nm == "u" or lv < len(LEVELS) - 1:
                            solve_sub(lv, t, nm)
                if lv + 1 < len(LEVELS):
                    lm(lv + 1)
                between()
            for t in range(TT):
                ps = aux.wait(dve, f"sol_u{t}")
                link(V.tensor_copy(A["v_in"][:, t * H:(t + 1) * H, :], half(ps, P)))
                aux.release(dve, f"sol_u{t}")
            V.tensor_copy(A["vnew"][0:CHUNK, :].rearrange("p (a b) -> p a b", b=P),
                          A["v_in"][0:CHUNK, 0:H, :]).then_inc(sem("gdn_vnew"), 1)
            dve.wait_ge(sem("gdn_w"), 2)

            def state(n):
                ps = aux.wait(dve, f"dS{n}")
                for hd in range(H):
                    o, d = A["state"][:, hd, :], ps[:, hd * P:(hd + 1) * P]
                    if n == 0:
                        last = V.tensor_copy(o, d)
                    else:
                        last = V.scalar_tensor_tensor(o, o, A["eg"][:, hd, (n + 1) * CHUNK - 1:(n + 1) * CHUNK], d,
                                                      ALU.mult, ALU.add)
                link(last)
                aux.release(dve, f"dS{n}")
                dve.sem_inc(sem("gdn_state"), 1)

            def vnew(n):
                t, po = n // 2, CHUNK * (n % 2)
                ps = aux.wait(dve, f"wS{n}")
                link(V.tensor_tensor(half(A["vnew"][po:po + CHUNK, :], P), A["v_in"][po:po + CHUNK, t * H:(t + 1) * H, :],
                                     half(ps[po:po + CHUNK, :], P), ALU.add))
                aux.release(dve, f"wS{n}")
                dve.sem_inc(sem("gdn_vnew"), 1)

            def sb_keep(hd):
                ps = psum[:, 4 + aux.units[f"sz{hd}"] % 4, 0:384]
                s = A["s"][:, hd % 2, :]
                dve.wait_ge(sem("sb_ln"), hd + 1)
                link(V.scalar_tensor_tensor(s, ps, 0.0, A["pt"][:, hd % 2, :], ALU.max, ALU.add))
                V.tensor_tensor(s, s, C("sb_neg"), ALU.mult).then_inc(sem("sb_lk"), 1)

            def sb_masked(hd):
                dve.wait_ge(sem("sb_sum"), hd + 1)
                ps = psum[:, 4 + aux.units[f"sz{hd}"] % 4, 0:384]
                link(V.tensor_tensor(A["s"][:, hd % 2, :], ps, C("sb_mask"), ALU.add))
                aux.release(dve, f"sz{hd}")
                dve.sem_inc(sem("sb_s"), 1)
            ng = [0]

            def mix(b, hf, p):
                n = ng[0]
                u = 2 * hf + p
                ps = proj.wait(dve, f"o{b}{u}")
                dve.wait_ge(sem("gate"), n + 1)
                g = A["gsb"][:, n % 2, :]
                o = A["mixed"][:, 2 * u:2 * u + 2, :].rearrange("p a b -> p (a b)")
                if b == "a":
                    link(V.tensor_tensor(A["tmp2"][:, u, :], ps, g, ALU.mult))
                elif b == "c":
                    link(V.tensor_tensor(A["tmp"], ps, g, ALU.mult))
                    link(V.tensor_tensor(A["tmp2"][:, u, :], A["tmp2"][:, u, :], A["tmp"], ALU.add))
                else:
                    link(V.tensor_tensor(A["tmp"], ps, g, ALU.mult))
                    link(V.tensor_tensor(o, A["tmp2"][:, u, :], A["tmp"], ALU.add))
                    c = slice(2 * u, 2 * u + 2)
                    split(mixed[0][:, c, :], mixed[1][:, c, :], A["mixed"][:, c, :]).then_inc(sem("mixed"), 1)
                proj.release(dve, f"o{b}{u}")
                dve.sem_inc(sem("gate_used"), 1)
                ng[0] += 1
            sbout = lambda hd: head_out("spv", hd, yc, "yc")
            state(0); sb_keep(0); sb_keep(1); mix("a", 0, 0); vnew(1); mix("a", 0, 1); sb_masked(0)
            state(1); sb_masked(1); sbout(0); mix("a", 1, 0); sbout(1); vnew(2); mix("a", 1, 1)
            sb_keep(2); sb_keep(3); state(2); sb_masked(2); sb_masked(3); sbout(2); sbout(3)
            vnew(3); mix("c", 0, 0); mix("c", 0, 1)
            for hd in range(H):
                rs = sq[:, hd, :]
                inverse_root(rs)
                o = A["gdn_v"][:, hd, :]
                link(V.scalar_tensor_tensor(o, o, S_("gdn_o"), rs, ALU.mult, ALU.mult))
                link(V.tensor_tensor(o, o, A["gz"][:, hd, :], ALU.mult))
                split(yb[0][:, hd, :], yb[1][:, hd, :], o).then_inc(sem("yb"), 1)
            mix("c", 1, 0); mix("c", 1, 1)
            for hf in range(2):
                for p in range(2):
                    mix("b", hf, p)

            def residual(names, done, n=0):
                for nm in names:
                    ps = proj.wait(dve, nm)
                    o = x[:, 2 * n:2 * n + 2, :]
                    link(V.tensor_tensor(o, o, half(ps), ALU.add))
                    proj.release(dve, nm)
                    dve.sem_inc(sem(done), 1)
                    n += 1
            residual(("out00", "out01"), "x1")
            normalise("mem", M["mem"], M["mem"], "norm_mem", hm)
            residual(("out10", "out11"), "x1", 2)
            normalise("xq", x, M["mem"], "norm_xq", H_PARTS)
            V.tensor_scalar(M["st"][:, 24:25], S_("mq"), SCALE, None, ALU.mult)

            def mem_norm(nm, gain, base):
                for hd in range(H):
                    rs = M["sq"][:, hd, :]
                    inverse_root(rs)
                    o = M[nm][:, hd, :]
                    V.scalar_tensor_tensor(o, o, gain, rs, ALU.mult, ALU.mult).then_inc(sem("mem_qk"), 1)
            mem_norm("k", S_("mk"), 0)
            mem_norm("q", M["st"][:, 24:25], H)
            MSP = ((0, T), (T, T))
            mmax = lambda hd: softmax_max(M["s"], M["st"], "mem", "mS", hd, MSP, None)
            mnorm = lambda hd: softmax_norm(M["s"], M["st"], "mem", hd, MSP)
            mout = lambda hd: head_out("mpv", hd, ym, "ym")
            mmax(0); mmax(1); mnorm(0); mnorm(1)
            for hd in range(H):
                mout(hd)
                if hd + 2 < H:
                    mmax(hd + 2)
                    mnorm(hd + 2)
            residual(("mo0", "mo1", "mo2", "mo3"), "x2")

            normalise("ffn", x, M["mem"], "norm_ffn", H_PARTS)

            def taps(c):
                ps = half(proj.wait(dve, f"up{c}"))
                dve.wait_ge(sem("ffn_tap"), c + 1)
                for s in (1, 2):
                    for g in range(2):
                        ch = g * FC + c
                        o = F["y"][:, c % 3, g, s:T]
                        last = V.scalar_tensor_tensor(o, ps[:, g, 0:T - s], S_("ffn_conv", 3 * ch + 2 - s), o,
                                                      ALU.mult, ALU.add)
                    link(last)
                proj.release(dve, f"up{c}")
                dve.sem_inc(sem("ffn_conv"), 1)

            def product(c):
                dve.wait_ge(sem("ffn_silu"), c + 1)
                if c >= 4:
                    dve.wait_ge(sem("ffn_act_used"), c - 3)
                link(V.tensor_tensor(F["act"][:, c % 2, :], F["sa"][:, c % 3, :], F["y"][:, c % 3, 1, :], ALU.mult))
                split(act_high[:, c % 4, :], act_low[:, c % 4, :], F["act"][:, c % 2, :]).then_inc(sem("ffn_act"), 1)
            for c in range(FC + 1):
                if c < FC:
                    taps(c)
                if c:
                    product(c - 1)
            for b in range(4):
                ps = aux.wait(dve, f"down{b}")
                o = x[:, 2 * b:2 * b + 2, :]
                link(V.tensor_tensor(o, o, half(ps), ALU.add))
                aux.release(dve, f"down{b}")
                dve.sem_inc(sem("x3"), 1)

            normalise("n1", x, R["cat"], "norm1", H_PARTS)
            dve.wait_ge(sem("c2_loaded"), 16)

            def rotary(nm):
                cos, sin = (R["c2"][:, C2[f"{f}{nm}"]].rearrange("p (a b) -> p a b", a=1).broadcast_to([P, 2, T])
                            for f in ("cos", "sin"))
                for q in range(2):
                    ps = half(aux.wait(dve, f"rot_{nm}{q}"))
                    raw, o = R[f"{nm}raw"][:, 2 * q:2 * q + 2, :], R[nm][:, 2 * q:2 * q + 2, :]
                    V.tensor_tensor(o, ps, sin, ALU.mult)
                    link(V.tensor_tensor(raw, raw, cos, ALU.mult))
                    link(V.tensor_tensor(o, o, raw, ALU.add))
                    aux.release(dve, f"rot_{nm}{q}")
                    dve.sem_inc(sem(f"ret_{nm}"), 1)
            rotary("q")
            rotary("k")

            def ret_decay(hd):
                ps = aux.wait(dve, f"rs{hd}")
                if hd >= 2:
                    dve.wait_ge(sem("ret_o"), hd - 1)
                d0 = C2["decay"].start + hd * 384
                link(V.tensor_tensor(R["pt"][:, hd % 2, :], ps[:, 0:384], R["c2"][:, d0:d0 + 384], ALU.mult))
                aux.release(dve, f"rs{hd}")
                dve.sem_inc(sem("ret_p"), 1)
            for hd in range(H):
                ret_decay(hd)
            for u in range(2):
                ps = half(proj.wait(dve, f"u2{u}"))
                dve.wait_ge(sem("conv_gc"), u + 1)
                o = R["gc"][:, 2 * u:2 * u + 2, :]
                link(V.tensor_tensor(o, o, ps, ALU.mult))
                proj.release(dve, f"u2{u}")
                dve.sem_inc(sem("conv_in"), 1)
            for hd in range(H):
                ps = aux.wait(dve, f"rm{hd}")
                o = R["qraw"][:, hd, :]
                link(V.tensor_tensor(o, o, ps[:, 0:T], ALU.subtract))
                aux.release(dve, f"rm{hd}")
                dve.sem_inc(sem("ret_d"), 1)
            for u in range(2):
                dve.wait_ge(sem("conv_tap"), u + 1)
                for s in (1, 2):
                    for i in range(2):
                        ch = 2 * u + i
                        o = R["cat"][:, H + ch, s:T]
                        last = V.scalar_tensor_tensor(o, R["gc"][:, ch, 0:T - s], S_("conv2", 3 * ch + 2 - s), o,
                                                      ALU.mult, ALU.add)
                    link(last)
            for hd in range(H):
                rs = sq[:, hd, :]
                inverse_root(rs)
                o = R["qraw"][:, hd, :]
                link(V.scalar_tensor_tensor(o, o, S_("ret_gn", hd), rs, ALU.mult, ALU.mult))
                link(V.tensor_tensor(R["cat"][:, hd, :], o, R["g"][:, hd, :], ALU.mult))
                split(cat[0][:, hd, :], cat[1][:, hd, :], R["cat"][:, hd, :]).then_inc(sem("cat"), 1)
            for u in range(2):
                dve.wait_ge(sem("conv_gb"), u + 1)
                c = slice(H + 2 * u, H + 2 * u + 2)
                o = R["cat"][:, c, :]
                link(V.tensor_tensor(o, o, R["gb"][:, 2 * u:2 * u + 2, :], ALU.mult))
                split(cat[0][:, c, :], cat[1][:, c, :], o).then_inc(sem("cat"), 2)
            residual(("o200", "o201", "o210", "o211"), "x4")

            normalise("n2", x, h, "norm2")
            link(V.memset(X["zero"], 0.0))
            dve.sem_inc(sem("zeroed"), 1)
            ps = aux.wait(dve, "router")
            lg, r = X["lg"], X["r"]
            link(V.tensor_copy(lg, half(ps[:, 0:2 * 72], 72)))
            aux.release(dve, "router")
            link(V.tensor_reduce(r[:, :, 0:1], lg[:, :, 0:8], AX, ALU.max))
            link(V.tensor_scalar(r[:, :, 1:2], r[:, :, 0:1], -1.0, None, ALU.mult))
            dve.sem_inc(sem("group_max"), 1)

            def first_of_max(dst, src, top):
                for t in range(TT):
                    last = V.scalar_tensor_tensor(r[:, t, 16:24], src[:, t, :], r[:, t, top:top + 1], C("first", n=8),
                                                  ALU.is_ge, ALU.mult)
                link(last)
                link(V.tensor_reduce(r[:, :, 24:25], r[:, :, 16:24], AX, ALU.max))
                for t in range(TT):
                    last = V.tensor_scalar(dst[:, t, :], r[:, t, 16:24], r[:, t, 24:25], None, ALU.is_equal)
                link(last)
            first_of_max(X["one_g"], lg[:, :, 0:8], 0)
            for t in range(TT):
                oh = X["one_g"][:, t, :].rearrange("p (a b) -> p a b", b=1).broadcast_to([P, 8, 8])
                last = V.tensor_tensor(half(X["el"][:, t, :], 8), half(lg[:, t, 8:72], 8), oh, ALU.mult)
            link(last)
            for t in range(TT):
                last = V.tensor_reduce(r[:, t, 32:40], X["el"][:, t, :].rearrange("p (g e) -> p e g", e=8), AX, ALU.add)
            link(last)
            link(V.tensor_reduce(r[:, :, 3:4], r[:, :, 32:40], AX, ALU.max))
            first_of_max(r[:, :, 40:48], r[:, :, 32:40], 3)
            for t in range(TT):
                last = V.scalar_tensor_tensor(r[:, t, 32:40], r[:, t, 40:48], NEG, r[:, t, 32:40], ALU.mult, ALU.add)
            link(last)
            link(V.tensor_reduce(r[:, :, 4:5], r[:, :, 32:40], AX, ALU.max))
            first_of_max(r[:, :, 48:56], r[:, :, 32:40], 4)
            V.tensor_tensor(r[:, :, 5:6], r[:, :, 4:5], r[:, :, 3:4], ALU.subtract).then_inc(sem("expert_max"), 1)
            link(V.tensor_tensor(r[:, :, 56:64], r[:, :, 40:48], r[:, :, 48:56], ALU.add))
            for t in range(TT):
                oh = X["one_g"][:, t, :].rearrange("p (a b) -> p a b", b=1).broadcast_to([P, 8, 8])
                ee = r[:, t, 56:64].rearrange("p (a b) -> p a b", a=1).broadcast_to([P, 8, 8])
                last = V.tensor_tensor(half(X["member"][:, t, :], 8), oh, ee, ALU.mult)
            last.then_inc(sem("member"), 1)
            dve.wait_ge(sem("group_exp"), 1)
            dve.wait_ge(sem("expert_exp"), 1)
            link(V.tensor_scalar(r[:, :, 7:8], r[:, :, 6:7], 1.0, None, ALU.add))
            link(V.tensor_tensor(r[:, :, 7:8], r[:, :, 7:8], r[:, :, 2:3], ALU.mult))
            link(V.reciprocal(r[:, :, 7:8], r[:, :, 7:8]))
            link(V.tensor_tensor(r[:, :, 6:7], r[:, :, 6:7], r[:, :, 7:8], ALU.mult))
            for t in range(TT):
                last = V.tensor_scalar(r[:, t, 40:48], r[:, t, 40:48], r[:, t, 7:8], None, ALU.mult)
            link(last)
            for t in range(TT):
                last = V.scalar_tensor_tensor(r[:, t, 40:48], r[:, t, 48:56], r[:, t, 6:7], r[:, t, 40:48],
                                              ALU.mult, ALU.add)
            link(last)
            for t in range(TT):
                oh = X["one_g"][:, t, :].rearrange("p (a b) -> p a b", b=1).broadcast_to([P, 8, 8])
                ee = r[:, t, 40:48].rearrange("p (a b) -> p a b", a=1).broadcast_to([P, 8, 8])
                last = V.tensor_tensor(half(X["gate"][:, t, :], 8), oh, ee, ALU.mult)
            link(last)
            ps = aux.wait(dve, "rank")
            V.tensor_reduce(X["count"][:, 0:1], ps[:, 2 * E:3 * E], AX, ALU.max)
            link(V.scalar_tensor_tensor(X["rank"], half(ps[:, 0:2 * E], E), 2.0 * T, X["member"], ALU.add, ALU.mult))
            link(V.tensor_scalar(X["rank"], X["rank"], -2.0 * T, None, ALU.add))
            dve.sem_inc(sem("ranked"), 1)
            link(V.tensor_scalar(X["count"][:, 8:8 + MAXPASS - 1], C("steps"), X["count"][:, 0:1], float(NG),
                                 ALU.is_lt, ALU.mult))
            link(V.tensor_reduce(X["count"][:, 1:2], X["count"][:, 8:8 + MAXPASS - 1], AX, ALU.add))
            link(V.tensor_scalar(X["count"][:, 1:2], X["count"][:, 1:2], float(NG), None, ALU.add))
            V.tensor_copy(n_iter_i[:, :], X["count"][:, 1:2]).then_inc(sem("n_iter"), 1)

            def places(g0, done):
                for t in range(TT):
                    rk = X["rank"][:, t, bass.ds(g0, GROUP)]
                    last = V.tensor_tensor(half(X["s"][:, t, :], CAP),
                                           C("slots").rearrange("p (a b) -> p a b", a=1).broadcast_to([P, GROUP, CAP]),
                                           rk.rearrange("p (a b) -> p a b", b=1).broadcast_to([P, GROUP, CAP]),
                                           ALU.is_equal)
                last.then_inc(sem("placed"), 1)

            def gated(g0):
                for t in range(TT):
                    gt = X["gate"][:, t, bass.ds(g0, GROUP)]
                    s = X["s"][:, t, :].rearrange("p (a r c) -> p a r c", a=GROUP, r=1).broadcast_to([P, GROUP, 4, CAP])
                    last = V.tensor_tensor(X["sg"][:, t, :].rearrange("p (a r c) -> p a r c", a=GROUP, r=4), s,
                                           gt.rearrange("p (a r c) -> p a r c", r=1, c=1).broadcast_to([P, GROUP, 4, CAP]),
                                           ALU.mult)
                    rk = X["rank"][:, t, bass.ds(g0, GROUP)]
                    last = V.tensor_scalar(rk, rk, -float(CAP), None, ALU.add)
                last.then_inc(sem("places"), 1)
            dve.wait_ge(sem("n_iter"), 1)
            n_iter = dve.value_load(n_iter_i[0:1, 0:1], min_val=NG, max_val=NG * MAXPASS)
            places(0, 0)
            dve.wait_ge(sem("placed"), 1)
            gated(0)
            with dve.Fori(0, n_iter) as i:
                dve.wait_ge(sem("xt_hi"), i + 1)
                V.tensor_copy(X["xt"][:, 4:8, :], half(psum[:, 5, :], P)).then_inc(sem("xt_hi_kept"), 1)
                for j in range(GROUP):
                    q = i * GROUP + (j + 1)
                    dve.wait_ge(sem("e_silu"), q)
                    V.tensor_tensor(X["act"], X["sil"], psum[:, 6, P:2 * P], ALU.mult).then_inc(sem("e_act"), 1)
                    dve.wait_ge(sem("down"), q)
                    V.tensor_copy(X["yb"], psum[:, 7, 0:256]).then_inc(sem("e_y"), 1)
                g0 = ((i + 1) % NG) * GROUP
                dve.wait_ge(sem("places"), i + 1)
                places(g0, i)
                dve.wait_ge(sem("placed"), i + 2)
                gated(g0)
            dve.wait_ge(sem("moe_done"), 1)
            for b in range(4):
                o = x[:, 2 * b:2 * b + 2, :]
                V.tensor_tensor(o, o, half(psum[:, b, :]), ALU.add).then_inc(sem("x5"), 1)
            dve.wait_ge(sem("x5"), 4)
            inverse_root(sq[:, 0, :])
            for k in range(DC):
                V.scalar_tensor_tensor(h[:, k, :], x[:, k, :], S_("final", k), sq[:, 0, :], ALU.mult,
                                       ALU.mult).then_inc(sem("result"), 1)

        @block.gpsimd
        def _(pool):
            for n, name in enumerate(UNITS):
                pool.wait_ge(sem("w_high"), n + 1)
                nc.gpsimd.tensor_tensor(low(name), raw[:, place(name), :], high(name).bitcast(F32),
                                        ALU.subtract).then_inc(sem("w_low"), 1)

        @block.sync
        def _(sp):
            sp.dma_start(x, x_in).then_inc(sem("x_loaded"), 16)
            sp.dma_start(c1[:, 0:C1_EARLY], c1_in[:, 0:C1_EARLY]).then_inc(sem("consts_loaded"), 16)
            sp.dma_start(sm, sm_in).then_inc(sem("consts_loaded"), 16)
            for n, name in enumerate(UNITS):
                if n >= RAW:
                    sp.wait_ge(*done[UNITS[n - RAW]])
                if n == 3:
                    sp.dma_start(A["rows_w"], rows_w_in).then_inc(sem("rows_w_loaded"), 16)
                    sp.dma_start(c1[:, C1_EARLY:], c1_in[:, C1_EARLY:]).then_inc(sem("late_consts_loaded"), 16)
                    sp.dma_start(rb[0:1, :], rb_in).then_inc(sem("rb_loaded"), 16)
                if name == "mk0":
                    sp.wait_ge(sem("mixed"), 4)
                    sp.dma_start(M["mem"], mem_in).then_inc(sem("mem_loaded"), 16)
                if name == "U4":
                    sp.wait_ge(sem("x1"), 4)
                    sp.dma_start(R["c2"], c2_in).then_inc(sem("c2_loaded"), 16)
                    sp.dma_start(X["router_w"], router_w_in).then_inc(sem("router_w_loaded"), 16)
                sp.dma_start(raw[:, place(name), :], dense_in[n]).then_inc(loaded(name)[0], 16)

            def load(e, b):
                sp.dma_start(expert_gu[b].rearrange("p c g f -> p (c g f)"),
                             experts_in[e, :, 0:2 * SLOT]).then_inc(sem(f"gu_loaded{b}"), 16)

            def load_down(e, b):
                sp.dma_start(expert_dn[b].rearrange("p c d -> p (c d)"),
                             experts_in[e, :, 2 * SLOT:3 * SLOT]).then_inc(sem(f"dn_loaded{b}"), 16)
            sp.wait_ge(sem("ret_p"), H)
            load(0, 0)
            sp.wait_ge(*done[UNITS[LAST - RAW + 2]])
            load_down(0, 0)
            sp.wait_ge(*done[UNITS[LAST]])
            load(1, 1)
            load_down(1, 1)
            for e in (2, 3):
                sp.wait_ge(sem("gate_up"), e - 1)
                load(e, e % 2)
                sp.wait_ge(sem("down"), e - 1)
                load_down(e, e % 2)
            sp.wait_ge(sem("n_iter"), 1)
            n_iter = sp.value_load(n_iter_i[0:1, 0:1], min_val=NG, max_val=NG * MAXPASS)
            with sp.Fori(1, n_iter) as i:
                for j in range(GROUP):
                    e = (i % NG) * GROUP + j
                    sp.wait_ge(sem("gate_up"), i * GROUP + (j - 1))
                    load_e = sp.snap(e)
                    sp.dma_start(expert_gu[j % 2].rearrange("p c g f -> p (c g f)"),
                                 experts_in[bass.ds(load_e, 1), :, 0:2 * SLOT].rearrange("a p w -> p (a w)")
                                 ).then_inc(sem(f"gu_loaded{j % 2}"), 16)
                    sp.wait_ge(sem("down"), i * GROUP + (j - 1))
                    sp.dma_start(expert_dn[j % 2].rearrange("p c d -> p (c d)"),
                                 experts_in[bass.ds(load_e, 1), :, 2 * SLOT:3 * SLOT].rearrange("a p w -> p (a w)")
                                 ).then_inc(sem(f"dn_loaded{j % 2}"), 16)
            for q in range(4):
                sp.wait_ge(sem("result"), 2 * (q + 1))
                sp.dma_start(out[:, 2 * q:2 * q + 2, :], h[:, 2 * q:2 * q + 2, :]).then_inc(sem("stored"), 16)
            sp.wait_ge(sem("stored"), 64)




def constants():
    i = np.arange(P)
    c1 = np.zeros((P, NC1), np.float32)

    def put(c, at, name, v):
        c[:, at[name]] = v
    put(c1, C1, "ident", np.eye(P))
    put(c1, C1, "ones", 1.0)
    put(c1, C1, "inv128", 1.0 / P)
    put(c1, C1, "inv1024", 1.0 / D)
    put(c1, C1, "tri", i[:, None] >= i[None, :])
    put(c1, C1, "before", i[:, None] < i[None, :])
    causal = np.where(i[None, :] <= i[:, None], 0.0, NEG)
    put(c1, C1, "fox_mask", np.concatenate([causal, np.zeros((P, P)), causal], 1))
    strict = i[:, None] < i[None, :]
    full = np.ones((P, P), bool)
    ok = np.concatenate([strict, full, strict], 1)
    put(c1, C1, "sb_neg", np.where(ok, -1.0, 0.0))
    put(c1, C1, "sb_mask", np.where(ok, 0.0, NEG))
    same = i[:, None] // CHUNK == i[None, :] // CHUNK
    put(c1, C1, "chunk_mask", np.where(same & (i[None, :] >= i[:, None]), 0.0, NEG))
    lv = []
    for s in LEVELS:
        lv.append((i[:, None] // (2 * s) == i[None, :] // (2 * s)) & (i[:, None] // s % 2 == 0) & (i[None, :] // s % 2 == 1))
    put(c1, C1, "levels", np.concatenate(lv, 1))
    for hd in range(H):
        c1[i % 32 == hd, C1["sel"].start + hd * 256:C1["sel"].start + (hd + 1) * 256] = 1.0
        c1[i % 32 == hd, C1["negsel"].start + hd * P:C1["negsel"].start + (hd + 1) * P] = -1.0
    put(c1, C1, "slots", np.arange(CAP)[None, :])
    put(c1, C1, "first", E - np.arange(E)[None, :])
    put(c1, C1, "reset", (np.arange(T) % CHUNK != 0)[None, :])
    put(c1, C1, "steps", CAP * np.arange(1, MAXPASS)[None, :])
    put(c1, C1, "eps", EPS)
    c2 = np.zeros((P, NC2), np.float32)
    hf = P // 2
    rot = np.zeros((P, P))
    rot[i[:hf] + hf, i[:hf]] = -1.0
    rot[i[:hf], i[:hf] + hf] = 1.0
    put(c2, C2, "rot", rot)
    inv = (np.float32(10000.0) ** (-np.arange(hf, dtype=np.float32) / np.float32(hf))).astype(np.float32)
    ang = (np.arange(T, dtype=np.float32)[None, :] * inv[:, None]).astype(np.float32)
    cos, sin = np.tile(np.cos(ang), (2, 1)), np.tile(np.sin(ang), (2, 1))
    put(c2, C2, "cosq", cos * SCALE)
    put(c2, C2, "sinq", sin * SCALE)
    put(c2, C2, "cosk", cos)
    put(c2, C2, "sink", sin)
    for hd in range(H):
        lg = np.log1p(-(2.0 ** (-5.0 - hd)))
        rel = (i[None, :] - i[:, None]).astype(np.float64)
        diag = np.where(rel >= 0, np.exp(lg * np.maximum(rel, 0)), 0.0)
        off = np.exp(lg * (rel + P))
        o = C2["decay"].start + hd * 384
        c2[:, o:o + 384] = np.concatenate([diag, off, diag], 1)
    return c1, c2


def kernel(**inputs):
    import concourse.bacc as bacc
    from concourse.bass_utils import run_bass_kernel_spmd

    a = {k: np.asarray(v) for k, v in inputs.items()}
    f32 = np.float32

    def chunks(v):
        return np.ascontiguousarray(v.reshape(-1, P).T)

    def tile(w):
        return w.reshape(-1, P, w.shape[1]).transpose(1, 0, 2)

    c1, c2 = constants()
    sm = np.zeros((P, NSM), f32)

    def put(name, v):
        sm[:, SM[name]] = v
    for name, key in (("norm_mix", "norm_mix"), ("norm_xq", "norm_xq"), ("norm_mem", "norm_mem"), ("norm_ffn", "norm_ffn"),
                      ("norm1", "norm1_w_2"), ("norm2", "norm2_w_2"), ("final", "final_norm_w_2"), ("fox_q", "fox_qnorm"),
                      ("fox_k", "fox_knorm"), ("gdn_o", "gdn_onorm"), ("mq", "mq_norm"), ("mk", "mk_norm"),
                      ("ret_gn", "ret_gn_w_2"), ("gate_b", "gate_bias"), ("ffn_b", "ffn_conv_b")):
        put(name, chunks(a[key].reshape(-1)))
    for name, key in (("gdn_conv", "gdn_conv"), ("ffn_conv", "ffn_conv"), ("conv2", "conv_w_2")):
        w = a[key][0]
        put(name, w.reshape(w.shape[0], -1, P).transpose(2, 1, 0).reshape(P, -1))
    r0 = SM["rows"].start
    sm[0:H, r0] = a["fox_fbias"][0]
    sm[64:64 + H, r0 + 1] = a["gdn_a_log"][0]
    sm[64:64 + H, r0 + 2] = a["gdn_dt_bias"][0]

    win = a["w_in"][0]
    col, n = {}, 0
    for name, width in (("fq", 512), ("fk", 512), ("fv", 512), ("ff", 4), ("gq", 512), ("gk", 512), ("gv", 512), ("gb", 4),
                        ("ga", 4), ("gz", 512), ("sq", 512), ("sk", 512), ("sv", 512), ("gate", 3072)):
        col[name] = win[:, n:n + width]
        n += width
    rows_w = np.ascontiguousarray(tile(np.concatenate([col["ff"], col["gb"], col["ga"]], 1)))
    win2, wo2 = a["w_in_2"][0], a["w_o_2"][0]
    dense = np.empty((len(UNITS), P, UNIT), f32)

    def lay(name, w):
        dense[ORDER[name]] = tile(w).reshape(P, UNIT)

    def lay_all(name, w, width):
        for u in range(w.shape[1] // width):
            lay(f"{name}{u}", w[:, u * width:(u + 1) * width])
    for name in ("gq", "gk", "gv", "gz", "fq", "fk", "fv", "sq", "sk", "sv"):
        lay_all(name, col[name], 256)
    for bn, b in enumerate("abc"):
        for hf in range(2):
            lay_all(f"g{b}{hf}", col["gate"][:, bn * D + hf * 512:bn * D + (hf + 1) * 512], 256)
        lay_all(f"o{b}_", a[f"w_o{b}"][0], 512)
    for hf in range(2):
        lay_all(f"out{hf}", a["w_out"][0][:, hf * 512:(hf + 1) * 512], 256)
        lay_all(f"o2{hf}", wo2[:, hf * 512:(hf + 1) * 512], 256)
    lay_all("mk", a["w_mkv"][0][:, 0:512], 256)
    lay_all("mv", a["w_mkv"][0][:, 512:1024], 256)
    lay_all("mq", a["w_mq"][0], 256)
    lay_all("mo_", a["w_mo"][0], 512)
    up, dn = a["w_up"][0], a["w_down"][0]
    for c in range(FC):
        lay(f"U{c}", np.concatenate([up[:, c * P:(c + 1) * P], up[:, (FC + c) * P:(FC + c + 1) * P]], 1))
    for j in range(FC // 2):
        lay(f"D{j}", dn[j * 256:(j + 1) * 256])
    for j, name in enumerate(("q2", "k2", "v2", "g2", "gb2", "gc2", "u2")):
        lay_all(name, win2[:, j * 512:(j + 1) * 512], 256)
    router_w = np.ascontiguousarray(tile(np.concatenate(
        [a["router_g_w_2"][0], a["router_e_w_2"][0].transpose(1, 0, 2).reshape(D, E)], 1)))
    rb = np.ascontiguousarray(np.concatenate([a["router_g_b_2"][0], a["router_e_b_2"][0].reshape(-1)])[None, :])
    experts = np.empty((E, P, 3 * SLOT), f32)
    ev = experts.reshape(E, P, 3, SLOT)
    gub = np.stack([a["w_gate_2"][0], a["w_up_2"][0]], 2).reshape(E, DC, P, 1024).transpose(0, 2, 1, 3)
    ev[:, :, 0] = gub[:, :, 0:4].reshape(E, P, SLOT)
    ev[:, :, 1] = gub[:, :, 4:8].reshape(E, P, SLOT)
    ev[:, :, 2] = a["w_down_2"][0].reshape(E, 4, P, D).transpose(0, 2, 1, 3).reshape(E, P, SLOT)
    del gub

    def features(v):
        return np.ascontiguousarray(v[0].T.reshape(DC, P, T).transpose(1, 0, 2))

    nc = bacc.Bacc("TRN2", target_bir_lowering=False, num_devices=1)
    arrays, args = {}, []
    for name, v in (("c1", c1), ("c2", c2), ("small", sm), ("router_b", rb), ("x_t", features(a["x"])),
                    ("mem_t", features(a["mem"])), ("dense", dense), ("rows_w", rows_w), ("router_w", router_w),
                    ("experts", experts)):
        arrays[name] = v
        args.append(nc.dram_tensor(name, v.shape, mybir.dt.from_np(v.dtype), kind="ExternalInput").ap())
    args.append(nc.dram_tensor("out_t", (P, DC, T), F32, kind="ExternalOutput").ap())
    program(nc, *args)
    r = run_bass_kernel_spmd(nc, [arrays], core_ids=[0])
    got = r.results[0]["out_t"]
    return np.ascontiguousarray(got.transpose(1, 0, 2).reshape(D, T).T)[None]
```
